# Optimizing a Trainium2 kernel written in Bass

```python
import jax, jax.numpy as jnp
from jax import lax
import numpy as np

D_MODEL = 1024
BATCH = 1
SEQ = 512
DEPTH = 1
DEC_BATCH = 1
DEC_SEQ = 32
PAST_LEN = 1024

CHUNK = 64
EPS = 1e-6
H_A = 8
Q_LORA = 384
KV_LORA = 256
NOPE = 64
ROPE = 32
V_A = 64
ROPE_THETA = 10000.0
Q_BLOCK = 128
MLA_SCALE = (NOPE + ROPE) ** -0.5
H_B = 8
DH_B = 64
BAND_PREV = 8
BAND = (BAND_PREV + 1) * CHUNK
WINDOW_B = BAND_PREV * CHUNK
REL_CLIP = 256
BAND_SCALE = DH_B ** -0.5
PEER_HEADS = 8
N_KEYS = 128
N_EXPERTS = N_KEYS * N_KEYS
D_KEY = 256
TOPK = 16
PEER_BLOCK = 128
PLE_DIM = 256
IN_SPLITS = (Q_LORA, KV_LORA, ROPE, H_B * DH_B, H_B * DH_B, H_B * DH_B, D_MODEL, D_MODEL)
IN_COLS = sum(IN_SPLITS)

kernel_name = "hybrid_mla_band_peer_stream_step"

def rmsnorm(x, g):
    xf = x.astype(jnp.float32)
    y = xf * lax.rsqrt(jnp.mean(xf * xf, axis=-1, keepdims=True) + EPS)
    return (y * g.astype(jnp.float32)).astype(x.dtype)

def rope(x, pos):
    half = ROPE // 2
    freqs = ROPE_THETA ** (-jnp.arange(half, dtype=jnp.float32) / half)
    ang = pos.astype(jnp.float32)[:, None] * freqs[None, :]
    shape = (ang.shape[0],) + (1,) * (x.ndim - 3) + (half,)
    cos = jnp.cos(ang).reshape(shape)
    sin = jnp.sin(ang).reshape(shape)
    xf = x.astype(jnp.float32)
    x1, x2 = xf[..., :half], xf[..., half:]
    return jnp.concatenate([x1 * cos - x2 * sin, x1 * sin + x2 * cos], axis=-1).astype(x.dtype)

def mixer_inputs(h, pos, w_in, g_q, g_kv, w_uq, w_uk):
    B, T, _ = h.shape
    offsets = [int(o) for o in np.cumsum(IN_SPLITS)[:-1]]
    c_q, c_kv, k_r, q_b, k_b, v_b, gate_a, gate_b = jnp.split(h @ w_in, offsets, axis=-1)
    q = (rmsnorm(c_q, g_q) @ w_uq).reshape(B, T, H_A, NOPE + ROPE)
    q_rope = rope(q[..., NOPE:], pos)
    q_lat = jnp.einsum('bthn,chn->bthc', q[..., :NOPE], w_uk)
    c_kv = rmsnorm(c_kv, g_kv)
    k_r = rope(k_r, pos)
    q_b = q_b.reshape(B, T, H_B, DH_B)
    k_b = k_b.reshape(B, T, H_B, DH_B)
    v_b = v_b.reshape(B, T, H_B, DH_B)
    return q_lat, q_rope, c_kv, k_r, q_b, k_b, v_b, gate_a, gate_b

def mla_attend(q_lat, q_rope, c_kv, k_rope, mask):
    s = (jnp.einsum('bqhc,bkc->bhqk', q_lat, c_kv)
         + jnp.einsum('bqhr,bkr->bhqk', q_rope, k_rope)).astype(jnp.float32) * MLA_SCALE
    if mask is not None:
        s = jnp.where(mask, s, -1e30)
    w = jax.nn.softmax(s, axis=-1).astype(c_kv.dtype)
    return jnp.einsum('bhqk,bkc->bqhc', w, c_kv)

def mla_prompt(q_lat, q_rope, c_kv, k_rope):
    B, S = q_lat.shape[:2]
    nb = S // Q_BLOCK
    k_chunk = jnp.arange(S) // CHUNK
    ql = q_lat.reshape(B, nb, Q_BLOCK, H_A, KV_LORA).swapaxes(0, 1)
    qr = q_rope.reshape(B, nb, Q_BLOCK, H_A, ROPE).swapaxes(0, 1)

    def one_block(args):
        i, ql_b, qr_b = args
        q_chunk = (i * Q_BLOCK + jnp.arange(Q_BLOCK)) // CHUNK
        mask = k_chunk[None, :] <= q_chunk[:, None]
        return mla_attend(ql_b, qr_b, c_kv, k_rope, mask)

    o = lax.map(one_block, (jnp.arange(nb), ql, qr))
    return o.swapaxes(0, 1).reshape(B, S, H_A, KV_LORA)

def rel_bias_lookup(table, q_pos, k_pos):
    rel = jnp.clip(q_pos[:, None] - k_pos[None, :], -REL_CLIP, REL_CLIP) + REL_CLIP
    return table[:, rel]

def band_attend(q, k, v, bias, mask):
    s = jnp.einsum('bqhd,bkhd->bhqk', q, k).astype(jnp.float32) * BAND_SCALE + bias.astype(jnp.float32)
    if mask is not None:
        s = jnp.where(mask, s, -1e30)
    w = jax.nn.softmax(s, axis=-1).astype(v.dtype)
    return jnp.einsum('bhqk,bkhd->bqhd', w, v)

def band_prompt(q, k, v, table):
    B, S = q.shape[:2]
    nc = S // CHUNK
    pad = ((0, 0), (WINDOW_B, 0), (0, 0), (0, 0))
    k_pad = jnp.pad(k, pad)
    v_pad = jnp.pad(v, pad)
    q_c = q.reshape(B, nc, CHUNK, H_B, DH_B).swapaxes(0, 1)
    bias = rel_bias_lookup(table, jnp.arange(CHUNK) + WINDOW_B, jnp.arange(BAND))

    def one_chunk(args):
        c, q_blk = args
        start = c * CHUNK
        k_blk = lax.dynamic_slice_in_dim(k_pad, start, BAND, axis=1)
        v_blk = lax.dynamic_slice_in_dim(v_pad, start, BAND, axis=1)
        valid = (start - WINDOW_B + jnp.arange(BAND)) >= 0
        return band_attend(q_blk, k_blk, v_blk, bias, valid[None, :])

    o = lax.map(one_chunk, (jnp.arange(nc), q_c))
    return o.swapaxes(0, 1).reshape(B, S, H_B * DH_B)

def band_sample(q, k, v, cache_k, cache_v, table, past_len):
    B, T = q.shape[:2]
    Lc = cache_k.shape[1]
    k_all = jnp.concatenate([cache_k, k], axis=1)
    v_all = jnp.concatenate([cache_v, v], axis=1)
    q_pos = past_len + jnp.arange(T)
    k_pos = past_len - Lc + jnp.arange(Lc + T)
    bias = rel_bias_lookup(table, q_pos, k_pos)
    o = band_attend(q, k_all, v_all, bias, None)
    return o.reshape(B, T, H_B * DH_B), k_all[:, T:], v_all[:, T:]

def peer_ffn(h, w_query, sub_keys, expert_u, expert_v):
    B, T, D = h.shape
    n = B * T
    nb = -(-n // PEER_BLOCK)
    x = jnp.pad(h.reshape(n, D), ((0, nb * PEER_BLOCK - n), (0, 0))).reshape(nb, PEER_BLOCK, D)

    def one_block(xb):
        q = (xb @ w_query).reshape(PEER_BLOCK, PEER_HEADS, 2, D_KEY // 2)
        s = jnp.einsum('nhpd,hpkd->nhpk', q, sub_keys)
        top_s, top_i = lax.top_k(s, TOPK)
        cand = top_s[:, :, 0, :, None] + top_s[:, :, 1, None, :]
        best_s, best_c = lax.top_k(cand.reshape(PEER_BLOCK, PEER_HEADS, TOPK * TOPK), TOPK)
        i1 = jnp.take_along_axis(top_i[:, :, 0], best_c // TOPK, axis=-1)
        i2 = jnp.take_along_axis(top_i[:, :, 1], best_c % TOPK, axis=-1)
        idx = i1 * N_KEYS + i2
        g = jax.nn.softmax(best_s.astype(jnp.float32), axis=-1).astype(xb.dtype)
        a = jax.nn.gelu(jnp.einsum('nd,nhkd->nhk', xb, expert_u[idx]), approximate=False)
        return jnp.einsum('nhk,nhkd->nd', g * a, expert_v[idx])

    y = lax.map(one_block, x).reshape(nb * PEER_BLOCK, D)[:n]
    return y.reshape(B, T, D)

def trunk_layer(x, p, past, W):
    (g_mix, w_in, g_q, g_kv, w_uq, w_uk, w_uv, rel_tab, w_a_proj, w_b_proj, w_out,
     g_ffn, w_query, sub_keys, eu, ev, g_ple, w_ple_gate, w_ple_proj) = W
    B, T, _ = x.shape
    start = 0 if past is None else past[0].shape[1]
    pos = start + jnp.arange(T)
    h = rmsnorm(x, g_mix)
    q_lat, q_rope, c_kv, k_r, q_b, k_b, v_b, gate_a, gate_b = mixer_inputs(h, pos, w_in, g_q, g_kv, w_uq, w_uk)
    if past is None:
        o_lat = mla_prompt(q_lat, q_rope, c_kv, k_r)
        o_b = band_prompt(q_b, k_b, v_b, rel_tab)
        wb = min(WINDOW_B, T)
        new_bk, new_bv = k_b[:, T - wb:], v_b[:, T - wb:]
    else:
        cache_lat, cache_kr, cache_bk, cache_bv = past
        o_lat = mla_attend(q_lat, q_rope,
                           jnp.concatenate([cache_lat, c_kv], axis=1),
                           jnp.concatenate([cache_kr, k_r], axis=1), None)
        o_b, new_bk, new_bv = band_sample(q_b, k_b, v_b, cache_bk, cache_bv, rel_tab, start)
    o_a = jnp.einsum('bthc,chv->bthv', o_lat, w_uv).reshape(B, T, H_A * V_A)
    merged = jax.nn.sigmoid(gate_a) * (o_a @ w_a_proj) + jax.nn.sigmoid(gate_b) * (o_b @ w_b_proj)
    x = x + merged @ w_out
    x = x + peer_ffn(rmsnorm(x, g_ffn), w_query, sub_keys, eu, ev)
    x = x + jax.nn.sigmoid(rmsnorm(x, g_ple) @ w_ple_gate) * (p @ w_ple_proj)
    return x, (c_kv, k_r, new_bk, new_bv)

def setup_inputs(seed: int = 0) -> dict:
    key = jax.random.key(seed)
    ks = iter(jax.random.split(key, 40))
    nrm = lambda shape, s=1.0: jax.random.normal(next(ks), shape, jnp.float32) * s
    gain = lambda shape: 1.0 + nrm(shape, 0.05)
    wb = min(WINDOW_B, PAST_LEN)
    return {
        "x_prompt": nrm((BATCH, SEQ, D_MODEL)),
        "x_sample": nrm((DEC_BATCH, DEC_SEQ, D_MODEL)),
        "cache_latent": nrm((DEPTH, DEC_BATCH, PAST_LEN, KV_LORA)),
        "cache_krope": nrm((DEPTH, DEC_BATCH, PAST_LEN, ROPE)),
        "cache_band_k": nrm((DEPTH, DEC_BATCH, wb, H_B, DH_B)),
        "cache_band_v": nrm((DEPTH, DEC_BATCH, wb, H_B, DH_B)),
        "p_prompt": nrm((DEPTH, BATCH, SEQ, PLE_DIM)),
        "p_sample": nrm((DEPTH, DEC_BATCH, DEC_SEQ, PLE_DIM)),
        "g_mix": gain((DEPTH, D_MODEL)),
        "w_in": nrm((DEPTH, D_MODEL, IN_COLS), D_MODEL ** -0.5),
        "g_q_lora": gain((DEPTH, Q_LORA)),
        "g_kv_lora": gain((DEPTH, KV_LORA)),
        "w_uq": nrm((DEPTH, Q_LORA, H_A * (NOPE + ROPE)), Q_LORA ** -0.5),
        "w_uk": nrm((DEPTH, KV_LORA, H_A, NOPE), KV_LORA ** -0.5),
        "w_uv": nrm((DEPTH, KV_LORA, H_A, V_A), KV_LORA ** -0.5),
        "rel_bias": nrm((DEPTH, H_B, 2 * REL_CLIP + 1), 0.1),
        "w_a_proj": nrm((DEPTH, H_A * V_A, D_MODEL), (H_A * V_A) ** -0.5),
        "w_b_proj": nrm((DEPTH, H_B * DH_B, D_MODEL), (H_B * DH_B) ** -0.5),
        "w_out": nrm((DEPTH, D_MODEL, D_MODEL), D_MODEL ** -0.5),
        "g_ffn": gain((DEPTH, D_MODEL)),
        "w_query": nrm((DEPTH, D_MODEL, PEER_HEADS * D_KEY), D_MODEL ** -0.5),
        "sub_keys": nrm((DEPTH, PEER_HEADS, 2, N_KEYS, D_KEY // 2), (D_KEY // 2) ** -0.5),
        "expert_u": nrm((DEPTH, N_EXPERTS, D_MODEL), D_MODEL ** -0.5),
        "expert_v": nrm((DEPTH, N_EXPERTS, D_MODEL), 0.5),
        "g_ple": gain((DEPTH, D_MODEL)),
        "w_ple_gate": nrm((DEPTH, D_MODEL, D_MODEL), D_MODEL ** -0.5),
        "w_ple_proj": nrm((DEPTH, PLE_DIM, D_MODEL), PLE_DIM ** -0.5),
        "g_final": gain((D_MODEL,)),
    }

def reference(x_prompt, x_sample, cache_latent, cache_krope, cache_band_k, cache_band_v,
              p_prompt, p_sample, g_mix, w_in, g_q_lora, g_kv_lora, w_uq, w_uk, w_uv,
              rel_bias, w_a_proj, w_b_proj, w_out, g_ffn, w_query, sub_keys, expert_u,
              expert_v, g_ple, w_ple_gate, w_ple_proj, g_final):
    xp, xs = x_prompt, x_sample
    st_p, st_s = [], []
    for i in range(DEPTH):
        W = (g_mix[i], w_in[i], g_q_lora[i], g_kv_lora[i], w_uq[i], w_uk[i], w_uv[i],
             rel_bias[i], w_a_proj[i], w_b_proj[i], w_out[i], g_ffn[i], w_query[i],
             sub_keys[i], expert_u[i], expert_v[i], g_ple[i], w_ple_gate[i], w_ple_proj[i])
        xp, sp = trunk_layer(xp, p_prompt[i], None, W)
        xs, ss = trunk_layer(xs, p_sample[i],
                             (cache_latent[i], cache_krope[i], cache_band_k[i], cache_band_v[i]), W)
        st_p.append(sp)
        st_s.append(ss)
    y_prompt = rmsnorm(xp, g_final)
    y_sample = rmsnorm(xs, g_final)
    latent_prompt = jnp.stack([s[0] for s in st_p])
    krope_prompt = jnp.stack([s[1] for s in st_p])
    band_k_prompt = jnp.stack([s[2] for s in st_p])
    band_v_prompt = jnp.stack([s[3] for s in st_p])
    latent_sample = jnp.stack([s[0] for s in st_s])
    krope_sample = jnp.stack([s[1] for s in st_s])
    band_k_sample = jnp.stack([s[2] for s in st_s])
    band_v_sample = jnp.stack([s[3] for s in st_s])
    return (y_prompt, y_sample, latent_prompt, krope_prompt, band_k_prompt, band_v_prompt,
            latent_sample, krope_sample, band_k_sample, band_v_sample)


_drawn_inputs = setup_inputs


def setup_inputs(seed=0):
    import zlib

    import numpy as np

    out = dict(_drawn_inputs(seed))
    spreads = {}
    factors = {'g_q_lora': 4.268, 'rel_bias': 3.13, 'g_ple': 6.317}
    for name, (base, spread) in spreads.items():
        noise = np.random.default_rng([zlib.crc32(name.encode()), seed]).standard_normal(out[name].shape)
        drawn = base * np.exp(spread * noise) if base else spread * noise
        out[name] = __import__('jax').numpy.asarray(drawn.astype(out[name].dtype))
    for name, factor in factors.items():
        out[name] = (out[name] * factor).astype(out[name].dtype)
    return out
```

```python
from contextlib import ExitStack

import numpy as np

import concourse.bass as bass
from concourse import mybir

F32 = mybir.dt.float32
U32 = mybir.dt.uint32
ALU = mybir.AluOpType
ACT = mybir.ActivationFunctionType
AXX = mybir.AxisListType.X
AXXY = mybir.AxisListType.XY

P = 128
D = 1024
KD = D // P
SEQ, SAMP, PAST = 512, 32, 1024
T = SEQ + SAMP
H2 = T // 2
QL, KVL, NOPE, ROPE = 384, 256, 64, 32
HEADS, PAIRS = 8, 4
NQ, NC = QL // P, KVL // P
MLA_SCALE = float(NOPE + ROPE) ** -0.5
BAND_SCALE = 0.125
WIN = 512
BANDK = WIN + SAMP
MLAK = PAST + SAMP
MLA3 = MLAK // 3
NEG = -1e30
REMOVED = -3e38
EPS = 1e-6
QT = SEQ // P
TT = QT + 1
NK = 128
TOPK = 16
UNITS = 2 * QT + 1
GPASS = 2
IP = NK // GPASS
GB = 2
GT = 8

C_IDENT, C_ONES, C_IOTA, C_DUP, C_MASKL, C_MASKR, C_EPS, C_END = 0, 128, 256, 384, 512, 640, 768, 769
G_MIX, G_FFN, G_PLE, G_FIN, G_Q, G_KV, G_END = 0, 8, 16, 24, 32, 35, 37


def tensor_wait(nc, k, pe, sem, value):
    pe.wait_ge(sem, value)
    nc.tensor.matmul(k.ps[:, 7, 511:512], k.const[:, C_ONES:C_ONES + P], k.const[:, C_ONES:C_ONES + 1],
                     start=True, stop=True)


def rows_of(tile):
    return P if tile < QT else SAMP


class Core:
    pass


def named_semaphores(nc, ctx, prefix, names):
    return [ctx.enter_context(nc.semaphore(f"{prefix}_{n}")) for n in names.split()]


def rms_norm(nc, k, name, sems, use, base, src, dst, chunks, gain, store=None, stores=0):
    squared, summed, rooted, inverted, normed, stored = sems
    with nc.Block(name) as block:
        @block.scalar
        def _(act):
            for c in range(chunks):
                if c >= 2:
                    act.wait_ge(summed, base + c - 1)
                nc.scalar.activation(k.square[:, c % 2, :], src(c), ACT.Square).then_inc(squared, 1)
            act.wait_ge(summed, base + chunks)
            nc.scalar.activation(k.rstd[:, :].rearrange("p (h t) -> p h t", h=2), k.ps[:, 0:2, 0:H2], ACT.Sqrt,
                                 bias=k.const[:, C_EPS:C_EPS + 1], scale=1.0 / (chunks * P)).then_inc(rooted, 1)

        @block.tensor
        def _(pe):
            for c in range(chunks):
                pe.wait_ge(squared, base + c + 1)
                for h in range(2):
                    last = nc.tensor.matmul(k.ps[:, h, 0:H2], k.const[:, C_ONES:C_ONES + P],
                                            k.square[:, c % 2, h * H2:(h + 1) * H2],
                                            start=c == 0, stop=c == chunks - 1)
                last.then_inc(summed, 1)

        @block.vector
        def _(dve):
            dve.wait_ge(rooted, use + 1)
            nc.vector.reciprocal(k.rstd[:, :], k.rstd[:, :]).then_inc(inverted, 1)
            dve.wait_ge(inverted, use + 1)
            for c in range(chunks):
                nc.vector.scalar_tensor_tensor(out=dst(c), in0=src(c), scalar=k.gain[:, gain + c:gain + c + 1],
                                               in1=k.rstd[:, :], op0=ALU.mult, op1=ALU.mult).then_inc(normed, 1)

        if store is not None:
            @block.sync
            def _(sp):
                sp.wait_ge(normed, base + chunks)
                for out, tile in store:
                    sp.dma_start(out, tile).then_inc(stored, 16)
                sp.wait_ge(stored, 16 * (stores + len(store)))


def accumulate(nc, out, pairs):
    n = len(pairs)
    for j, (lhs, rhs) in enumerate(pairs):
        last = nc.tensor.matmul(out, lhs, rhs, start=j == 0, stop=j == n - 1)
    return last


def load_inputs(nc, k, d):
    with nc.Block("load") as block, nc.semaphore("load_done") as loaded:
        @block.sync
        def _(sp):
            sp.dma_start(k.xT[:, :, :], d["xT"]).then_inc(loaded, 16)
            sp.dma_start(k.const[:, :], d["consts"]).then_inc(loaded, 16)
            sp.dma_start(k.gain[:, :], d["gains"]).then_inc(loaded, 16)
            sp.wait_ge(loaded, 48)


def latent_projection(nc, k, d, a):
    blocks = NQ + NC + 1
    with ExitStack() as ctx:
        w = ctx.enter_context(nc.sbuf_tensor("w_small", [P, 2, KD, P], F32))
        w0_in, w1_in, product, bank_free = named_semaphores(nc, ctx, "lp", "w0_in w1_in product bank_free")
        w_in = [w0_in, w1_in]
        with nc.Block("latent_projection") as block:
            @block.sync
            def _(sp):
                for s in range(2):
                    sp.dma_start(w[:, s], d["w_small"][s]).then_inc(w_in[s], 16)
                with sp.Fori(0, blocks // 2 - 1) as i:
                    for s in range(2):
                        sp.wait_ge(product, i * 4 + 2 * s + 2)
                        sp.dma_start(w[:, s], d["w_small"][bass.ds(i * 2 + (s + 2), 1)].rearrange("o p k m -> p (o k) m")
                                     ).then_inc(w_in[s], 16)

            @block.tensor
            def _(pe):
                pe.sem_inc(bank_free, 4)
                with pe.Fori(0, blocks // 2) as i:
                    for s in range(2):
                        pe.wait_ge(w_in[s], i * 16 + 16)
                        for h in range(2):
                            u = 2 * s + h
                            pe.wait_ge(bank_free, i * 4 + u + 1)
                            accumulate(nc, k.ps[:, u, 0:H2],
                                       [(w[:, s, c, :], k.hT[:, c, h * H2:(h + 1) * H2]) for c in range(KD)]
                                       ).then_inc(product, 1)

            @block.scalar
            def _(act):
                with act.Fori(0, blocks // 2) as i:
                    for s in range(2):
                        for h in range(2):
                            u = 2 * s + h
                            act.wait_ge(product, i * 4 + u + 1)
                            nc.scalar.activation(a.proj[:, bass.ds(i * 2 + s, 1), h * H2:(h + 1) * H2],
                                                 k.ps[:, u:u + 1, 0:H2], ACT.Copy).then_inc(bank_free, 1)


def rotary_key(nc, k, d, a):
    with ExitStack() as ctx:
        loaded, turned, summed, copied, flipped, kept, stored = named_semaphores(
            nc, ctx, "rk", "loaded turned summed copied flipped kept stored")
        with nc.Block("rotary_key") as block:
            @block.sync
            def _(sp):
                sp.dma_start(a.rope[:, :], d["rope"]).then_inc(loaded, 16)
                sp.dma_start(a.keyS[:, :, 0:PAST], d["cache_latT"]).then_inc(loaded, 16)
                sp.dma_start(a.kdupS[NOPE:P, 0:PAST], d["cache_krT"]).then_inc(loaded, 16)
                sp.dma_start(a.valueS[:, 0:PAST // P, :], d["cache_lat"]).then_inc(loaded, 16)
                sp.wait_ge(loaded, 64)
                sp.wait_ge(copied, 2)
                sp.dma_start(d["o_krope"], a.kdup[0:ROPE, :]).then_inc(stored, 16)
                sp.wait_ge(stored, 16)

            @block.vector
            def _(dve):
                dve.wait_ge(loaded, 64)
                nc.vector.tensor_tensor(a.turn[0:NOPE, :], a.proj[0:NOPE, NQ + NC, :], a.rope[0:NOPE, :],
                                        ALU.mult).then_inc(turned, 1)
                for c in range(NC):
                    nc.vector.tensor_copy(a.keyS[:, c, PAST:MLAK], a.proj[:, NQ + c, SEQ:T])
                dve.wait_ge(copied, 2)
                nc.vector.tensor_copy(a.kdupS[NOPE:P, PAST:MLAK], a.kdup[NOPE:P, SEQ:T]).then_inc(kept, 1)

            @block.tensor
            def _(pe):
                pe.wait_ge(turned, 1)
                for h in range(2):
                    nc.tensor.matmul(k.ps[:, h, 0:H2], k.const[0:NOPE, C_DUP:C_DUP + P],
                                     a.turn[0:NOPE, h * H2:(h + 1) * H2], start=True, stop=True).then_inc(summed, 1)
                for t in range(TT):
                    r = rows_of(t)
                    for c in range(NC):
                        last = nc.tensor.transpose(k.ps[0:r, 2 + t, c * P:(c + 1) * P],
                                                   a.proj[:, NQ + c, t * P:t * P + r],
                                                   k.const[:, C_IDENT:C_IDENT + P])
                    last.then_inc(flipped, 1)

            @block.scalar
            def _(act):
                for h in range(2):
                    act.wait_ge(summed, h + 1)
                    nc.scalar.activation(a.kdup[:, h * H2:(h + 1) * H2], k.ps[:, h, 0:H2],
                                         ACT.Copy).then_inc(copied, 1)
                for t in range(TT):
                    act.wait_ge(flipped, t + 1)
                    r = rows_of(t)
                    out = a.value[:, t, :] if t < QT else a.valueS[0:r, PAST // P, :]
                    nc.scalar.activation(out, k.ps[0:r, 2 + t, 0:KVL], ACT.Copy).then_inc(kept, 1)


class Softmax:

    def __init__(self, nc, k, sems, band, sample_keys):
        self.nc, self.k, self.band, self.sample_keys = nc, k, band, sample_keys
        (self.scored, self.biased, self.peaked, self.exped, self.scaled, self.turned, self.probT, self.mixed,
         self.kept, self.inv_done) = sems

    def rows(self, u):
        return P if u < UNITS - 1 else 2 * SAMP

    def keys(self, u):
        return P * (u % QT + 1) if u < UNITS - 1 else self.sample_keys

    def blocks(self, u):
        n = self.keys(u)
        return [(b, min(P, n - b)) for b in range(0, n, P)]

    def tensor(self, pe, p, scores, values):
        nc, k = self.nc, self.k
        scores(0)
        scores(1)
        for u in range(UNITS):
            if u + 2 < UNITS:
                pe.wait_ge(self.biased if self.band else self.exped, p * UNITS + (u + 2 if u + 2 == UNITS - 1 and not self.band else u + 1))
                scores(u + 2)
            if u < UNITS - 1:
                pe.wait_ge(self.scaled, p * UNITS + u + 1)
            else:
                tensor_wait(nc, k, pe, self.scaled, p * UNITS + u + 1)
            r = self.rows(u)
            for j, (b, n) in enumerate(self.blocks(u)):
                out = k.ps[0:n, 3 + u % 2, j * r:j * r + r] if j < 8 else k.ps[0:n, 7, 0:r]
                last = nc.tensor.transpose(out, k.prob[0:r, u % 2, b:b + n], k.const[0:r, C_IDENT:C_IDENT + r])
            last.then_inc(self.turned, 1)
            pe.wait_ge(self.probT, p * UNITS + u + 1)
            if u >= 2:
                pe.wait_ge(self.kept, p * UNITS + u - 1)
            values(u).then_inc(self.mixed, 1)

    def scalar(self, act, p, keep):
        nc, k = self.nc, self.k
        for u in range(UNITS + 2):
            if u < UNITS:
                r, n = self.rows(u), self.keys(u)
                act.wait_ge(self.peaked, p * UNITS + u + 1)
                if self.band:
                    nc.scalar.activation(k.prob[0:r, u % 2, 0:n], k.biased[0:r, u % 2, 0:n], ACT.Exp,
                                         bias=k.peak[0:r, u % 2:u % 2 + 1],
                                         accum_out=k.total[0:r, u % 2:u % 2 + 1]).then_inc(self.exped, 1)
                else:
                    dst = k.prob[0:r, u % 2, 0:n]
                    if u < UNITS - 1:
                        src = k.ps[0:r, u % 2, 0:n]
                    else:
                        src, dst = k.ps[0:r, 0:3, 0:MLA3], dst.rearrange("p (a b) -> p a b", a=3)
                    nc.scalar.activation(dst, src, ACT.Exp, bias=k.peak[0:r, u % 2:u % 2 + 1], scale=MLA_SCALE,
                                         accum_out=k.total[0:r, u % 2:u % 2 + 1]).then_inc(self.exped, 1)
            if 1 <= u <= UNITS:
                v = u - 1
                act.wait_ge(self.turned, p * UNITS + v + 1)
                r, blocks = self.rows(v), self.blocks(v)
                full = min(8, len([b for b in blocks if b[1] == P]))
                last = nc.scalar.activation(k.probT[:, v % 2, 0:full * r], k.ps[:, 3 + v % 2, 0:full * r], ACT.Copy)
                for j in range(full, len(blocks)):
                    n = blocks[j][1]
                    src = k.ps[0:n, 3 + v % 2, j * r:j * r + r] if j < 8 else k.ps[0:n, 7, 0:r]
                    last = nc.scalar.activation(k.probT[0:n, v % 2, j * r:j * r + r], src, ACT.Copy)
                last.then_inc(self.probT, 1)
            if u >= 2:
                act.wait_ge(self.mixed, p * UNITS + u - 1)
                keep(u - 2).then_inc(self.kept, 1)

    def vector(self, dve, p):
        nc, k = self.nc, self.k
        for u in range(UNITS + 1):
            if u < UNITS:
                r, n = self.rows(u), self.keys(u)
                dve.wait_ge(self.scored, p * UNITS + u + 1)
                if self.band:
                    if u < UNITS - 1:
                        q0 = P * (u % QT)
                        nc.vector.tensor_tensor(k.biased[0:r, u % 2, 0:n], k.ps[0:r, u % 2, 0:n],
                                                k.bias[:, u // QT, WIN - q0:WIN - q0 + n],
                                                ALU.add).then_inc(self.biased, 1)
                    else:
                        nc.vector.tensor_tensor(k.biased[0:r, u % 2, 0:WIN], k.ps[0:r, 0, 0:WIN],
                                                k.biasS[:, 0:WIN], ALU.add)
                        nc.vector.tensor_tensor(k.biased[0:r, u % 2, WIN:n], k.ps[0:r, 2, 0:SAMP],
                                                k.biasS[:, WIN:n], ALU.add).then_inc(self.biased, 1)
                    dve.wait_ge(self.biased, p * UNITS + u + 1)
                    nc.vector.tensor_reduce(k.peak[0:r, u % 2:u % 2 + 1], k.biased[0:r, u % 2, 0:n], AXX, ALU.max,
                                            negate=True).then_inc(self.peaked, 1)
                else:
                    if u < UNITS - 1:
                        nc.vector.tensor_reduce(k.rawpeak[0:r, u % 2:u % 2 + 1], k.ps[0:r, u % 2, 0:n], AXX, ALU.max,
                                                negate=True).then_inc(self.biased, 1)
                    else:
                        nc.vector.tensor_reduce(k.rawpeak[0:r, u % 2:u % 2 + 1], k.ps[0:r, 0:3, 0:MLA3], AXXY,
                                                ALU.max, negate=True).then_inc(self.biased, 1)
                    dve.wait_ge(self.biased, p * UNITS + u + 1)
                    nc.vector.tensor_scalar(k.peak[0:r, u % 2:u % 2 + 1], k.rawpeak[0:r, u % 2:u % 2 + 1], MLA_SCALE,
                                            None, ALU.mult).then_inc(self.peaked, 1)
            if u >= 1:
                v = u - 1
                r, n = self.rows(v), self.keys(v)
                dve.wait_ge(self.exped, p * UNITS + v + 1)
                nc.vector.reciprocal(k.inverse[0:r, v % 2:v % 2 + 1], k.total[0:r, v % 2:v % 2 + 1]
                                     ).then_inc(self.inv_done, 1)
                dve.wait_ge(self.inv_done, p * UNITS + v + 1)
                nc.vector.tensor_scalar(k.prob[0:r, v % 2, 0:n], k.prob[0:r, v % 2, 0:n],
                                        k.inverse[0:r, v % 2:v % 2 + 1], None, ALU.mult).then_inc(self.scaled, 1)


SOFTMAX_SEMS = "scored biased peaked exped scaled turned probT mixed kept inv_done"


def softmax_buffers(nc, k, ctx, keys, band):
    p = "ba" if band else "ma"
    k.prob = ctx.enter_context(nc.sbuf_tensor(f"{p}_prob", [P, 2, keys], F32))
    k.probT = ctx.enter_context(nc.sbuf_tensor(f"{p}_probT", [P, 2, 9 * 2 * SAMP], F32))
    k.peak, k.rawpeak, k.total, k.inverse = (
        ctx.enter_context(nc.sbuf_tensor(f"{p}_{n}", [P, 2], F32)) for n in ("peak", "rawpeak", "total", "inverse"))
    if band:
        k.biased = ctx.enter_context(nc.sbuf_tensor("biased", [P, 2, keys], F32))
        k.bias = ctx.enter_context(nc.sbuf_tensor("bias", [P, 2, WIN + P], F32))
        k.biasS = ctx.enter_context(nc.sbuf_tensor("biasS", [2 * SAMP, keys], F32))


def band_attention(nc, k, d, a):
    with ExitStack() as ctx:
        softmax_buffers(nc, k, ctx, BANDK, True)
        wq = ctx.enter_context(nc.sbuf_tensor("bw_q", [P, KD, P], F32))
        wk = ctx.enter_context(nc.sbuf_tensor("bw_k", [P, KD, P], F32))
        wv = ctx.enter_context(nc.sbuf_tensor("bw_v", [P, KD, P], F32))
        q = ctx.enter_context(nc.sbuf_tensor("b_q", [P, T], F32))
        kk = ctx.enter_context(nc.sbuf_tensor("b_k", [P, SEQ + BANDK], F32))
        v = ctx.enter_context(nc.sbuf_tensor("b_v", [P, 2 * QT + 1, P], F32))
        wq_in, wk_in, wv_in, cache_in, bias_in, projected, in_sbuf, stored, moved = named_semaphores(
            nc, ctx, "ba", "wq_in wk_in wv_in cache_in bias_in projected in_sbuf stored moved")
        sm = Softmax(nc, k, named_semaphores(nc, ctx, "ba", SOFTMAX_SEMS), True, BANDK)

        def one(x, p):
            return x[bass.ds(p, 1)]

        def load_weights(sp, p):
            for w, name, sem in ((wq, "w_bq", wq_in), (wk, "w_bk", wk_in), (wv, "w_bv", wv_in)):
                sp.dma_start(w[:, :, :], one(d[name], p).rearrange("o p k m -> p (o k) m")).then_inc(sem, 16)

        def load_cache(sp, p):
            sp.dma_start(kk[:, SEQ:SEQ + WIN], one(d["cache_bkT"], p).rearrange("o p t -> p (o t)")).then_inc(cache_in, 16)
            sp.dma_start(v[:, QT:2 * QT, :], one(d["cache_bv"], p).rearrange("o p n c -> p (o n) c")).then_inc(cache_in, 16)

        def load_bias(sp, p):
            sp.dma_start(k.bias[:, :, :], one(d["bias"], p).rearrange("o p h m -> p (o h) m")).then_inc(bias_in, 16)
            sp.dma_start(k.biasS[:, :], one(d["biasS"], p).rearrange("o p m -> p (o m)")).then_inc(bias_in, 16)

        def store(sp, p):
            sp.wait_ge(in_sbuf, p * 3 + 3)
            sp.wait_ge(cache_in, p * 32 + 32)
            sp.dma_start(one(d["o_bkT"], p).rearrange("o p t -> p (o t)"), kk[:, 0:SEQ]).then_inc(stored, 16)
            sp.dma_start(one(d["o_bkS"], p).rearrange("o p t -> p (o t)"), kk[:, SEQ + SAMP:SEQ + BANDK]).then_inc(stored, 16)
            sp.dma_start(one(d["o_bv"], p).rearrange("o p n c -> p (o n) c"), v[:, 0:QT, :]).then_inc(stored, 16)
            sp.dma_start(one(d["o_bvS"], p).rearrange("o p c -> p (o c)"), v[0:SAMP, 2 * QT, :]).then_inc(stored, 16)

        with nc.Block("band_attention") as block:
            @block.sync
            def _(sp):
                sp.dma_start(d["o_bvold"], d["cache_bv_kept"]).then_inc(moved, 16)
                load_weights(sp, 0)
                load_cache(sp, 0)
                load_bias(sp, 0)
                with sp.Fori(0, PAIRS - 1) as p:
                    store(sp, p)
                    sp.wait_ge(projected, p * 3 + 3)
                    load_weights(sp, p + 1)
                    sp.wait_ge(sm.biased, (p + 1) * UNITS)
                    load_bias(sp, p + 1)
                    sp.wait_ge(sm.mixed, (p + 1) * UNITS)
                    sp.wait_ge(stored, p * 64 + 64)
                    load_cache(sp, p + 1)
                store(sp, PAIRS - 1)
                sp.wait_ge(stored, PAIRS * 64)
                sp.wait_ge(moved, 16)

            @block.tensor
            def _(pe):
                with pe.Fori(0, PAIRS) as p:
                    pe.wait_ge(sm.kept, p * UNITS)
                    for w, sem, bank in ((wq, wq_in, 0), (wk, wk_in, 2)):
                        pe.wait_ge(sem, p * 16 + 16)
                        for h in range(2):
                            last = accumulate(nc, k.ps[:, bank + h, 0:H2],
                                              [(w[:, c, :], k.hT[:, c, h * H2:(h + 1) * H2]) for c in range(KD)])
                        last.then_inc(projected, 1)
                    pe.wait_ge(wv_in, p * 16 + 16)
                    for t in range(TT):
                        r = rows_of(t)
                        last = accumulate(nc, k.ps[0:r, 4, t * P:(t + 1) * P] if t < QT else k.ps[0:r, 5, 0:P],
                                          [(k.hT[:, c, t * P:t * P + r], wv[:, c, :]) for c in range(KD)])
                    last.then_inc(projected, 1)

                    def scores(u):
                        if u == 0:
                            pe.wait_ge(in_sbuf, p * 3 + 3)
                        if u < UNITS - 1:
                            a0, q0 = 64 * (u // QT), P * (u % QT)
                            last = nc.tensor.matmul(k.ps[:, u % 2, 0:sm.keys(u)], q[a0:a0 + 64, q0:q0 + P],
                                                    kk[a0:a0 + 64, 0:sm.keys(u)], start=True, stop=True)
                        else:
                            tensor_wait(nc, k, pe, cache_in, p * 32 + 32)
                            for hh in range(2):
                                a0 = 64 * hh
                                for bank, k0, n in ((0, SEQ, WIN), (2, SEQ + WIN, SAMP)):
                                    last = nc.tensor.matmul(k.ps[SAMP * hh:SAMP * (hh + 1), bank, 0:n],
                                                            q[a0:a0 + 64, SEQ:T], kk[a0:a0 + 64, k0:k0 + n],
                                                            start=True, stop=True)
                        last.then_inc(sm.scored, 1)

                    def values(u):
                        if u < UNITS - 1:
                            a0 = 64 * (u // QT)
                            return accumulate(nc, k.ps[a0:a0 + 64, 5 + u % 2, 0:P],
                                              [(v[:, j, a0:a0 + 64], k.probT[:, u % 2, j * P:(j + 1) * P])
                                               for j in range(u % QT + 1)])
                        for hh in range(2):
                            a0, r = 64 * hh, 2 * SAMP
                            last = accumulate(nc, k.ps[a0:a0 + 64, 5 + u % 2, 0:SAMP],
                                              [(v[0:n, QT + j, a0:a0 + 64],
                                                k.probT[0:n, u % 2, j * r + SAMP * hh:j * r + SAMP * (hh + 1)])
                                               for j, (_, n) in enumerate(sm.blocks(u))])
                        return last

                    sm.tensor(pe, p, scores, values)

            @block.scalar
            def _(act):
                with act.Fori(0, PAIRS) as p:
                    act.wait_ge(stored, p * 64)
                    act.wait_ge(projected, p * 3 + 1)
                    nc.scalar.activation(q[:, :].rearrange("p (h t) -> p h t", h=2), k.ps[:, 0:2, 0:H2], ACT.Copy,
                                         scale=BAND_SCALE).then_inc(in_sbuf, 1)
                    act.wait_ge(projected, p * 3 + 2)
                    nc.scalar.activation(kk[:, 0:H2], k.ps[:, 2, 0:H2], ACT.Copy)
                    nc.scalar.activation(kk[:, H2:SEQ], k.ps[:, 3, 0:SEQ - H2], ACT.Copy)
                    nc.scalar.activation(kk[:, SEQ + WIN:SEQ + BANDK], k.ps[:, 3, SEQ - H2:H2],
                                         ACT.Copy).then_inc(in_sbuf, 1)
                    act.wait_ge(projected, p * 3 + 3)
                    nc.scalar.activation(v[:, 0:QT, :], k.ps[:, 4, :].rearrange("p (t c) -> p t c", t=QT), ACT.Copy)
                    nc.scalar.activation(v[0:SAMP, 2 * QT, :], k.ps[0:SAMP, 5, 0:P], ACT.Copy).then_inc(in_sbuf, 1)

                    def keep(u):
                        if u < UNITS - 1:
                            a0, q0 = 64 * (u // QT), P * (u % QT)
                            return nc.scalar.activation(a.oB[a0:a0 + 64, bass.ds(p, 1), q0:q0 + P],
                                                        k.ps[a0:a0 + 64, 5 + u % 2:6 + u % 2, 0:P], ACT.Copy)
                        return nc.scalar.activation(a.oB[:, bass.ds(p, 1), SEQ:T],
                                                    k.ps[:, 5 + u % 2:6 + u % 2, 0:SAMP], ACT.Copy)

                    sm.scalar(act, p, keep)

            @block.vector
            def _(dve):
                with dve.Fori(0, PAIRS) as p:
                    dve.wait_ge(bias_in, p * 32 + 32)
                    sm.vector(dve, p)


def latent_attention(nc, k, d, a):
    with ExitStack() as ctx:
        softmax_buffers(nc, k, ctx, MLAK, False)
        wq = ctx.enter_context(nc.sbuf_tensor("m_wq", [P, 2, NQ, P], F32))
        wk = ctx.enter_context(nc.sbuf_tensor("m_wk", [NOPE, 2, KVL], F32))
        wv = ctx.enter_context(nc.sbuf_tensor("m_wv", [P, 2, NC, NOPE], F32))
        qn = ctx.enter_context(nc.sbuf_tensor("m_qn", [NOPE, 2, T], F32))
        qr = ctx.enter_context(nc.sbuf_tensor("m_qr", [P, 2, T], F32))
        ql = ctx.enter_context(nc.sbuf_tensor("m_ql", [P, NC, 2, T], F32))
        ol = ctx.enter_context(nc.sbuf_tensor("m_ol", [P, NC, 2, T], F32))
        qlS = ctx.enter_context(nc.sbuf_tensor("m_qlS", [P, NC + 1, 2 * SAMP], F32))
        w_in, projected, split, turned, lifted, in_sbuf, packed, lowered, pair_done = named_semaphores(
            nc, ctx, "ma", "w_in projected split rotated lifted in_sbuf packed lowered pair_done")
        sm = Softmax(nc, k, named_semaphores(nc, ctx, "ma", SOFTMAX_SEMS), False, MLAK)
        LIFTS = 2 * NC * 2

        def load(sp, p):
            sp.dma_start(wq[:, :, :, :].rearrange("p a k m -> p (a k m)"),
                         d["w_uq"][bass.ds(p, 1)].rearrange("o p m -> p (o m)")).then_inc(w_in, 16)
            sp.dma_start(wk[:, :, :].rearrange("p a m -> p (a m)"),
                         d["w_ukT"][bass.ds(p, 1)].rearrange("o p m -> p (o m)")).then_inc(w_in, 16)
            sp.dma_start(wv[:, :, :, :].rearrange("p a k m -> p (a k m)"),
                         d["w_uv"][bass.ds(p, 1)].rearrange("o p m -> p (o m)")).then_inc(w_in, 16)

        with nc.Block("latent_attention") as block:
            @block.sync
            def _(sp):
                load(sp, 0)
                with sp.Fori(0, PAIRS - 1) as p:
                    sp.wait_ge(lowered, p + 1)
                    load(sp, p + 1)

            @block.tensor
            def _(pe):
                with pe.Fori(0, PAIRS) as p:
                    pe.wait_ge(pair_done, p)
                    pe.wait_ge(w_in, p * 48 + 48)
                    for hh in range(2):
                        for h in range(2):
                            last = accumulate(nc, k.ps[:, 2 * hh + h, 0:H2],
                                              [(wq[:, hh, c, :], a.proj[:, c, h * H2:(h + 1) * H2]) for c in range(NQ)])
                        last.then_inc(projected, 1)
                    for hh in range(2):
                        pe.wait_ge(split, p * 2 + hh + 1)
                        if hh == 1:
                            pe.wait_ge(turned, p * 2 + 2)
                            pe.wait_ge(split, p * 2 + 2)
                        for c in range(NC):
                            for h in range(2):
                                bank = (4 + 4 * hh + 2 * c + h) % 8
                                nc.tensor.matmul(k.ps[:, bank, 0:H2], wk[:, hh, c * P:(c + 1) * P],
                                                 qn[:, hh, h * H2:(h + 1) * H2], start=True, stop=True
                                                 ).then_inc(lifted, 1)

                    def scores(u):
                        if u == 0:
                            pe.wait_ge(in_sbuf, p * LIFTS + LIFTS)
                            pe.wait_ge(packed, p + 1)
                        if u < UNITS - 1:
                            hh, q0, n = u // QT, P * (u % QT), sm.keys(u)
                            out = k.ps[:, u % 2, 0:n]
                            for c in range(NC):
                                nc.tensor.matmul(out, ql[:, c, hh, q0:q0 + P], a.proj[:, NQ + c, 0:n],
                                                 start=c == 0, stop=False)
                            nc.tensor.matmul(out, qr[NOPE:P, hh, q0:q0 + P], a.kdup[NOPE:P, 0:n],
                                             start=False, stop=False)
                            last = nc.tensor.matmul(k.ps[:, u % 2, q0:q0 + P], k.const[0:1, C_MASKL:C_MASKL + P],
                                                    k.const[0:1, C_MASKR:C_MASKR + P], start=False, stop=True)
                        else:
                            for j in range(3):
                                k0 = j * MLA3
                                out = k.ps[0:2 * SAMP, j, 0:MLA3]
                                for c in range(NC):
                                    nc.tensor.matmul(out, qlS[:, c, :], a.keyS[:, c, k0:k0 + MLA3],
                                                     start=c == 0, stop=False)
                                last = nc.tensor.matmul(out, qlS[NOPE:P, NC, :], a.kdupS[NOPE:P, k0:k0 + MLA3],
                                                        start=False, stop=True)
                        last.then_inc(sm.scored, 1)

                    def values(u):
                        r = sm.rows(u)
                        for c in range(NC):
                            pairs = []
                            for j, (_, n) in enumerate(sm.blocks(u)):
                                v = a.value[:, j, :] if u < UNITS - 1 else a.valueS[0:n, j, :]
                                pairs.append((v[:, c * P:(c + 1) * P], k.probT[0:n, u % 2, j * r:(j + 1) * r]))
                            last = accumulate(nc, k.ps[:, 5 + u % 2, c * P:c * P + r], pairs)
                        return last

                    sm.tensor(pe, p, scores, values)
                    pe.wait_ge(sm.kept, (p + 1) * UNITS)
                    for hh in range(2):
                        for h in range(2):
                            last = accumulate(nc, k.ps[64 * hh:64 * (hh + 1), h, 0:H2],
                                              [(wv[:, hh, c, :], ol[:, c, hh, h * H2:(h + 1) * H2]) for c in range(NC)])
                    last.then_inc(lowered, 1)

            @block.scalar
            def _(act):
                with act.Fori(0, PAIRS) as p:
                    for hh in range(2):
                        act.wait_ge(projected, p * 2 + hh + 1)
                        nc.scalar.activation(qn[:, hh, :].rearrange("p (h t) -> p h t", h=2),
                                             k.ps[0:NOPE, 2 * hh:2 * hh + 2, 0:H2], ACT.Copy).then_inc(split, 1)
                    for hh in range(2):
                        for c in range(NC):
                            for h in range(2):
                                j = 4 * hh + 2 * c + h
                                act.wait_ge(lifted, p * LIFTS + j + 1)
                                nc.scalar.activation(ql[:, c, hh, h * H2:(h + 1) * H2], k.ps[:, (4 + j) % 8, 0:H2],
                                                     ACT.Copy).then_inc(in_sbuf, 1)

                    def keep(u):
                        r, bank = sm.rows(u), 5 + u % 2
                        if u < UNITS - 1:
                            hh, q0 = u // QT, P * (u % QT)
                            return nc.scalar.activation(ol[:, :, hh, q0:q0 + P],
                                                        k.ps[:, bank, 0:2 * P].rearrange("p (c t) -> p c t", c=NC),
                                                        ACT.Copy)
                        for c in range(NC):
                            last = nc.scalar.activation(ol[:, c, :, SEQ:T],
                                                        k.ps[:, bank, c * P:c * P + r].rearrange("p (h t) -> p h t", h=2),
                                                        ACT.Copy)
                        return last

                    sm.scalar(act, p, keep)
                    act.wait_ge(lowered, p + 1)
                    nc.scalar.activation(a.oA[:, bass.ds(p, 1), :].rearrange("p o (h t) -> p (o h) t", h=2),
                                         k.ps[:, 0:2, 0:H2], ACT.Copy).then_inc(pair_done, 1)

            @block.vector
            def _(dve):
                with dve.Fori(0, PAIRS) as p:
                    for hh in range(2):
                        dve.wait_ge(projected, p * 2 + hh + 1)
                        nc.vector.tensor_tensor(qr[NOPE:P, hh, :].rearrange("p (h t) -> p h t", h=2),
                                                k.ps[NOPE:P, 2 * hh:2 * hh + 2, 0:H2],
                                                a.rope[NOPE:P, :].rearrange("p (h t) -> p h t", h=2),
                                                ALU.mult).then_inc(turned, 1)
                    dve.wait_ge(turned, p * 2 + 2)
                    nc.vector.tensor_copy(qlS[NOPE:P, NC, :].rearrange("p (h t) -> p h t", h=2), qr[NOPE:P, :, SEQ:T])
                    dve.wait_ge(in_sbuf, p * LIFTS + LIFTS)
                    for c in range(NC):
                        last = nc.vector.tensor_copy(qlS[:, c, :].rearrange("p (h t) -> p h t", h=2), ql[:, c, :, SEQ:T])
                    last.then_inc(packed, 1)
                    sm.vector(dve, p)


def gated_merge(nc, k, d, a):
    KC = 2 * KD + 2 * PAIRS
    with ExitStack() as ctx:
        w = ctx.enter_context(nc.sbuf_tensor("gm_w", [P, 2, KC, P], F32))
        gate = ctx.enter_context(nc.sbuf_tensor("gm_gate", [P, 2, T], F32))
        w0_in, w1_in, gated, valued, gate_done, term, merged = named_semaphores(
            nc, ctx, "gm", "w0_in w1_in gated valued gate_done term merged")
        w_in = [w0_in, w1_in]

        def load(sp, s, m):
            sp.dma_start(w[:, s], d["w_merge"][bass.ds(m, 1)].rearrange("o p k m -> p (o k) m")).then_inc(w_in[s], 16)

        with nc.Block("gated_merge") as block:
            @block.sync
            def _(sp):
                for s in range(2):
                    load(sp, s, s)
                with sp.Fori(0, KD // 2 - 1) as i:
                    for s in range(2):
                        sp.wait_ge(valued, i * 4 + 2 * s + 2)
                        load(sp, s, i * 2 + (s + 2))

            @block.tensor
            def _(pe):
                with pe.Fori(0, KD // 2) as i:
                    for s in range(2):
                        pe.wait_ge(w_in[s], i * 16 + 16)
                        for b in range(2):
                            pe.wait_ge(gate_done, i * 4 + 2 * s)
                            for h in range(2):
                                last = accumulate(nc, k.ps[:, 2 * b + h, 0:H2],
                                                  [(w[:, s, b * KD + c, :], k.hT[:, c, h * H2:(h + 1) * H2])
                                                   for c in range(KD)])
                            last.then_inc(gated, 1)
                        for b, o in enumerate((a.oA, a.oB)):
                            pe.wait_ge(term, i * 4 + 2 * s)
                            for h in range(2):
                                last = accumulate(nc, k.ps[:, 4 + 2 * b + h, 0:H2],
                                                  [(w[:, s, 2 * KD + b * PAIRS + c, :], o[:, c, h * H2:(h + 1) * H2])
                                                   for c in range(PAIRS)])
                            last.then_inc(valued, 1)

            @block.scalar
            def _(act):
                with act.Fori(0, KD // 2) as i:
                    for s in range(2):
                        act.wait_ge(merged, i * 2 + s)
                        for b in range(2):
                            act.wait_ge(gated, i * 4 + 2 * s + b + 1)
                            nc.scalar.activation(gate[:, b, :].rearrange("p (h t) -> p h t", h=2),
                                                 k.ps[:, 2 * b:2 * b + 2, 0:H2], ACT.Sigmoid).then_inc(gate_done, 1)

            @block.vector
            def _(dve):
                with dve.Fori(0, KD // 2) as i:
                    for s in range(2):
                        for b in range(2):
                            dve.wait_ge(gate_done, i * 4 + 2 * s + b + 1)
                            dve.wait_ge(valued, i * 4 + 2 * s + b + 1)
                            g = gate[:, b, :].rearrange("p (h t) -> p h t", h=2)
                            nc.vector.tensor_tensor(g, g, k.ps[:, 4 + 2 * b:6 + 2 * b, 0:H2], ALU.mult).then_inc(term, 1)
                        dve.wait_ge(term, i * 4 + 2 * s + 2)
                        nc.vector.tensor_tensor(a.merged[:, bass.ds(i * 2 + s, 1), :],
                                                gate[:, 0:1, :], gate[:, 1:2, :], ALU.add).then_inc(merged, 1)


def output_projection(nc, k, d, a):
    with ExitStack() as ctx:
        w = ctx.enter_context(nc.sbuf_tensor("op_w", [P, 2, KD, P], F32))
        w0_in, w1_in, product, bank_free = named_semaphores(nc, ctx, "op", "w0_in w1_in product bank_free")
        w_in = [w0_in, w1_in]

        def load(sp, s, m):
            sp.dma_start(w[:, s], d["w_out"][bass.ds(m, 1)].rearrange("o p k m -> p (o k) m")).then_inc(w_in[s], 16)

        with nc.Block("output_projection") as block:
            @block.sync
            def _(sp):
                for s in range(2):
                    load(sp, s, s)
                with sp.Fori(0, KD // 2 - 1) as i:
                    for s in range(2):
                        sp.wait_ge(product, i * 4 + 2 * s + 2)
                        load(sp, s, i * 2 + (s + 2))

            @block.tensor
            def _(pe):
                pe.sem_inc(bank_free, 4)
                with pe.Fori(0, KD // 2) as i:
                    for s in range(2):
                        pe.wait_ge(w_in[s], i * 16 + 16)
                        for h in range(2):
                            u = 2 * s + h
                            pe.wait_ge(bank_free, i * 4 + u + 1)
                            accumulate(nc, k.ps[:, u, 0:H2],
                                       [(w[:, s, c, :], a.merged[:, c, h * H2:(h + 1) * H2]) for c in range(KD)]
                                       ).then_inc(product, 1)

            @block.vector
            def _(dve):
                with dve.Fori(0, KD // 2) as i:
                    for s in range(2):
                        for h in range(2):
                            u = 2 * s + h
                            dve.wait_ge(product, i * 4 + u + 1)
                            x = k.xT[:, bass.ds(i * 2 + s, 1), h * H2:(h + 1) * H2]
                            nc.vector.tensor_tensor(x, x, k.ps[:, u:u + 1, 0:H2], ALU.add).then_inc(bank_free, 1)


def retrieve(nc, k, d, f):
    with ExitStack() as ctx:
        w = ctx.enter_context(nc.sbuf_tensor("r_w", [P, 2, KD + 1, P], F32))
        qT = ctx.enter_context(nc.sbuf_tensor("r_q", [P, 2, T], F32))
        score = ctx.enter_context(nc.sbuf_tensor("r_score", [P, 2, TT, NK], F32))
        rest = ctx.enter_context(nc.sbuf_tensor("r_rest", [P, TT, NK], F32))
        top = ctx.enter_context(nc.sbuf_tensor("r_top", [P, 2, TT, TOPK], F32))
        at = ctx.enter_context(nc.sbuf_tensor("r_at", [P, 2, TT, TOPK], U32))
        atf = ctx.enter_context(nc.sbuf_tensor("r_atf", [P, 2, TT, TOPK], F32))
        cand = ctx.enter_context(nc.sbuf_tensor("r_cand", [P, TT, TOPK * TOPK], F32))
        left = ctx.enter_context(nc.sbuf_tensor("r_left", [P, TT, TOPK * TOPK], F32))
        best = ctx.enter_context(nc.sbuf_tensor("r_best", [P, TT, TOPK], F32))
        where = ctx.enter_context(nc.sbuf_tensor("r_where", [P, TT, TOPK], U32))
        part = ctx.enter_context(nc.sbuf_tensor("r_part", [P, 2, TT, TOPK], U32))
        partf = ctx.enter_context(nc.sbuf_tensor("r_partf", [P, 2, TT, TOPK], F32))
        hit = ctx.enter_context(nc.sbuf_tensor("r_hit", [P, TT, TOPK, TOPK], F32))
        tot = ctx.enter_context(nc.sbuf_tensor("r_tot", [P, TT], F32))
        res = ctx.enter_context(nc.sbuf_tensor("r_res", [P, 3, TT, HEADS * TOPK], F32))
        (w0_in, w1_in, queried, q_in_sbuf, scored, score_in, score_free, step, exp_ready, exped, reset, turned,
         turn_free) = named_semaphores(
            nc, ctx, "re", "w0_in w1_in queried q_in_sbuf scored score_in score_free step exp_ready exped reset "
            "turned turn_free")
        w_in = [w0_in, w1_in]
        scratch = ctx.enter_context(nc.sbuf_tensor("r_scratch", [P, 64], F32))
        iota16 = k.const[:, C_IOTA:C_IOTA + TOPK]

        def load(sp, s, m):
            sp.dma_start(w[:, s], d["w_query"][bass.ds(m, 1)].rearrange("o p k m -> p (o k) m")).then_inc(w_in[s], 16)

        with nc.Block("retrieve") as block:
            @block.sync
            def _(sp):
                for s in range(2):
                    load(sp, s, s)
                with sp.Fori(0, HEADS - 1) as i:
                    for s in range(2):
                        sp.wait_ge(scored, i * 2 + s + 1)
                        load(sp, s, i * 2 + (s + 2))

            @block.tensor
            def _(pe):
                with pe.Fori(0, HEADS) as i:
                    for s in range(2):
                        pe.wait_ge(w_in[s], i * 16 + 16)
                        pe.wait_ge(q_in_sbuf, i * 2)
                        for h in range(2):
                            last = accumulate(nc, k.ps[:, 2 * s + h, 0:H2],
                                              [(w[:, s, c, :], k.hT[:, c, h * H2:(h + 1) * H2]) for c in range(KD)])
                        last.then_inc(queried, 1)
                    for s in range(2):
                        pe.wait_ge(q_in_sbuf, i * 2 + s + 1)
                        pe.wait_ge(score_in, i * 2)
                        for t in range(TT):
                            r = rows_of(t)
                            out = k.ps[0:r, 4 + 2 * s, t * P:(t + 1) * P] if t < QT else k.ps[0:r, 5 + 2 * s, 0:P]
                            last = nc.tensor.matmul(out, qT[:, s, t * P:t * P + r], w[:, s, KD, :],
                                                    start=True, stop=True)
                        last.then_inc(scored, 1)
                pe.wait_ge(step, HEADS * STEPS)
                for j in range(3 * TT):
                    a, t = j // TT, j % TT
                    r = rows_of(t)
                    if j >= 4:
                        pe.wait_ge(turn_free, j - 3)
                    nc.tensor.transpose(k.ps[:, j % 4, 0:r], res[0:r, a, t, :],
                                        k.const[0:r, C_IDENT:C_IDENT + r]).then_inc(turned, 1)

            @block.scalar
            def _(act):
                with act.Fori(0, HEADS) as i:
                    for s in range(2):
                        act.wait_ge(queried, i * 2 + s + 1)
                        act.wait_ge(scored, i * 2)
                        nc.scalar.activation(qT[:, s, :].rearrange("p (h t) -> p h t", h=2),
                                             k.ps[:, 2 * s:2 * s + 2, 0:H2], ACT.Copy).then_inc(q_in_sbuf, 1)
                    for s in range(2):
                        act.wait_ge(scored, i * 2 + s + 1)
                        act.wait_ge(score_free, i * 2 + s + 1)
                        nc.scalar.activation(score[:, s, 0:QT, :], k.ps[:, 4 + 2 * s, :].rearrange("p (t c) -> p t c", t=QT),
                                             ACT.Copy)
                        nc.scalar.activation(score[0:SAMP, s, QT, :], k.ps[0:SAMP, 5 + 2 * s, 0:P],
                                             ACT.Copy).then_inc(score_in, 1)
                    act.wait_ge(exp_ready, i + 1)
                    nc.scalar.activation(best[:, :, :], best[:, :, :], ACT.Exp).then_inc(exped, 1)
                for j in range(3 * TT):
                    a, t = j // TT, j % TT
                    act.wait_ge(turned, j + 1)
                    nc.scalar.activation(f.pick[:, a, t * P:t * P + rows_of(t)], k.ps[:, j % 4, 0:rows_of(t)],
                                         ACT.Copy).then_inc(turn_free, 1)

            @block.vector
            def _(dve):
                nc.vector.memset(score[:, :, QT, :], 0.0).then_inc(reset, 1)
                dve.wait_ge(reset, 1)
                dve.sem_inc(score_free, 2)
                with dve.Fori(0, HEADS) as i:
                    n, waits = [0], [0]

                    def done(ins):
                        n[0] += 1
                        ins.then_inc(step, 1)

                    def after():
                        vector_wait(step, i * STEPS + n[0])

                    def vector_wait(sem, value):
                        dve.wait_ge(sem, value)
                        nc.vector.memset(scratch[:, waits[0]:waits[0] + 1], 0.0)
                        waits[0] += 1

                    def sixteen(value, spare, tops, index):
                        for t in range(TT):
                            done(nc.vector.max(tops[:, t, 0:8], value[:, t, :]))
                        after()
                        for t in range(TT):
                            nc.vector.max_index(index[:, t, 0:8], tops[:, t, 0:8], value[:, t, :])
                            done(nc.vector.match_replace(spare[:, t, :], tops[:, t, 0:8], value[:, t, :], REMOVED))
                        after()
                        for t in range(TT):
                            done(nc.vector.max(tops[:, t, 8:16], spare[:, t, :]))
                        after()
                        for t in range(TT):
                            last = nc.vector.max_index(index[:, t, 8:16], tops[:, t, 8:16], spare[:, t, :])
                            done(last)

                    for s in range(2):
                        vector_wait(score_in, i * 2 + s + 1)
                        sixteen(score[:, s], rest, top[:, s], at[:, s])
                        after()
                        nc.vector.tensor_copy(atf[:, s], at[:, s]).then_inc(score_free, 1)
                    for t in range(TT):
                        done(nc.vector.tensor_tensor(
                            cand[:, t, :].rearrange("p (a b) -> p a b", a=TOPK),
                            top[:, 0, t, :].unsqueeze(2).to_broadcast([P, TOPK, TOPK]),
                            top[:, 1, t, :].unsqueeze(1).to_broadcast([P, TOPK, TOPK]), ALU.add))
                    after()
                    sixteen(cand, left, best, where)
                    after()
                    done(nc.vector.tensor_scalar(part[:, 0], where[:, :, :], 4, None, ALU.logical_shift_right))
                    done(nc.vector.tensor_scalar(part[:, 1], where[:, :, :], TOPK - 1, None, ALU.bitwise_and))
                    after()
                    done(nc.vector.tensor_copy(partf[:, :, :, :], part[:, :, :, :]))
                    after()
                    for s in range(2):
                        for t in range(TT):
                            done(nc.vector.tensor_tensor(
                                hit[:, t], partf[:, s, t, :].unsqueeze(2).to_broadcast([P, TOPK, TOPK]),
                                iota16.unsqueeze(1).to_broadcast([P, TOPK, TOPK]), ALU.is_equal))
                        after()
                        for t in range(TT):
                            done(nc.vector.tensor_tensor(
                                hit[:, t], hit[:, t], atf[:, s, t, :].unsqueeze(1).to_broadcast([P, TOPK, TOPK]),
                                ALU.mult))
                        after()
                        done(nc.vector.tensor_reduce(res[:, s, :, bass.ds(i * TOPK, TOPK)], hit[:, :, :, :], AXX, ALU.add))
                        after()
                    done(nc.vector.tensor_copy(tot[:, :], best[:, :, 0]))
                    after()
                    nc.vector.tensor_tensor(best[:, :, :], best[:, :, :],
                                            tot[:, :].unsqueeze(2).to_broadcast([P, TT, TOPK]),
                                            ALU.subtract).then_inc(exp_ready, 1)
                    dve.wait_ge(exped, i + 1)
                    done(nc.vector.tensor_reduce(tot[:, :], best[:, :, :], AXX, ALU.add))
                    after()
                    done(nc.vector.reciprocal(tot[:, :], tot[:, :]))
                    after()
                    done(nc.vector.tensor_tensor(res[:, 2, :, bass.ds(i * TOPK, TOPK)], best[:, :, :],
                                                 tot[:, :].unsqueeze(2).to_broadcast([P, TT, TOPK]), ALU.mult))
                    after()
                    assert n[0] == STEPS, n[0]


STEPS = 3 * 4 * TT + TT + 3 + 2 * (2 * TT + 1) + 4


def gate_matrix(nc, k, f, sems, g):
    hot, product, bank_free = sems
    groups = T // GT
    first = C_IOTA + g * IP
    base = g * groups
    with nc.Block(f"gate_matrix{g}") as block:
        @block.vector
        def _(dve):
            with dve.Fori(0, groups // 2) as i:
                for s in range(2):
                    dve.wait_ge(product, i * 2 + (base + s))
                    for j in range(GT):
                        t = bass.ds(i * (2 * GT) + (s * GT + j), 1)
                        nc.vector.tensor_scalar(f.hotJ[:, s, j, :], k.const[:, C_IOTA:C_IOTA + NK], f.pick[:, 1, t],
                                                None, ALU.is_equal)
                        last = nc.vector.tensor_scalar(f.hotI[:, s, j, :], k.const[:, first:first + IP],
                                                       f.pick[:, 0, t], f.pick[:, 2, t], ALU.is_equal, ALU.mult)
                    last.then_inc(hot, 1)

        @block.tensor
        def _(pe):
            if g == 0:
                pe.sem_inc(bank_free, 4)
            with pe.Fori(0, groups // 4) as i:
                for s in range(4):
                    pe.wait_ge(hot, i * 4 + (base + s + 1))
                    pe.wait_ge(bank_free, i * 4 + (base + s + 1))
                    for j in range(GT):
                        last = nc.tensor.matmul(k.ps[:, s, j * IP:(j + 1) * IP], f.hotJ[:, s % 2, j, :],
                                                f.hotI[:, s % 2, j, :], start=True, stop=True)
                    last.then_inc(product, 1)

        @block.scalar
        def _(act):
            with act.Fori(0, groups // 4) as i:
                for s in range(4):
                    act.wait_ge(product, i * 4 + (base + s + 1))
                    nc.scalar.activation(f.gates[:, :, bass.ds(i * (4 * GT) + s * GT, GT)],
                                         k.ps[:, s, :].rearrange("p (t i) -> p i t", t=GT),
                                         ACT.Copy).then_inc(bank_free, 1)


def expert_pass(nc, k, d, f, sems, g):
    u_in, v_in, hidden, activated, weighted, mixed, added = sems
    n = IP // GB
    HU = 2 * GB
    YU = 2 * KD
    hb, yb, lb = g * n * HU, g * n * YU, g * n * 16

    def halves(h):
        return slice(h * H2, (h + 1) * H2)

    with nc.Block(f"expert_pass{g}") as block:
        @block.sync
        def _(sp):
            def load(s, b):
                sp.dma_start(f.u[:, s], d["u"][bass.ds(b * GB + (g * IP + s), 1)].rearrange("o p k m -> p (o k) m")
                             ).then_inc(u_in[s], 16)
            for s in range(GB):
                load(s, 0)
            with sp.Fori(0, n - 1) as b:
                for s in range(GB):
                    sp.wait_ge(hidden, b * HU + (hb + 2 * s + 2))
                    load(s, b + 1)

        @block.gpsimd
        def _(pool):
            def load(s, b):
                pool.dma_start(f.v[:, s], d["v"][bass.ds(b * GB + (g * IP + s), 1)].rearrange("o p m -> p (o m)")
                               ).then_inc(v_in[s], 16)
            for s in range(GB):
                load(s, 0)
            with pool.Fori(0, n - 1) as b:
                pool.wait_ge(mixed, b * YU + (yb + YU))
                for s in range(GB):
                    load(s, b + 1)

        @block.tensor
        def _(pe):
            def hide(b, first):
                for s in range(GB):
                    pe.wait_ge(u_in[s], b * 16 + (lb + 16))
                    for h in range(2):
                        if not first:
                            pe.wait_ge(activated, b * HU + (hb + 2 * s + h + 1 - HU))
                        accumulate(nc, k.ps[:, 2 * s + h, 0:H2],
                                   [(f.u[:, s, c, :], k.hT[:, c, halves(h)]) for c in range(KD)]).then_inc(hidden, 1)

            def mix(b):
                pe.wait_ge(weighted, b * HU + (hb + 2 * HU))
                for s in range(GB):
                    pe.wait_ge(v_in[s], b * 16 + (lb + 16))
                for c in range(KD):
                    for h in range(2):
                        y = 2 * c + h
                        pe.wait_ge(added, b * YU + (yb + y + 1))
                        for s in range(GB):
                            last = nc.tensor.matmul(k.ps[:, 4 + y % 4:5 + y % 4, 0:H2], f.v[:, s, c * P:(c + 1) * P],
                                                    f.gates[:, bass.ds(b * GB + s, 1), halves(h)],
                                                    start=s == 0, stop=s == GB - 1)
                        last.then_inc(mixed, 1)

            if g == 0:
                pe.sem_inc(added, 4)
            hide(0, True)
            with pe.Fori(0, n - 1) as b:
                hide(b + 1, False)
                mix(b)
            mix(n - 1)

        @block.scalar
        def _(act):
            if g == 0:
                act.sem_inc(weighted, HU)
            with act.Fori(0, n) as b:
                for s in range(GB):
                    for h in range(2):
                        j = 2 * s + h
                        act.wait_ge(hidden, b * HU + (hb + j + 1))
                        act.wait_ge(weighted, b * HU + (hb + j + 1))
                        nc.scalar.activation(f.act[:, s:s + 1, halves(h)], k.ps[:, j:j + 1, 0:H2],
                                             ACT.Gelu).then_inc(activated, 1)

        @block.vector
        def _(dve):
            def weight(b):
                for s in range(GB):
                    for h in range(2):
                        dve.wait_ge(activated, b * HU + (hb + 2 * s + h + 1))
                        w = f.gates[:, bass.ds(b * GB + s, 1), halves(h)]
                        nc.vector.tensor_tensor(w, w, f.act[:, s:s + 1, halves(h)], ALU.mult).then_inc(weighted, 1)

            def add(b):
                for c in range(KD):
                    for h in range(2):
                        y = 2 * c + h
                        dve.wait_ge(mixed, b * YU + (yb + y + 1))
                        x = k.xT[:, c:c + 1, halves(h)]
                        nc.vector.tensor_tensor(x, x, k.ps[:, 4 + y % 4:5 + y % 4, 0:H2], ALU.add).then_inc(added, 1)

            weight(0)
            with dve.Fori(0, n - 1) as b:
                weight(b + 1)
                add(b)
            add(n - 1)


def layer_embedding(nc, k, d):
    KP = 256 // P
    with ExitStack() as ctx:
        w = ctx.enter_context(nc.sbuf_tensor("le_w", [P, 2, KD + KP, P], F32))
        pT = ctx.enter_context(nc.sbuf_tensor("le_p", [P, KP, T], F32))
        gate = ctx.enter_context(nc.sbuf_tensor("le_gate", [P, 2, T], F32))
        p_in, w0_in, w1_in, gated, valued, gate_done, term, added = named_semaphores(
            nc, ctx, "le", "p_in w0_in w1_in gated valued gate_done term added")
        w_in = [w0_in, w1_in]

        def load(sp, s, m):
            sp.dma_start(w[:, s], d["w_ple"][bass.ds(m, 1)].rearrange("o p k m -> p (o k) m")).then_inc(w_in[s], 16)

        with nc.Block("layer_embedding") as block:
            @block.sync
            def _(sp):
                sp.dma_start(pT[:, :, :], d["pT"]).then_inc(p_in, 16)
                for s in range(2):
                    load(sp, s, s)
                with sp.Fori(0, KD // 2 - 1) as i:
                    for s in range(2):
                        sp.wait_ge(valued, i * 2 + s + 1)
                        load(sp, s, i * 2 + (s + 2))

            @block.tensor
            def _(pe):
                pe.wait_ge(p_in, 16)
                with pe.Fori(0, KD // 2) as i:
                    for s in range(2):
                        pe.wait_ge(w_in[s], i * 16 + 16)
                        pe.wait_ge(gate_done, i * 2)
                        for h in range(2):
                            last = accumulate(nc, k.ps[:, 4 * s + h, 0:H2],
                                              [(w[:, s, c, :], k.hT[:, c, h * H2:(h + 1) * H2]) for c in range(KD)])
                        last.then_inc(gated, 1)
                        pe.wait_ge(term, i * 2)
                        for h in range(2):
                            last = accumulate(nc, k.ps[:, 4 * s + 2 + h, 0:H2],
                                              [(w[:, s, KD + c, :], pT[:, c, h * H2:(h + 1) * H2]) for c in range(KP)])
                        last.then_inc(valued, 1)

            @block.scalar
            def _(act):
                with act.Fori(0, KD // 2) as i:
                    for s in range(2):
                        act.wait_ge(added, i * 2)
                        act.wait_ge(gated, i * 2 + s + 1)
                        nc.scalar.activation(gate[:, s, :].rearrange("p (h t) -> p h t", h=2),
                                             k.ps[:, 4 * s:4 * s + 2, 0:H2], ACT.Sigmoid).then_inc(gate_done, 1)

            @block.vector
            def _(dve):
                with dve.Fori(0, KD // 2) as i:
                    for s in range(2):
                        dve.wait_ge(gate_done, i * 2 + s + 1)
                        dve.wait_ge(valued, i * 2 + s + 1)
                        g = gate[:, s, :].rearrange("p (h t) -> p h t", h=2)
                        nc.vector.tensor_tensor(g, g, k.ps[:, 4 * s + 2:4 * s + 4, 0:H2], ALU.mult).then_inc(term, 1)
                        dve.wait_ge(term, i * 2 + s + 1)
                        x = k.xT[:, bass.ds(i * 2 + s, 1), :]
                        nc.vector.tensor_tensor(x, x, gate[:, s:s + 1, :], ALU.add).then_inc(added, 1)


def stream_step(nc, d):
    with ExitStack() as ctx:
        k = Core()

        def sb(name, shape, dtype=F32, c=ctx):
            return c.enter_context(nc.sbuf_tensor(name, shape, dtype))

        k.ps = ctx.enter_context(nc.psum_tensor("banks", [P, 8, 512], F32))
        k.xT = sb("xT", [P, KD, T])
        k.hT = sb("hT", [P, KD, T])
        k.const = sb("const", [P, C_END])
        k.gain = sb("gain", [P, G_END])
        k.rstd = sb("rstd", [P, T])
        norm_sems = named_semaphores(nc, ctx, "norm", "squared summed rooted inverted normed stored")
        norms = [0, 0, 0]

        def norm(name, src, dst, chunks, gain, store=None):
            with nc.sbuf_tensor(f"{name}_square", [P, 2, T], F32) as k.square:
                rms_norm(nc, k, name, norm_sems, norms[0], norms[1], src, dst, chunks, gain, store, norms[2])
            norms[0] += 1
            norms[2] += len(store or [])
            norms[1] += chunks

        load_inputs(nc, k, d)
        norm("norm_mix", lambda c: k.xT[:, c, :], lambda c: k.hT[:, c, :], KD, G_MIX)
        with ExitStack() as mixer:
            a = Core()
            a.merged = sb("merged", [P, KD, T], c=mixer)
            a.oA = sb("oA", [P, PAIRS, T], c=mixer)
            a.oB = sb("oB", [P, PAIRS, T], c=mixer)
            with ExitStack() as mla:
                a.proj = sb("proj", [P, NQ + NC + 1, T], c=mla)
                a.rope = sb("rope", [P, T], c=mla)
                a.kdup = sb("kdup", [P, T], c=mla)
                a.kdupS = sb("kdupS", [P, MLAK], c=mla)
                a.keyS = sb("keyS", [P, NC, MLAK], c=mla)
                a.value = sb("value", [P, QT, KVL], c=mla)
                a.valueS = sb("valueS", [P, PAST // P + 1, KVL], c=mla)
                latent_projection(nc, k, d, a)
                norm("norm_q", lambda c: a.proj[:, c, :], lambda c: a.proj[:, c, :], NQ, G_Q)
                norm("norm_kv", lambda c: a.proj[:, NQ + c, :], lambda c: a.proj[:, NQ + c, :], NC, G_KV,
                     [(d["o_latent"], a.proj[:, NQ:NQ + NC, :])])
                with nc.sbuf_tensor("turn", [P, T], F32) as a.turn:
                    rotary_key(nc, k, d, a)
                latent_attention(nc, k, d, a)
            band_attention(nc, k, d, a)
            gated_merge(nc, k, d, a)
            output_projection(nc, k, d, a)
        norm("norm_ffn", lambda c: k.xT[:, c, :], lambda c: k.hT[:, c, :], KD, G_FFN)
        with ExitStack() as ffn:
            f = Core()
            f.pick = sb("pick", [P, 3, T], c=ffn)
            retrieve(nc, k, d, f)
            f.gates = sb("gates", [P, IP, T], c=ffn)
            gate_sems = named_semaphores(nc, ffn, "gate", "hot product bank_free")
            u0, u1, v0, v1, *rest = named_semaphores(nc, ffn, "ex", "u0 u1 v0 v1 hidden activated weighted mixed added")
            for g in range(GPASS):
                with ExitStack() as c:
                    f.hotJ = sb(f"hotJ{g}", [P, 2, GT, NK], c=c)
                    f.hotI = sb(f"hotI{g}", [P, 2, GT, IP], c=c)
                    gate_matrix(nc, k, f, gate_sems, g)
                with ExitStack() as c:
                    f.u = sb(f"u{g}", [P, GB, KD, P], c=c)
                    f.v = sb(f"v{g}", [P, GB, D], c=c)
                    f.act = sb(f"act{g}", [P, GB, T], c=c)
                    expert_pass(nc, k, d, f, [[u0, u1], [v0, v1], *rest], g)
        norm("norm_ple", lambda c: k.xT[:, c, :], lambda c: k.hT[:, c, :], KD, G_PLE)
        layer_embedding(nc, k, d)
        norm("norm_final", lambda c: k.xT[:, c, :], lambda c: k.hT[:, c, :], KD, G_FIN,
             [(d["o_y"], k.hT[:, :, :])])


def kernel(**inputs):
    import concourse.bacc as bacc
    from concourse.bass_utils import run_bass_kernel_spmd

    x = {n: np.asarray(v) for n, v in inputs.items()}

    def blocks(w):
        kk, m = w.shape
        return np.ascontiguousarray(w.reshape(kk // P, P, m // P, P).transpose(2, 1, 0, 3))

    def feature_major(v):
        return np.ascontiguousarray(v.T.reshape(v.shape[1] // P, P, v.shape[0]).transpose(1, 0, 2))

    def columns(v):
        return v.reshape(-1, P).T

    def swapped(w):
        return np.concatenate([w[..., ROPE // 2:], w[..., :ROPE // 2]], -1)

    w_in = x["w_in"][0]
    o = np.cumsum([0, QL, KVL, ROPE, 512, 512, 512, D, D])
    kr = w_in[:, o[2]:o[3]]
    arrays = {}
    arrays["xT"] = feature_major(np.concatenate([x["x_prompt"][0], x["x_sample"][0]]))
    arrays["pT"] = feature_major(np.concatenate([x["p_prompt"][0, 0], x["p_sample"][0, 0]]))
    arrays["w_small"] = blocks(np.concatenate([w_in[:, :o[2]], kr, swapped(kr), np.zeros((D, 64), np.float32)], 1))
    for n, j in (("w_bq", 3), ("w_bk", 4), ("w_bv", 5)):
        arrays[n] = blocks(w_in[:, o[j]:o[j + 1]])
    arrays["w_merge"] = np.concatenate([blocks(w_in[:, o[6]:o[7]]), blocks(w_in[:, o[7]:o[8]]),
                                        blocks(x["w_a_proj"][0]), blocks(x["w_b_proj"][0])], 2)
    arrays["w_out"] = blocks(x["w_out"][0])
    keys = x["sub_keys"][0].reshape(2 * HEADS, NK, P).transpose(0, 2, 1)[:, :, None, :]
    arrays["w_query"] = np.concatenate([blocks(x["w_query"][0]), keys], 2)
    arrays["w_ple"] = np.concatenate([blocks(x["w_ple_gate"][0]), blocks(x["w_ple_proj"][0])], 2)
    uq = x["w_uq"][0].reshape(QL, HEADS, NOPE + ROPE)
    uq = np.concatenate([uq, swapped(uq[..., NOPE:])], -1)
    arrays["w_uq"] = uq.reshape(NQ, P, PAIRS, 2, P).transpose(2, 1, 3, 0, 4).reshape(PAIRS, P, -1)
    arrays["w_ukT"] = x["w_uk"][0].reshape(KVL, PAIRS, 2, NOPE).transpose(1, 3, 2, 0).reshape(PAIRS, NOPE, -1)
    arrays["w_uv"] = x["w_uv"][0].reshape(NC, P, PAIRS, 2, NOPE).transpose(2, 1, 3, 0, 4).reshape(PAIRS, P, -1)
    lat = x["cache_latent"][0, 0]
    arrays["cache_latT"] = feature_major(lat)
    arrays["cache_lat"] = lat.reshape(PAST // P, P, KVL).transpose(1, 0, 2)
    arrays["cache_krT"] = np.concatenate([x["cache_krope"][0, 0].T] * 2)
    bk = x["cache_band_k"][0, 0].reshape(WIN, PAIRS, P)
    bv = x["cache_band_v"][0, 0].reshape(WIN, PAIRS, P)
    arrays["cache_bkT"] = bk.transpose(1, 2, 0)
    arrays["cache_bv"] = bv.reshape(QT, P, PAIRS, P).transpose(2, 1, 0, 3)
    arrays["cache_bv_kept"] = bv[SAMP:].reshape(WIN - SAMP, PAIRS * P)
    rel = x["rel_bias"][0]
    clip = (rel.shape[1] - 1) // 2
    dist = np.arange(P)[:, None] - (np.arange(WIN + P) - WIN)[None]
    bias = rel[:, np.clip(dist, -clip, clip) + clip]
    bias[:, :64, WIN + 64:] = NEG
    arrays["bias"] = bias.reshape(PAIRS, 2, P, WIN + P).transpose(0, 2, 1, 3)
    dist = (WIN + np.arange(SAMP))[:, None] - np.arange(BANDK)[None]
    arrays["biasS"] = rel[:, np.clip(dist, -clip, clip) + clip].reshape(PAIRS, 2 * SAMP, BANDK)
    arrays["u"] = x["expert_u"][0].reshape(NK, NK, KD, P).transpose(0, 3, 2, 1)
    arrays["v"] = x["expert_v"][0].reshape(NK, NK, D)
    arrays["gains"] = np.concatenate([columns(x[n].reshape(-1)) for n in
                                      ("g_mix", "g_ffn", "g_ple", "g_final", "g_q_lora", "g_kv_lora")], 1)
    half = ROPE // 2
    freqs = (np.float32(10000.0) ** (-np.arange(half, dtype=np.float32) / np.float32(half))).astype(np.float32)
    pos = np.concatenate([np.arange(SEQ), PAST + np.arange(SAMP)]).astype(np.float32)
    ang = (freqs[:, None] * pos[None]).astype(np.float32)
    cos, sin = np.cos(ang), np.sin(ang)
    arrays["rope"] = np.concatenate([cos, cos, -sin, sin] * 2).astype(np.float32)
    const = np.zeros((P, C_END), np.float32)
    const[:, C_IDENT:C_IDENT + P] = np.eye(P)
    const[:, C_ONES:C_ONES + P] = 1.0
    const[:, C_IOTA:C_IOTA + P] = np.arange(P)
    const[:, C_DUP:C_DUP + P] = np.arange(P)[:, None] % ROPE == np.arange(P)[None] % ROPE
    const[0, C_MASKL:C_MASKL + 64] = 1.0
    const[0, C_MASKR + 64:C_MASKR + P] = NEG
    const[:, C_EPS] = EPS
    arrays["consts"] = const

    outs = {"o_y": [P, KD, T], "o_latent": [P, NC, T], "o_krope": [ROPE, T], "o_bkT": [PAIRS, P, SEQ],
            "o_bkS": [PAIRS, P, WIN], "o_bv": [PAIRS, P, QT, P], "o_bvS": [PAIRS, SAMP, P],
            "o_bvold": [WIN - SAMP, PAIRS * P]}
    nc = bacc.Bacc("TRN2", target_bir_lowering=False, num_devices=1)
    arrays = {n: np.ascontiguousarray(v) for n, v in arrays.items()}
    d = {n: nc.dram_tensor(f"in_{n}", v.shape, mybir.dt.from_np(v.dtype), kind="ExternalInput").ap()
         for n, v in arrays.items()}
    for n, shape in outs.items():
        d[n] = nc.dram_tensor(n, shape, F32, kind="ExternalOutput").ap()
    stream_step(nc, d)
    r = run_bass_kernel_spmd(nc, [{f"in_{n}": v for n, v in arrays.items()}], core_ids=[0]).results[0]

    def token_major(v):
        return v.transpose(2, 1, 0).reshape(v.shape[2], -1)

    y, latent = token_major(r["o_y"]), token_major(r["o_latent"])
    krope = r["o_krope"].T
    band_k = r["o_bkT"].transpose(2, 0, 1).reshape(1, 1, SEQ, HEADS, 64)
    band_kS = r["o_bkS"].transpose(2, 0, 1).reshape(1, 1, WIN, HEADS, 64)
    band_v = r["o_bv"].transpose(2, 1, 0, 3).reshape(1, 1, SEQ, HEADS, 64)
    band_vS = np.concatenate([r["o_bvold"], r["o_bvS"].transpose(1, 0, 2).reshape(SAMP, PAIRS * P)])
    return (y[None, :SEQ], y[None, SEQ:], latent[None, None, :SEQ], krope[None, None, :SEQ], band_k, band_v,
            latent[None, None, SEQ:], krope[None, None, SEQ:], band_kS, band_vS.reshape(1, 1, WIN, HEADS, 64))
```

```python
from contextlib import ExitStack

import numpy as np

import concourse.bass as bass
from concourse import mybir

F32 = mybir.dt.float32
F32R = mybir.dt.float32r
U32 = mybir.dt.uint32
ALU = mybir.AluOpType
ACT = mybir.ActivationFunctionType
AXX = mybir.AxisListType.X
AXXY = mybir.AxisListType.XY

P = 128
D = 1024
KD = D // P
SEQ, SAMP, PAST = 512, 32, 1024
T = SEQ + SAMP
H2 = T // 2
QL, KVL, NOPE, ROPE = 384, 256, 64, 32
HEADS, PAIRS = 8, 4
NQ, NC = QL // P, KVL // P
MLA_SCALE = float(NOPE + ROPE) ** -0.5
BAND_SCALE = 0.125
WIN = 512
BANDK = WIN + SAMP
MLAK = PAST + SAMP
MLA3 = MLAK // 3
NEG = -1e30
REMOVED = -3e38
EPS = 1e-6
QT = SEQ // P
TT = QT + 1
NK = 128
TOPK = 16
GB = 2
GT = 4

C_IDENT, C_ONES, C_IOTA, C_DUP, C_MASKL, C_MASKR, C_EPS, C_END = 0, 128, 256, 384, 512, 640, 768, 769
G_MIX, G_FFN, G_PLE, G_FIN, G_Q, G_KV, G_END = 0, 8, 16, 24, 32, 35, 37


def tensor_wait(nc, k, pe, bank, sem, value):
    pe.wait_ge(sem, value)
    nc.tensor.matmul(k.ps[:, bank, 511:512], k.const[:, C_ONES:C_ONES + P], k.const[:, C_ONES:C_ONES + 1],
                     start=True, stop=True)


def rows_of(tile):
    return P if tile < QT else SAMP


class Core:
    pass


def named_semaphores(nc, ctx, prefix, names):
    return [ctx.enter_context(nc.semaphore(f"{prefix}_{n}")) for n in names.split()]


def rms_norm(nc, k, name, sems, use, base, src, dst, chunks, gain, split=None, store=None, stores=0):
    squared, summed, rooted, inverted, normed, high, low, stored = sems
    with nc.Block(name) as block:
        @block.scalar
        def _(act):
            for c in range(chunks):
                if c >= 2:
                    act.wait_ge(summed, base + c - 1)
                nc.scalar.activation(k.square[:, c % 2, :], src(c), ACT.Square).then_inc(squared, 1)
            act.wait_ge(summed, base + chunks)
            nc.scalar.activation(k.rstd[:, :].rearrange("p (h t) -> p h t", h=2), k.ps[:, 0:2, 0:H2], ACT.Sqrt,
                                 bias=k.const[:, C_EPS:C_EPS + 1], scale=1.0 / (chunks * P)).then_inc(rooted, 1)
            if split is not None:
                for c in range(chunks):
                    act.wait_ge(normed, base + c + 1)
                    nc.scalar.activation(split[0][:, c, :], dst(c), ACT.Copy).then_inc(high, 1)

        @block.tensor
        def _(pe):
            for c in range(chunks):
                pe.wait_ge(squared, base + c + 1)
                for h in range(2):
                    last = nc.tensor.matmul(k.ps[:, h, 0:H2], k.const[:, C_ONES:C_ONES + P],
                                            k.square[:, c % 2, h * H2:(h + 1) * H2],
                                            start=c == 0, stop=c == chunks - 1)
                last.then_inc(summed, 1)

        @block.vector
        def _(dve):
            dve.wait_ge(rooted, use + 1)
            nc.vector.reciprocal(k.rstd[:, :], k.rstd[:, :]).then_inc(inverted, 1)
            dve.wait_ge(inverted, use + 1)
            for c in range(chunks):
                if split is not None and c >= 4:
                    dve.wait_ge(low, split[2] + c - 3)
                nc.vector.scalar_tensor_tensor(out=dst(c), in0=src(c), scalar=k.gain[:, gain + c:gain + c + 1],
                                               in1=k.rstd[:, :], op0=ALU.mult, op1=ALU.mult).then_inc(normed, 1)

        if split is not None:
            @block.gpsimd
            def _(pool):
                for c in range(chunks):
                    pool.wait_ge(high, split[2] + c + 1)
                    nc.gpsimd.tensor_tensor(split[1][:, c, :], dst(c), split[0][:, c, :].bitcast(F32),
                                            ALU.subtract).then_inc(low, 1)

        if store is not None:
            @block.sync
            def _(sp):
                sp.wait_ge(normed, base + chunks)
                for out, tile in store:
                    sp.dma_start(out, tile).then_inc(stored, 16)
                sp.wait_ge(stored, 16 * (stores + len(store)))


def accumulate(nc, out, pairs):
    n = len(pairs)
    for j, (lhs, rhs) in enumerate(pairs):
        last = nc.tensor.matmul(out, lhs, rhs, start=j == 0, stop=j == n - 1)
    return last


def split_products(weights, activations):
    (wh, wl), (xh, xl) = weights, activations
    return [(wh, xh), (wh, xl), (wl, xh)]


class Stream:

    def __init__(self, nc, ctx, name, dram, kc, blocks, body=2):
        self.nc, self.dram, self.kc, self.blocks, self.body = nc, dram, kc, blocks, body
        self.raw = ctx.enter_context(nc.sbuf_tensor(f"{name}_raw", [P, 2, kc * P], F32))
        self.high = ctx.enter_context(nc.sbuf_tensor(f"{name}_high", [P, 2, kc * P], F32R))
        self.low = ctx.enter_context(nc.sbuf_tensor(f"{name}_low", [P, 2, kc * P], F32R))
        in0, in1, self.high_done, self.low_done = named_semaphores(nc, ctx, name, "in0 in1 high_done low_done")
        self.loaded = (in0, in1)

    def load(self, sp, s, m):
        sp.dma_start(self.raw[:, s, :], self.dram[bass.ds(m, 1)].rearrange("o p k m -> p (o k m)")
                     ).then_inc(self.loaded[s], 16)

    def sync(self, sp):
        for s in range(2):
            self.load(sp, s, s)
        with sp.Fori(0, self.blocks // 2 - 1) as i:
            for s in range(2):
                sp.wait_ge(self.low_done, i * 2 + s + 1)
                self.load(sp, s, i * 2 + (s + 2))

    def round(self, act, i, q):
        s = q % 2
        act.wait_ge(self.loaded[s], i * (8 * self.body) + (q // 2 + 1) * 16)
        self.nc.scalar.activation(self.high[:, s, :], self.raw[:, s, :], ACT.Copy).then_inc(self.high_done, 1)

    def rest(self, pool):
        with pool.Fori(0, self.blocks // 2) as i:
            for s in range(2):
                pool.wait_ge(self.high_done, i * 2 + s + 1)
                self.nc.gpsimd.tensor_tensor(self.low[:, s, :], self.raw[:, s, :], self.high[:, s, :].bitcast(F32),
                                             ALU.subtract).then_inc(self.low_done, 1)

    def await_block(self, pe, i, q):
        pe.wait_ge(self.low_done, i * self.body + q + 1)

    def parts(self, q, c):
        cols = slice(c * P, (c + 1) * P)
        return self.high[:, q % 2, cols], self.low[:, q % 2, cols]


def halves(h):
    return slice(h * H2, (h + 1) * H2)


def both(pair, c, cols):
    return pair[0][:, c, cols], pair[1][:, c, cols]


def load_inputs(nc, k, d):
    with nc.Block("load") as block, nc.semaphore("load_done") as loaded:
        @block.sync
        def _(sp):
            sp.dma_start(k.xT[:, :, :], d["xT"]).then_inc(loaded, 16)
            sp.dma_start(k.const[:, :], d["consts"]).then_inc(loaded, 16)
            sp.dma_start(k.gain[:, :], d["gains"]).then_inc(loaded, 16)
            sp.wait_ge(loaded, 48)


def latent_projection(nc, k, d, a):
    blocks = NQ + NC + 1
    with ExitStack() as ctx:
        w = Stream(nc, ctx, "lp", d["w_small"], KD, blocks)
        product, bank_free = named_semaphores(nc, ctx, "lp", "product bank_free")
        with nc.Block("latent_projection") as block:
            @block.sync
            def _(sp):
                w.sync(sp)
                sp.dma_start(a.rope[:, :], d["rope"]).then_inc(a.loaded, 16)
                sp.dma_start(a.keyS[:, :, 0:PAST], d["cache_latT"]).then_inc(a.loaded, 16)
                sp.dma_start(a.kdupS[:, 0:PAST], d["cache_krT"]).then_inc(a.loaded, 16)
                sp.dma_start(a.valueS[:, 0:PAST // P, :], d["cache_lat"]).then_inc(a.loaded, 16)

            @block.gpsimd
            def _(pool):
                w.rest(pool)

            @block.tensor
            def _(pe):
                pe.sem_inc(bank_free, 4)
                with pe.Fori(0, blocks // 2) as i:
                    for s in range(2):
                        w.await_block(pe, i, s)
                        for h in range(2):
                            pe.wait_ge(bank_free, i * 4 + 2 * s + h + 1)
                            accumulate(nc, k.ps[:, 2 * s + h, 0:H2],
                                       [x for c in range(KD)
                                        for x in split_products(w.parts(s, c), both(k.h, c, halves(h)))]
                                       ).then_inc(product, 1)

            @block.scalar
            def _(act):
                def pair(i, more):
                    for s in range(2):
                        for h in range(2):
                            u = 2 * s + h
                            act.wait_ge(product, i * 4 + u + 1)
                            nc.scalar.activation(a.proj[:, bass.ds(i * 2 + s, 1), halves(h)],
                                                 k.ps[:, u:u + 1, 0:H2], ACT.Copy).then_inc(bank_free, 1)
                        if more:
                            w.round(act, i + 1, s)

                for s in range(2):
                    w.round(act, 0, s)
                with act.Fori(0, blocks // 2 - 1) as i:
                    pair(i, True)
                pair(blocks // 2 - 1, False)


def rotary_key(nc, k, d, a):
    with ExitStack() as ctx:
        turned, summed, copied, flipped, kept, stored = named_semaphores(
            nc, ctx, "rk", "turned summed copied flipped kept stored")
        with nc.Block("rotary_key") as block:
            @block.sync
            def _(sp):
                sp.wait_ge(copied, 2)
                sp.dma_start(d["o_krope"], a.kdup[0:ROPE, :]).then_inc(stored, 16)
                sp.wait_ge(stored, 16)

            @block.vector
            def _(dve):
                dve.wait_ge(a.loaded, 64)
                nc.vector.tensor_tensor(a.turn[0:NOPE, :], a.proj[0:NOPE, NQ + NC, :], a.rope[0:NOPE, :],
                                        ALU.mult).then_inc(turned, 1)
                for c in range(NC):
                    nc.vector.tensor_copy(a.keyS[:, c, PAST:MLAK], a.proj[:, NQ + c, SEQ:T])
                dve.wait_ge(copied, 2)
                nc.vector.tensor_copy(a.kdupS[:, PAST:MLAK], a.kdup[:, SEQ:T]).then_inc(kept, 1)

            @block.tensor
            def _(pe):
                for c in range(NC):
                    last = nc.tensor.transpose(k.ps[0:SAMP, 2, c * P:(c + 1) * P], a.proj[:, NQ + c, SEQ:T],
                                               k.const[:, C_IDENT:C_IDENT + P])
                last.then_inc(flipped, 1)
                pe.wait_ge(turned, 1)
                for h in range(2):
                    nc.tensor.matmul(k.ps[:, h, 0:H2], k.const[0:NOPE, C_DUP:C_DUP + P],
                                     a.turn[0:NOPE, halves(h)], start=True, stop=True).then_inc(summed, 1)

            @block.scalar
            def _(act):
                act.wait_ge(flipped, 1)
                nc.scalar.activation(a.valueS[0:SAMP, PAST // P, :], k.ps[0:SAMP, 2, 0:KVL], ACT.Copy).then_inc(kept, 1)
                for h in range(2):
                    act.wait_ge(summed, h + 1)
                    nc.scalar.activation(a.kdup[:, halves(h)], k.ps[:, h, 0:H2], ACT.Copy).then_inc(copied, 1)


def pair_count(i, par, per, done):
    return i * (2 * per) + (par * per + done)


def pair_after(i, par):
    return (i, 1) if par == 0 else (i + 1, 0)


def over_units(engine, units, step):
    with engine.Fori(0, PAIRS // 2 - 1) as i:
        for par in range(2):
            for u in range(units):
                step(i, par, u, True, True)
    for par in range(2):
        for u in range(units):
            step(PAIRS // 2 - 1, par, u, par == 0, False)


class Softmax:

    def __init__(self, nc, k, sems, units, sample_keys=0):
        self.nc, self.k, self.units, self.band, self.sample_keys = nc, k, units, units > 2 * QT, sample_keys
        (self.scored, self.biased, self.peaked, self.exped, self.scaled, self.turned, self.probT, self.mixed,
         self.kept, self.inv_done) = sems

    def rows(self, u):
        return P if u < 2 * QT else 2 * SAMP

    def keys(self, u):
        return P * (u % QT + 1) if u < 2 * QT else self.sample_keys

    def blocks(self, u):
        n = self.keys(u)
        return [(b, min(P, n - b)) for b in range(0, n, P)]

    def slot(self, par, u):
        return (par * self.units + u) % 2

    def count(self, i, par, u):
        return pair_count(i, par, self.units, u + 1)

    def ahead(self, i, par, u, n, more):
        if u + n < self.units:
            return i, par, u + n
        return (*pair_after(i, par), u + n - self.units) if more else None

    def tensor(self, pe, i, par, u, more, scores, project, values):
        nc, k = self.nc, self.k
        further = self.ahead(i, par, u, 2, more)
        if further is not None:
            pe.wait_ge(self.biased if self.band else self.exped, self.count(i, par, u))
            scores(*further)
        s = self.slot(par, u)
        if u < 2 * QT:
            pe.wait_ge(self.scaled, self.count(i, par, u))
        else:
            tensor_wait(nc, k, pe, 2, self.scaled, self.count(i, par, u))
        r = self.rows(u)
        for j, (b, n) in enumerate(self.blocks(u)):
            last = nc.tensor.transpose(k.ps[0:n, 3 + s, j * r:j * r + r], k.prob[0:r, s, b:b + n],
                                       k.const[0:r, C_IDENT:C_IDENT + r])
        last.then_inc(self.turned, 1)
        if more:
            project(*pair_after(i, par), u)
        pe.wait_ge(self.probT, self.count(i, par, u))
        pe.wait_ge(self.kept, self.count(i, par, u))
        values(i, par, u).then_inc(self.mixed, 1)

    def exponential(self, act, i, par, u):
        nc, k, s = self.nc, self.k, self.slot(par, u)
        r, n = self.rows(u), self.keys(u)
        act.wait_ge(self.peaked, self.count(i, par, u))
        src = k.biased[0:r, s, 0:n] if self.band else k.ps[0:r, s, 0:n]
        nc.scalar.activation(k.prob[0:r, s, 0:n], src, ACT.Exp, bias=k.peak[0:r, s:s + 1],
                             scale=1.0 if self.band else MLA_SCALE,
                             accum_out=k.total[0:r, s:s + 1]).then_inc(self.exped, 1)

    def transposed(self, act, i, par, u):
        nc, k, s = self.nc, self.k, self.slot(par, u)
        act.wait_ge(self.turned, self.count(i, par, u))
        r, blocks = self.rows(u), self.blocks(u)
        full = len([b for b in blocks if b[1] == P])
        last = nc.scalar.activation(k.probT[:, s, 0:full * r], k.ps[:, 3 + s, 0:full * r], ACT.Copy)
        for j in range(full, len(blocks)):
            n = blocks[j][1]
            last = nc.scalar.activation(k.probT[0:n, s, j * r:j * r + r], k.ps[0:n, 3 + s, j * r:j * r + r], ACT.Copy)
        last.then_inc(self.probT, 1)

    def scalar(self, act, i, par, u, more, collect, keep):
        unit = self.ahead(i, par, u, 2, more)
        if unit is not None:
            self.exponential(act, *unit)
        if more:
            collect(*pair_after(i, par), u)
        unit = self.ahead(i, par, u, 1, more)
        if unit is not None:
            self.transposed(act, *unit)
        act.wait_ge(self.mixed, self.count(i, par, u))
        keep(i, par, u).then_inc(self.kept, 1)

    def maxima(self, dve, i, par, u):
        nc, k, s = self.nc, self.k, self.slot(par, u)
        r, n = self.rows(u), self.keys(u)
        dve.wait_ge(self.scored, self.count(i, par, u))
        if not self.band:
            nc.vector.tensor_reduce(k.rawpeak[0:r, s:s + 1], k.ps[0:r, s, 0:n], AXX, ALU.max,
                                    negate=True).then_inc(self.biased, 1)
            dve.wait_ge(self.biased, self.count(i, par, u))
            nc.vector.tensor_scalar(k.peak[0:r, s:s + 1], k.rawpeak[0:r, s:s + 1], MLA_SCALE,
                                    None, ALU.mult).then_inc(self.peaked, 1)
            return
        if u < 2 * QT:
            q0 = P * (u % QT)
            nc.vector.tensor_tensor(k.biased[0:r, s, 0:n], k.ps[0:r, s, 0:n],
                                    k.bias[:, par, u // QT, WIN - q0:WIN - q0 + n], ALU.add).then_inc(self.biased, 1)
        else:
            nc.vector.tensor_tensor(k.biased[0:r, s, 0:WIN], k.ps[0:r, s, 0:WIN], k.biasS[:, par, 0:WIN], ALU.add)
            nc.vector.tensor_tensor(k.biased[0:r, s, WIN:n], k.ps[0:r, 2, 0:SAMP],
                                    k.biasS[:, par, WIN:n], ALU.add).then_inc(self.biased, 1)
        dve.wait_ge(self.biased, self.count(i, par, u))
        nc.vector.tensor_reduce(k.peak[0:r, s:s + 1], k.biased[0:r, s, 0:n], AXX, ALU.max,
                                negate=True).then_inc(self.peaked, 1)

    def vector(self, dve, i, par, u, more, await_bias=None):
        nc, k, s = self.nc, self.k, self.slot(par, u)
        unit = self.ahead(i, par, u, 1, more)
        if unit is not None:
            if unit[2] == 0 and await_bias is not None:
                await_bias(*unit[:2])
            self.maxima(dve, *unit)
        r, n = self.rows(u), self.keys(u)
        dve.wait_ge(self.exped, self.count(i, par, u))
        nc.vector.reciprocal(k.inverse[0:r, s:s + 1], k.total[0:r, s:s + 1]).then_inc(self.inv_done, 1)
        dve.wait_ge(self.inv_done, self.count(i, par, u))
        nc.vector.tensor_scalar(k.prob[0:r, s, 0:n], k.prob[0:r, s, 0:n], k.inverse[0:r, s:s + 1],
                                None, ALU.mult).then_inc(self.scaled, 1)


SOFTMAX_SEMS = "scored biased peaked exped scaled turned probT mixed kept inv_done"


def softmax_buffers(nc, k, ctx, p, keys, rows):
    k.prob = ctx.enter_context(nc.sbuf_tensor(f"{p}_prob", [P, 2, keys], F32))
    k.probT = ctx.enter_context(nc.sbuf_tensor(f"{p}_probT", [P, 2, rows], F32))
    k.peak, k.rawpeak, k.total, k.inverse = (
        ctx.enter_context(nc.sbuf_tensor(f"{p}_{n}", [P, 2], F32)) for n in ("peak", "rawpeak", "total", "inverse"))


def latent_attention(nc, k, d, a):
    UNITS, GROUPS = 2 * QT, 6
    with ExitStack() as ctx:
        softmax_buffers(nc, k, ctx, "ma", SEQ, SEQ)
        wq = ctx.enter_context(nc.sbuf_tensor("m_wq", [P, 2, 2, NQ, P], F32))
        wk = ctx.enter_context(nc.sbuf_tensor("m_wk", [P, 2, NC, P], F32))
        q = ctx.enter_context(nc.sbuf_tensor("m_q", [P, 2, 2, T], F32))
        kk = ctx.enter_context(nc.sbuf_tensor("m_k", [P, 2, 2, SEQ], F32))
        v = ctx.enter_context(nc.sbuf_tensor("m_v", [P, 2, QT, P], F32))
        w_in0, w_in1, wide_in, projected, collected, rotated, spread = named_semaphores(
            nc, ctx, "ma", "w_in0 w_in1 wide_in projected collected rotated spread")
        w_in = (w_in0, w_in1)
        sm = Softmax(nc, k, named_semaphores(nc, ctx, "ma", SOFTMAX_SEMS), UNITS)

        def load(sp, i, par):
            p = i * 2 + par
            sp.dma_start(wq[:, par].rearrange("p a k m -> p (a k m)"),
                         d["w_uq"][bass.ds(p, 1)].rearrange("o p m -> p (o m)")).then_inc(w_in[par], 16)
            sp.dma_start(wk[:, par].rearrange("p k m -> p (k m)"),
                         d["w_uk"][bass.ds(p, 1)].rearrange("o p m -> p (o m)")).then_inc(w_in[par], 16)

        def rows(hh):
            return slice(NOPE * hh, NOPE * (hh + 1))

        with nc.Block("latent_attention") as block:
            @block.sync
            def _(sp):
                load(sp, 0, 0)
                sp.dma_start(a.wuv[:, :, :], d["w_uv"]).then_inc(wide_in, 16)
                load(sp, 0, 1)
                sp.dma_start(a.wukT[:, :, :], d["w_ukT"]).then_inc(a.lift_in, 16)
                with sp.Fori(1, PAIRS // 2) as i:
                    for par in range(2):
                        sp.wait_ge(projected, i * (2 * GROUPS) + (par - 1) * GROUPS)
                        load(sp, i, par)

            @block.tensor
            def _(pe):
                def project(i, par, g):
                    if g >= GROUPS:
                        return
                    if g == 0:
                        pe.wait_ge(w_in[par], i * 32 + 32)
                    bank = (2, 7)[g % 2]
                    pe.wait_ge(collected, pair_count(i, par, GROUPS, g + 1))
                    pe.wait_ge(rotated, pair_count(i, par, 4, g + 1))
                    if g < 4:
                        last = accumulate(nc, k.ps[:, bank, 0:H2],
                                          [(wq[:, par, g // 2, c, :], a.proj[:, c, halves(g % 2)]) for c in range(NQ)])
                    elif g == 4:
                        last = accumulate(nc, k.ps[:, bank, 0:SEQ],
                                          [(wk[:, par, c, :], a.proj[:, NQ + c, 0:SEQ]) for c in range(NC)])
                    else:
                        for t in range(QT):
                            last = accumulate(nc, k.ps[:, bank, t * P:(t + 1) * P],
                                              [(a.proj[:, NQ + c, t * P:(t + 1) * P],
                                                a.wuv[:, c, bass.ds((i * 2 + par) * P, P)]) for c in range(NC)])
                    last.then_inc(projected, 1)

                def scores(i, par, u):
                    if u == 0:
                        pe.wait_ge(collected, pair_count(i, par, GROUPS, GROUPS + 2))
                        pe.wait_ge(rotated, pair_count(i, par, 4, 4 + 2))
                    hh, q0, n, s = u // QT, P * (u % QT), sm.keys(u), sm.slot(par, u)
                    nc.tensor.matmul(k.ps[:, s, 0:n], q[:, par, hh, q0:q0 + P], kk[:, par, hh, 0:n],
                                     start=True, stop=False)
                    nc.tensor.matmul(k.ps[:, s, q0:q0 + P], k.const[0:1, C_MASKL:C_MASKL + P],
                                     k.const[0:1, C_MASKR:C_MASKR + P], start=False, stop=True).then_inc(sm.scored, 1)

                def values(i, par, u):
                    s, r = sm.slot(par, u), rows(u // QT)
                    return accumulate(nc, k.ps[r, 5 + s, 0:P],
                                      [(v[:, par, j, r], k.probT[:, s, j * P:(j + 1) * P]) for j in range(u % QT + 1)])

                pe.wait_ge(wide_in, 16)
                for g in range(GROUPS):
                    project(0, 0, g)
                pe.wait_ge(spread, 4)
                for u in range(2):
                    scores(0, 0, u)
                over_units(pe, UNITS, lambda i, par, u, more, more2:
                           sm.tensor(pe, i, par, u, more, scores, project, values))

            @block.scalar
            def _(act):
                def collect(i, par, g):
                    if g >= GROUPS:
                        return
                    act.wait_ge(projected, pair_count(i, par, GROUPS, g + 1))
                    bank = (2, 7)[g % 2]
                    if g < 4:
                        hh, h = g // 2, g % 2
                        r = rows(hh)
                        if h == 1:
                            nc.scalar.activation(a.qS[r, bass.ds((i * 2 + par) * 2 + hh, 1), :],
                                                 k.ps[r, bank:bank + 1, H2 - SAMP:H2], ACT.Copy)
                        last = nc.scalar.activation(q[r, par, hh, halves(h)], k.ps[r, bank, 0:H2], ACT.Copy)
                    elif g == 4:
                        for hh in range(2):
                            last = nc.scalar.activation(kk[rows(hh), par, hh, :], k.ps[rows(hh), bank, 0:SEQ], ACT.Copy)
                    else:
                        last = nc.scalar.activation(v[:, par].rearrange("p t c -> p (t c)"), k.ps[:, bank, :], ACT.Copy)
                    last.then_inc(collected, 1)

                def keep(i, par, u):
                    s, r, q0 = sm.slot(par, u), rows(u // QT), P * (u % QT)
                    return nc.scalar.activation(a.oA[r, bass.ds(i * 2 + par, 1), q0:q0 + P],
                                                k.ps[r, 5 + s:6 + s, 0:P], ACT.Copy)

                act.sem_inc(collected, 2)
                act.sem_inc(sm.kept, 2)
                for g in range(GROUPS):
                    collect(0, 0, g)
                for u in range(2):
                    sm.exponential(act, 0, 0, u)
                sm.transposed(act, 0, 0, 0)
                over_units(act, UNITS, lambda i, par, u, more, more2:
                           sm.scalar(act, i, par, u, more, collect, keep))

            @block.vector
            def _(dve):
                def rotate(i, par, g):
                    if g >= 4:
                        return
                    dve.wait_ge(projected, pair_count(i, par, GROUPS, g + 1))
                    hh, h, bank = g // 2, g % 2, (2, 7)[g % 2]
                    r = rows(1 - hh)
                    if h == 1:
                        nc.vector.tensor_tensor(a.qS[r, bass.ds((i * 2 + par) * 2 + hh, 1), :],
                                                k.ps[r, bank:bank + 1, H2 - SAMP:H2],
                                                a.rope[r, SEQ:T].unsqueeze(1), ALU.mult)
                    nc.vector.tensor_tensor(q[r, par, hh, halves(h)], k.ps[r, bank, 0:H2], a.rope[r, halves(h)],
                                            ALU.mult).then_inc(rotated, 1)

                def step(i, par, u, more, more2):
                    sm.vector(dve, i, par, u, more)
                    if more:
                        rotate(*pair_after(i, par), u)

                dve.sem_inc(rotated, 2)
                for par in range(2):
                    for hh in range(2):
                        r = rows(1 - hh)
                        nc.vector.tensor_copy(kk[r, par, hh, :], a.kdup[r, 0:SEQ]).then_inc(spread, 1)
                for g in range(4):
                    rotate(0, 0, g)
                sm.maxima(dve, 0, 0, 0)
                over_units(dve, UNITS, step)


def latent_sample(nc, k, d, a):
    TILES = HEADS * SAMP // P
    PER = HEADS // TILES
    KB = PAST // P + 1
    with ExitStack() as ctx:
        prob = ctx.enter_context(nc.sbuf_tensor("s_prob", [P, TILES, MLAK], F32))
        probT = ctx.enter_context(nc.sbuf_tensor("s_probT", [P, TILES, KB * P], F32))
        ql = ctx.enter_context(nc.sbuf_tensor("s_ql", [P, NC, HEADS, SAMP], F32))
        qr = ctx.enter_context(nc.sbuf_tensor("s_qr", [P, HEADS, SAMP], F32))
        ol = ctx.enter_context(nc.sbuf_tensor("s_ol", [P, NC, HEADS, SAMP], F32))
        rawpeak, peak, total, inverse = (ctx.enter_context(nc.sbuf_tensor(f"s_{n}", [P, TILES], F32))
                                         for n in ("rawpeak", "peak", "total", "inverse"))
        (lifted, in_sbuf, cleared, packed, scored, maximal, peaked, exped, inverted, scaled, turned, copied, mixed,
         kept, lowered, stored) = named_semaphores(
            nc, ctx, "ls", "lifted in_sbuf cleared packed scored maximal peaked exped inverted scaled turned copied "
            "mixed kept lowered stored")

        def rows(hh):
            return slice(NOPE * hh, NOPE * (hh + 1))

        with nc.Block("latent_sample") as block:
            @block.gpsimd
            def _(pool):
                nc.gpsimd.memset(qr[:, :, :], 0.0).then_inc(cleared, 1)

            @block.tensor
            def _(pe):
                pe.wait_ge(a.lift_in, 16)
                for hh in range(2):
                    for c in range(NC):
                        for p in range(PAIRS):
                            last = nc.tensor.matmul(k.ps[:, 4 + 2 * hh + c, p * SAMP:(p + 1) * SAMP],
                                                    a.wukT[rows(hh), p, c * P:(c + 1) * P],
                                                    a.qS[rows(hh), 2 * p + hh, :], start=True, stop=True)
                    last.then_inc(lifted, 1)
                pe.wait_ge(in_sbuf, 2)
                pe.wait_ge(packed, 2)
                for t in range(TILES):
                    heads = slice(t * PER, (t + 1) * PER)
                    for j in range(3):
                        keys = slice(j * MLA3, (j + 1) * MLA3)
                        last = accumulate(nc, k.ps[:, 3 * t + j, 0:MLA3],
                                          [(ql[:, c, heads, :].rearrange("p h t -> p (h t)"), a.keyS[:, c, keys])
                                           for c in range(NC)]
                                          + [(qr[:, heads, :].rearrange("p h t -> p (h t)"), a.kdupS[:, keys])])
                    last.then_inc(scored, 1)
                for t in range(TILES):
                    pe.wait_ge(scaled, t + 1)
                    for j in range(KB):
                        n = min(P, MLAK - j * P)
                        last = nc.tensor.transpose(k.ps[0:n, 3 * t + j // 4, (j % 4) * P:(j % 4 + 1) * P],
                                                   prob[:, t, j * P:j * P + n], k.const[:, C_IDENT:C_IDENT + P])
                        if j % 4 == 3 or j == KB - 1:
                            last.then_inc(turned, 1)
                for t in range(TILES):
                    pe.wait_ge(copied, 3 * t + 3)
                    for c in range(NC):
                        last = accumulate(nc, k.ps[:, 6 + t, c * P:(c + 1) * P],
                                          [(a.valueS[0:min(P, MLAK - j * P), j, c * P:(c + 1) * P],
                                            probT[0:min(P, MLAK - j * P), t, j * P:(j + 1) * P]) for j in range(KB)])
                    last.then_inc(mixed, 1)
                pe.wait_ge(kept, TILES)
                for head in range(HEADS):
                    last = accumulate(nc, k.ps[rows(head % 2), 0, (head // 2) * SAMP:(head // 2 + 1) * SAMP],
                                      [(a.wuv[:, c, head * NOPE:(head + 1) * NOPE], ol[:, c, head, :])
                                       for c in range(NC)])
                last.then_inc(lowered, 1)

            @block.scalar
            def _(act):
                for hh in range(2):
                    act.wait_ge(lifted, hh + 1)
                    for c in range(NC):
                        last = nc.scalar.activation(
                            ql[:, c].rearrange("p (g h) t -> p g h t", h=2)[:, :, hh, :],
                            k.ps[:, 4 + 2 * hh + c, 0:PAIRS * SAMP].rearrange("p (g t) -> p g t", g=PAIRS), ACT.Copy)
                    last.then_inc(in_sbuf, 1)
                for t in range(TILES):
                    act.wait_ge(peaked, t + 1)
                    nc.scalar.activation(prob[:, t, :].rearrange("p (a b) -> p a b", a=3),
                                         k.ps[:, 3 * t:3 * t + 3, 0:MLA3], ACT.Exp, bias=peak[:, t:t + 1],
                                         scale=MLA_SCALE, accum_out=total[:, t:t + 1]).then_inc(exped, 1)
                for t in range(TILES):
                    for j in range(3):
                        act.wait_ge(turned, 3 * t + j + 1)
                        n = P if j < 2 else MLAK - 8 * P
                        w = 4 * P if j < 2 else P
                        nc.scalar.activation(probT[0:n, t, 4 * j * P:4 * j * P + w], k.ps[0:n, 3 * t + j, 0:w],
                                             ACT.Copy).then_inc(copied, 1)
                for t in range(TILES):
                    act.wait_ge(mixed, t + 1)
                    nc.scalar.activation(ol[:, :, t * PER:(t + 1) * PER, :].rearrange("p c h t -> p c (h t)"),
                                         k.ps[:, 6 + t, 0:NC * P].rearrange("p (c m) -> p c m", c=NC),
                                         ACT.Copy).then_inc(kept, 1)
                act.wait_ge(lowered, 1)
                nc.scalar.activation(a.oA[:, :, SEQ:T], k.ps[:, 0, 0:PAIRS * SAMP].rearrange("p (c t) -> p c t", c=PAIRS),
                                     ACT.Copy).then_inc(stored, 1)

            @block.vector
            def _(dve):
                dve.wait_ge(cleared, 1)
                for hh in range(2):
                    r = rows(1 - hh)
                    nc.vector.tensor_copy(qr[r].rearrange("p (c h) t -> p c h t", h=2)[:, :, hh, :],
                                          a.qS[r].rearrange("p (c h) t -> p c h t", h=2)[:, :, hh, :]).then_inc(packed, 1)
                for t in range(TILES):
                    dve.wait_ge(scored, t + 1)
                    nc.vector.tensor_reduce(rawpeak[:, t:t + 1], k.ps[:, 3 * t:3 * t + 3, 0:MLA3], AXXY, ALU.max,
                                            negate=True).then_inc(maximal, 1)
                    dve.wait_ge(maximal, t + 1)
                    nc.vector.tensor_scalar(peak[:, t:t + 1], rawpeak[:, t:t + 1], MLA_SCALE, None,
                                            ALU.mult).then_inc(peaked, 1)
                for t in range(TILES):
                    dve.wait_ge(exped, t + 1)
                    nc.vector.reciprocal(inverse[:, t:t + 1], total[:, t:t + 1]).then_inc(inverted, 1)
                    dve.wait_ge(inverted, t + 1)
                    nc.vector.tensor_scalar(prob[:, t, :], prob[:, t, :], inverse[:, t:t + 1], None,
                                            ALU.mult).then_inc(scaled, 1)


def band_attention(nc, k, d, a):
    UNITS, GROUPS = 2 * QT + 1, 7
    with ExitStack() as ctx:
        softmax_buffers(nc, k, ctx, "ba", BANDK, SEQ)
        k.biased = ctx.enter_context(nc.sbuf_tensor("biased", [P, 2, BANDK], F32))
        k.bias = ctx.enter_context(nc.sbuf_tensor("bias", [P, 2, 2, WIN + P], F32))
        k.biasS = ctx.enter_context(nc.sbuf_tensor("biasS", [2 * SAMP, 2, BANDK], F32))
        raw = [ctx.enter_context(nc.sbuf_tensor(f"bw_{n}", [P, KD * P], F32)) for n in "qkv"]
        high = [ctx.enter_context(nc.sbuf_tensor(f"bw_high_{n}", [P, KD * P], F32R)) for n in "qkv"]
        low = [ctx.enter_context(nc.sbuf_tensor(f"bw_low_{n}", [P, KD * P], F32R)) for n in "qkv"]
        q = ctx.enter_context(nc.sbuf_tensor("b_q", [P, 2, T], F32))
        kk = ctx.enter_context(nc.sbuf_tensor("b_k", [P, 2, SEQ + BANDK], F32))
        v = ctx.enter_context(nc.sbuf_tensor("b_v", [P, 2, 2 * QT + 1, P], F32))
        sample = [ctx.enter_context(nc.sbuf_tensor(f"b_sample_{n}", [P, KD, P], F32R)) for n in ("high", "low")]
        (wq_in, wk_in, wv_in, cache_in0, cache_in1, bias_in0, bias_in1, stored0, stored1, moved, w_high, w_low,
         projected, collected, sampled) = named_semaphores(
            nc, ctx, "ba", "wq_in wk_in wv_in cache_in0 cache_in1 bias_in0 bias_in1 stored0 stored1 moved w_high w_low "
            "projected collected sampled")
        w_in, cache_in, bias_in = (wq_in, wk_in, wv_in), (cache_in0, cache_in1), (bias_in0, bias_in1)
        stored = (stored0, stored1)
        sm = Softmax(nc, k, named_semaphores(nc, ctx, "ba", SOFTMAX_SEMS), UNITS, BANDK)

        def one(name, i, par):
            return d[name][bass.ds(i * 2 + par, 1)]

        def load_weight(sp, j, i, par):
            sp.dma_start(raw[j][:, :], one(("w_bq", "w_bk", "w_bv")[j], i, par).rearrange("o p k m -> p (o k m)")
                         ).then_inc(w_in[j], 16)

        def load_cache(sp, i, par):
            sp.dma_start(kk[:, par, SEQ:SEQ + WIN], one("cache_bkT", i, par).rearrange("o p t -> p (o t)")
                         ).then_inc(cache_in[par], 16)
            sp.dma_start(v[:, par, QT:2 * QT, :], one("cache_bv", i, par).rearrange("o p n c -> p (o n) c")
                         ).then_inc(cache_in[par], 16)
            sp.dma_start(k.bias[:, par], one("bias", i, par).rearrange("o p h m -> p (o h) m")).then_inc(bias_in[par], 16)
            sp.dma_start(k.biasS[:, par, :], one("biasS", i, par).rearrange("o p m -> p (o m)")
                         ).then_inc(bias_in[par], 16)

        def store(sp, i, par):
            sp.wait_ge(collected, pair_count(i, par, GROUPS, GROUPS + 1))
            sp.wait_ge(cache_in[par], i * 32 + 32)
            for name, dims, tile in (("o_bkT", "o p t -> p (o t)", kk[:, par, 0:SEQ]),
                                     ("o_bkS", "o p t -> p (o t)", kk[:, par, SEQ + SAMP:SEQ + BANDK]),
                                     ("o_bv", "o p n c -> p (o n) c", v[:, par, 0:QT, :]),
                                     ("o_bvS", "o p c -> p (o c)", v[0:SAMP, par, 2 * QT, :])):
                sp.dma_start(one(name, i, par).rearrange(dims), tile).then_inc(stored[par], 16)

        with nc.Block("band_attention") as block:
            @block.sync
            def _(sp):
                for j in range(3):
                    load_weight(sp, j, 0, 0)
                load_cache(sp, 0, 0)
                for j in range(3):
                    sp.wait_ge(w_low, j + 1)
                    load_weight(sp, j, 0, 1)
                load_cache(sp, 0, 1)
                sp.dma_start(d["o_bvold"], d["cache_bv_kept"]).then_inc(moved, 16)
                with sp.Fori(0, PAIRS // 2 - 1) as i:
                    for par in range(2):
                        store(sp, i, par)
                        for j in range(3):
                            sp.wait_ge(w_low, pair_count(i, par, 3, 3 + j + 1))
                            load_weight(sp, j, i + 1, par)
                        sp.wait_ge(sm.mixed, sm.count(i, par, UNITS - 1))
                        sp.wait_ge(stored[par], i * 64 + 64)
                        load_cache(sp, i + 1, par)
                for par in range(2):
                    store(sp, PAIRS // 2 - 1, par)
                    sp.wait_ge(stored[par], PAIRS // 2 * 64)
                sp.wait_ge(moved, 16)

            @block.gpsimd
            def _(pool):
                with pool.Fori(0, PAIRS) as p:
                    for j in range(3):
                        pool.wait_ge(w_high, p * 3 + j + 1)
                        nc.gpsimd.tensor_tensor(low[j][:, :], raw[j][:, :], high[j][:, :].bitcast(F32),
                                                ALU.subtract).then_inc(w_low, 1)

            @block.tensor
            def _(pe):
                def project(i, par, g):
                    if g >= GROUPS:
                        return
                    j = min(g // 2, 2)
                    if g == 6:
                        pe.wait_ge(sampled, 2)
                    if g % 2 == 0 and g < 6:
                        pe.wait_ge(w_low, pair_count(i, par, 3, j + 1))
                    pe.wait_ge(collected, pair_count(i, par, GROUPS, g + 1))

                    def w(c):
                        return high[j][:, c * P:(c + 1) * P], low[j][:, c * P:(c + 1) * P]

                    if g < 4:
                        last = accumulate(nc, k.ps[:, 7, 0:H2],
                                          [x for c in range(KD) for x in split_products(w(c), both(k.h, c, halves(g % 2)))])
                    else:
                        for t in range(2 * (g - 4), min(2 * (g - 3), TT)):
                            o, cols = (t % 2) * P, slice(t * P, (t + 1) * P)
                            last = accumulate(nc, k.ps[:, 7, o:o + P],
                                              [x for c in range(KD) for x in split_products(
                                                  both(k.h, c, cols) if t < QT else both(sample, c, slice(0, P)), w(c))])
                    last.then_inc(projected, 1)

                def scores(i, par, u):
                    if u == 0:
                        pe.wait_ge(collected, pair_count(i, par, GROUPS, GROUPS + 1))
                    s = sm.slot(par, u)
                    if u < 2 * QT:
                        a0, q0 = 64 * (u // QT), P * (u % QT)
                        last = nc.tensor.matmul(k.ps[:, s, 0:sm.keys(u)], q[a0:a0 + 64, par, q0:q0 + P],
                                                kk[a0:a0 + 64, par, 0:sm.keys(u)], start=True, stop=True)
                    else:
                        tensor_wait(nc, k, pe, 2, cache_in[par], i * 32 + 32)
                        for hh in range(2):
                            a0 = 64 * hh
                            for bank, k0, n in ((s, SEQ, WIN), (2, SEQ + WIN, SAMP)):
                                last = nc.tensor.matmul(k.ps[SAMP * hh:SAMP * (hh + 1), bank, 0:n],
                                                        q[a0:a0 + 64, par, SEQ:T], kk[a0:a0 + 64, par, k0:k0 + n],
                                                        start=True, stop=True)
                    last.then_inc(sm.scored, 1)

                def values(i, par, u):
                    s = sm.slot(par, u)
                    if u < 2 * QT:
                        a0 = 64 * (u // QT)
                        return accumulate(nc, k.ps[a0:a0 + 64, 5 + s, 0:P],
                                          [(v[:, par, j, a0:a0 + 64], k.probT[:, s, j * P:(j + 1) * P])
                                           for j in range(u % QT + 1)])
                    for hh in range(2):
                        a0, r = 64 * hh, 2 * SAMP
                        last = accumulate(nc, k.ps[a0:a0 + 64, 5 + s, 0:SAMP],
                                          [(v[0:n, par, QT + j, a0:a0 + 64],
                                            k.probT[0:n, s, j * r + SAMP * hh:j * r + SAMP * (hh + 1)])
                                           for j, (_, n) in enumerate(sm.blocks(u))])
                    return last

                for g in range(GROUPS):
                    project(0, 0, g)
                for u in range(2):
                    scores(0, 0, u)
                over_units(pe, UNITS, lambda i, par, u, more, more2:
                           sm.tensor(pe, i, par, u, more, scores, project, values))

            @block.scalar
            def _(act):
                def round_weight(j, i, par):
                    act.wait_ge(w_in[j], pair_count(i, par, 16, 16))
                    nc.scalar.activation(high[j][:, :], raw[j][:, :], ACT.Copy).then_inc(w_high, 1)

                def collect(i, par, g, further):
                    if g >= GROUPS:
                        return
                    act.wait_ge(projected, pair_count(i, par, GROUPS, g + 1))
                    if g < 2:
                        last = nc.scalar.activation(q[:, par, halves(g)], k.ps[:, 7, 0:H2], ACT.Copy, scale=BAND_SCALE)
                    elif g == 2:
                        act.wait_ge(cache_in[par], i * 32 + 32)
                        last = nc.scalar.activation(kk[:, par, 0:H2], k.ps[:, 7, 0:H2], ACT.Copy)
                    elif g == 3:
                        nc.scalar.activation(kk[:, par, H2:SEQ], k.ps[:, 7, 0:SEQ - H2], ACT.Copy)
                        last = nc.scalar.activation(kk[:, par, SEQ + WIN:SEQ + BANDK], k.ps[:, 7, SEQ - H2:H2], ACT.Copy)
                    elif g < 6:
                        t = 2 * (g - 4)
                        last = nc.scalar.activation(v[:, par, t:t + 2, :].rearrange("p t c -> p (t c)"),
                                                    k.ps[:, 7, 0:2 * P], ACT.Copy)
                    else:
                        last = nc.scalar.activation(v[0:SAMP, par, 2 * QT, :], k.ps[0:SAMP, 7, 0:P], ACT.Copy)
                    last.then_inc(collected, 1)
                    if further and g in (1, 3, 6):
                        round_weight(min(g // 2, 2), *pair_after(i, par))

                def keep(i, par, u):
                    s, p = sm.slot(par, u), bass.ds(i * 2 + par, 1)
                    if u < 2 * QT:
                        a0, q0 = 64 * (u // QT), P * (u % QT)
                        return nc.scalar.activation(a.oB[a0:a0 + 64, p, q0:q0 + P],
                                                    k.ps[a0:a0 + 64, 5 + s:6 + s, 0:P], ACT.Copy)
                    return nc.scalar.activation(a.oB[:, p, SEQ:T], k.ps[:, 5 + s:6 + s, 0:SAMP], ACT.Copy)

                act.sem_inc(collected, 1)
                act.sem_inc(sm.kept, 2)
                for j in range(3):
                    round_weight(j, 0, 0)
                for g in range(GROUPS):
                    collect(0, 0, g, True)
                for u in range(2):
                    sm.exponential(act, 0, 0, u)
                sm.transposed(act, 0, 0, 0)
                over_units(act, UNITS, lambda i, par, u, more, more2:
                           sm.scalar(act, i, par, u, more, lambda i, par, g: collect(i, par, g, more2), keep))

            @block.vector
            def _(dve):
                def await_bias(i, par):
                    dve.wait_ge(bias_in[par], i * 32 + 32)

                for x, out in zip(k.h, sample):
                    nc.vector.tensor_copy(out[:, :, :].rearrange("p c (n t) -> p c n t", t=SAMP),
                                          x[:, :, SEQ:T].unsqueeze(2).to_broadcast([P, KD, P // SAMP, SAMP])
                                          ).then_inc(sampled, 1)
                await_bias(0, 0)
                sm.maxima(dve, 0, 0, 0)
                over_units(dve, UNITS, lambda i, par, u, more, more2:
                           sm.vector(dve, i, par, u, more, await_bias))


def gated_merge(nc, k, d, a):
    with ExitStack() as ctx:
        w = Stream(nc, ctx, "gm", d["w_merge"], KD, 3 * KD, 6)
        o = [[ctx.enter_context(nc.sbuf_tensor(f"gm_o{b}{p}", [P, PAIRS, T], F32R)) for p in ("high", "low")]
             for b in range(2)]
        gate = ctx.enter_context(nc.sbuf_tensor("gm_gate", [P, 2, T], F32))
        gated, valued, gate_done, term, merged, o_high, o_low, m_high, m_low = named_semaphores(
            nc, ctx, "gm", "gated valued gate_done term merged o_high o_low m_high m_low")

        with nc.Block("gated_merge") as block:
            @block.sync
            def _(sp):
                w.sync(sp)

            @block.gpsimd
            def _(pool):
                w.rest(pool)

            @block.tensor
            def _(pe):
                with pe.Fori(0, KD // 2) as i:
                    for s in range(2):
                        for b in range(2):
                            w.await_block(pe, i, 3 * s + b)
                            pe.wait_ge(gate_done, i * 4 + 2 * s + 1)
                            for h in range(2):
                                last = accumulate(nc, k.ps[:, 2 * b + h, 0:H2],
                                                  [x for c in range(KD)
                                                   for x in split_products(w.parts(3 * s + b, c), both(k.h, c, halves(h)))])
                            last.then_inc(gated, 1)
                        w.await_block(pe, i, 3 * s + 2)
                        pe.wait_ge(o_low, 2 * PAIRS)
                        pe.wait_ge(term, i * 4 + 2 * s + 1)
                        for b in range(2):
                            for h in range(2):
                                last = accumulate(nc, k.ps[:, 4 + 2 * b + h, 0:H2],
                                                  [x for c in range(PAIRS)
                                                   for x in split_products(w.parts(3 * s + 2, b * PAIRS + c),
                                                                           both(o[b], c, halves(h)))])
                            last.then_inc(valued, 1)

            @block.scalar
            def _(act):
                def pair(i, more):
                    for s in range(2):
                        act.wait_ge(merged, i * 2 + s + 1)
                        for b in range(2):
                            act.wait_ge(gated, i * 4 + 2 * s + b + 1)
                            nc.scalar.activation(gate[:, b, :].rearrange("p (h t) -> p h t", h=2),
                                                 k.ps[:, 2 * b:2 * b + 2, 0:H2], ACT.Sigmoid).then_inc(gate_done, 1)
                            ahead(i, 3 * s + b, more)
                        act.wait_ge(valued, i * 4 + 2 * s + 2)
                        ahead(i, 3 * s + 2, more)

                def ahead(i, q, more):
                    if q < 4:
                        w.round(act, i, q + 2)
                    elif more:
                        w.round(act, i + 1, q - 4)

                act.sem_inc(gate_done, 1)
                for q in range(2):
                    w.round(act, 0, q)
                for b, x in enumerate((a.oA, a.oB)):
                    for c in range(PAIRS):
                        nc.scalar.activation(o[b][0][:, c, :], x[:, c, :], ACT.Copy).then_inc(o_high, 1)
                with act.Fori(0, KD // 2 - 1) as i:
                    pair(i, True)
                pair(KD // 2 - 1, False)

            @block.vector
            def _(dve):
                dve.sem_inc(term, 1)
                dve.sem_inc(merged, 1)
                for b, x in enumerate((a.oA, a.oB)):
                    for c in range(PAIRS):
                        dve.wait_ge(o_high, b * PAIRS + c + 1)
                        nc.vector.tensor_tensor(o[b][1][:, c, :], x[:, c, :], o[b][0][:, c, :].bitcast(F32),
                                                ALU.subtract).then_inc(o_low, 1)
                with dve.Fori(0, KD // 2) as i:
                    for s in range(2):
                        for b in range(2):
                            dve.wait_ge(gate_done, i * 4 + 2 * s + b + 2)
                            dve.wait_ge(valued, i * 4 + 2 * s + b + 1)
                            g = gate[:, b, :].rearrange("p (h t) -> p h t", h=2)
                            nc.vector.tensor_tensor(g, g, k.ps[:, 4 + 2 * b:6 + 2 * b, 0:H2], ALU.mult).then_inc(term, 1)
                        dve.wait_ge(term, i * 4 + 2 * s + 3)
                        nc.vector.tensor_tensor(k.work[:, 0, :], gate[:, 0, :], gate[:, 1, :], ALU.add).then_inc(merged, 1)
                        dve.wait_ge(merged, i * 2 + s + 2)
                        m = bass.ds(i * 2 + s, 1)
                        nc.vector.tensor_copy(a.mergedH[:, m, :], k.work[:, 0:1, :]).then_inc(m_high, 1)
                        dve.wait_ge(m_high, i * 2 + s + 1)
                        nc.vector.tensor_tensor(a.mergedL[:, m, :], k.work[:, 0:1, :],
                                                a.mergedH[:, m, :].bitcast(F32), ALU.subtract).then_inc(m_low, 1)
                        dve.wait_ge(m_low, i * 2 + s + 1)


def output_projection(nc, k, d, a):
    with ExitStack() as ctx:
        w = Stream(nc, ctx, "op", d["w_out"], KD, KD)
        product, bank_free = named_semaphores(nc, ctx, "op", "product bank_free")
        with nc.Block("output_projection") as block:
            @block.sync
            def _(sp):
                w.sync(sp)

            @block.gpsimd
            def _(pool):
                w.rest(pool)

            @block.tensor
            def _(pe):
                pe.sem_inc(bank_free, 4)
                with pe.Fori(0, KD // 2) as i:
                    for s in range(2):
                        w.await_block(pe, i, s)
                        for h in range(2):
                            pe.wait_ge(bank_free, i * 4 + 2 * s + h + 1)
                            accumulate(nc, k.ps[:, 2 * s + h, 0:H2],
                                       [x for c in range(KD)
                                        for x in split_products(w.parts(s, c), both((a.mergedH, a.mergedL), c, halves(h)))]
                                       ).then_inc(product, 1)

            @block.scalar
            def _(act):
                for s in range(2):
                    w.round(act, 0, s)
                with act.Fori(0, KD // 2 - 1) as i:
                    for s in range(2):
                        act.wait_ge(product, i * 4 + 2 * s + 2)
                        w.round(act, i + 1, s)

            @block.vector
            def _(dve):
                with dve.Fori(0, KD // 2) as i:
                    for s in range(2):
                        for h in range(2):
                            u = 2 * s + h
                            dve.wait_ge(product, i * 4 + u + 1)
                            x = k.xT[:, bass.ds(i * 2 + s, 1), halves(h)]
                            nc.vector.tensor_tensor(x, x, k.ps[:, u:u + 1, 0:H2], ALU.add).then_inc(bank_free, 1)


def retrieve(nc, k, d, f):
    with ExitStack() as ctx:
        w = Stream(nc, ctx, "re", d["w_query"], KD, 2 * HEADS)
        keys = ctx.enter_context(nc.sbuf_tensor("r_keys", [P, 2, 2, P], F32))
        qT = ctx.enter_context(nc.sbuf_tensor("r_q", [P, 2, T], F32))
        score = ctx.enter_context(nc.sbuf_tensor("r_score", [P, 2, TT, NK], F32))
        rest = ctx.enter_context(nc.sbuf_tensor("r_rest", [P, TT, NK], F32))
        top = ctx.enter_context(nc.sbuf_tensor("r_top", [P, 2, TT, TOPK], F32))
        at = ctx.enter_context(nc.sbuf_tensor("r_at", [P, 2, TT, TOPK], U32))
        atf = ctx.enter_context(nc.sbuf_tensor("r_atf", [P, 2, TT, TOPK], F32))
        cand = ctx.enter_context(nc.sbuf_tensor("r_cand", [P, TT, TOPK * TOPK], F32))
        left = ctx.enter_context(nc.sbuf_tensor("r_left", [P, TT, TOPK * TOPK], F32))
        best = ctx.enter_context(nc.sbuf_tensor("r_best", [P, TT, TOPK], F32))
        where = ctx.enter_context(nc.sbuf_tensor("r_where", [P, TT, TOPK], U32))
        part = ctx.enter_context(nc.sbuf_tensor("r_part", [P, 2, TT, TOPK], U32))
        partf = ctx.enter_context(nc.sbuf_tensor("r_partf", [P, 2, TT, TOPK], F32))
        hit = ctx.enter_context(nc.sbuf_tensor("r_hit", [P, 2, TT, TOPK, TOPK], F32))
        tot = ctx.enter_context(nc.sbuf_tensor("r_tot", [P, TT], F32))
        res = ctx.enter_context(nc.sbuf_tensor("r_res", [P, 3, TT, HEADS * TOPK], F32))
        (keys_in0, keys_in1, queried, q_in_sbuf, scored, score_in, score_free, step, hit_ready, looked_up, exp_ready, exped,
         reset, turned, turn_free) = named_semaphores(
            nc, ctx, "re", "keys_in0 keys_in1 queried q_in_sbuf scored score_in score_free step hit_ready looked_up "
            "exp_ready exped reset turned turn_free")
        keys_in = (keys_in0, keys_in1)
        scratch = ctx.enter_context(nc.sbuf_tensor("r_scratch", [P, 64], F32))
        iota16 = k.const[:, C_IOTA:C_IOTA + TOPK]

        def load_keys(sp, j, i):
            sp.dma_start(keys[:, j], d["keys"][bass.ds(i, 1)].rearrange("o p s m -> p (o s) m")).then_inc(keys_in[j], 16)

        with nc.Block("retrieve") as block:
            @block.sync
            def _(sp):
                load_keys(sp, 0, 0)
                for s in range(2):
                    w.load(sp, s, s)
                load_keys(sp, 1, 1)
                for s in range(2):
                    sp.wait_ge(w.low_done, s + 1)
                    w.load(sp, s, s + 2)
                with sp.Fori(1, HEADS // 2) as i:
                    for j in range(2):
                        sp.wait_ge(scored, i * 4 + (2 * j - 1))
                        load_keys(sp, j, i * 2 + j)
                        m = i * 2 + j
                        for s in range(2):
                            sp.wait_ge(w.low_done, m * 2 + (s - 1))
                            w.load(sp, s, m * 2 + s)

            @block.gpsimd
            def _(pool):
                def low(i):
                    for s in range(2):
                        pool.wait_ge(w.high_done, i * 2 + s + 1)
                        nc.gpsimd.tensor_tensor(w.low[:, s, :], w.raw[:, s, :], w.high[:, s, :].bitcast(F32),
                                                ALU.subtract).then_inc(w.low_done, 1)

                def look_up(i):
                    for s in range(2):
                        pool.wait_ge(hit_ready, i * 2 + s + 1)
                        nc.gpsimd.tensor_tensor(hit[:, s], hit[:, s],
                                                atf[:, s].unsqueeze(2).to_broadcast([P, TT, TOPK, TOPK]),
                                                ALU.mult).then_inc(looked_up, 1)

                low(0)
                with pool.Fori(0, HEADS - 1) as i:
                    low(i + 1)
                    look_up(i)
                look_up(HEADS - 1)

            @block.tensor
            def _(pe):
                pe.sem_inc(scored, 1)
                def head(i, j):
                    m = i * 2 + j
                    for s in range(2):
                        pe.wait_ge(w.low_done, m * 2 + s + 1)
                        pe.wait_ge(q_in_sbuf, m * 2 + 1)
                        for h in range(2):
                            last = accumulate(nc, k.ps[:, 2 * s + h, 0:H2],
                                              [x for c in range(KD)
                                               for x in split_products(w.parts(s, c), both(k.h, c, halves(h)))])
                        last.then_inc(queried, 1)
                    pe.wait_ge(keys_in[j], i * 16 + 16)
                    for s in range(2):
                        pe.wait_ge(q_in_sbuf, m * 2 + s + 2)
                        pe.wait_ge(score_in, m * 2 + 1)
                        for t in range(TT):
                            r = rows_of(t)
                            out = k.ps[0:r, 4 + 2 * s, t * P:(t + 1) * P] if t < QT else k.ps[0:r, 5 + 2 * s, 0:P]
                            last = nc.tensor.matmul(out, qT[:, s, t * P:t * P + r], keys[:, j, s, :],
                                                    start=True, stop=True)
                        last.then_inc(scored, 1)

                with pe.Fori(0, HEADS // 2) as i:
                    for j in range(2):
                        head(i, j)
                pe.wait_ge(step, HEADS * STEPS)
                for j in range(3 * TT):
                    a, t = j // TT, j % TT
                    r = rows_of(t)
                    if j >= 4:
                        pe.wait_ge(turn_free, j - 3)
                    nc.tensor.transpose(k.ps[:, j % 4, 0:r], res[0:r, a, t, :],
                                        k.const[0:r, C_IDENT:C_IDENT + r]).then_inc(turned, 1)

            @block.scalar
            def _(act):
                def copies(i, more=True):
                    for s in range(2):
                        act.wait_ge(queried, i * 2 + s + 1)
                        act.wait_ge(scored, i * 2 + 1)
                        nc.scalar.activation(qT[:, s, :].rearrange("p (h t) -> p h t", h=2),
                                             k.ps[:, 2 * s:2 * s + 2, 0:H2], ACT.Copy).then_inc(q_in_sbuf, 1)
                        if more:
                            w.round(act, i + 1, s)
                    for s in range(2):
                        act.wait_ge(scored, i * 2 + s + 2)
                        act.wait_ge(score_free, i * 2 + s + 1)
                        nc.scalar.activation(score[:, s, 0:QT, :], k.ps[:, 4 + 2 * s, :].rearrange("p (t c) -> p t c", t=QT),
                                             ACT.Copy)
                        nc.scalar.activation(score[0:SAMP, s, QT, :], k.ps[0:SAMP, 5 + 2 * s, 0:P],
                                             ACT.Copy).then_inc(score_in, 1)

                def exponentials(i):
                    act.wait_ge(exp_ready, i + 1)
                    nc.scalar.activation(best[:, :, :], best[:, :, :], ACT.Exp).then_inc(exped, 1)

                act.sem_inc(q_in_sbuf, 1)
                act.sem_inc(score_in, 1)
                for s in range(2):
                    w.round(act, 0, s)
                copies(0)
                with act.Fori(0, HEADS - 2) as i:
                    copies(i + 1)
                    exponentials(i)
                copies(HEADS - 1, more=False)
                exponentials(HEADS - 2)
                exponentials(HEADS - 1)
                for j in range(3 * TT):
                    a, t = j // TT, j % TT
                    act.wait_ge(turned, j + 1)
                    nc.scalar.activation(f.pick[:, a, t * P:t * P + rows_of(t)], k.ps[:, j % 4, 0:rows_of(t)],
                                         ACT.Copy).then_inc(turn_free, 1)

            @block.vector
            def _(dve):
                nc.vector.memset(score[:, :, QT, :], 0.0).then_inc(reset, 1)
                dve.wait_ge(reset, 1)
                dve.sem_inc(score_free, 2)
                with dve.Fori(0, HEADS) as i:
                    n, waits = [0], [0]

                    def done(ins):
                        n[0] += 1
                        ins.then_inc(step, 1)

                    def after():
                        vector_wait(step, i * STEPS + n[0])

                    def vector_wait(sem, value):
                        dve.wait_ge(sem, value)
                        nc.vector.memset(scratch[:, waits[0]:waits[0] + 1], 0.0)
                        waits[0] += 1

                    def sixteen(value, spare, tops, index):
                        for t in range(TT):
                            done(nc.vector.max(tops[:, t, 0:8], value[:, t, :]))
                        after()
                        for t in range(TT):
                            nc.vector.max_index(index[:, t, 0:8], tops[:, t, 0:8], value[:, t, :])
                            done(nc.vector.match_replace(spare[:, t, :], tops[:, t, 0:8], value[:, t, :], REMOVED))
                        after()
                        for t in range(TT):
                            done(nc.vector.max(tops[:, t, 8:16], spare[:, t, :]))
                        after()
                        for t in range(TT):
                            last = nc.vector.max_index(index[:, t, 8:16], tops[:, t, 8:16], spare[:, t, :])
                            done(last)

                    for s in range(2):
                        vector_wait(score_in, i * 2 + s + 2)
                        sixteen(score[:, s], rest, top[:, s], at[:, s])
                        after()
                        nc.vector.tensor_copy(atf[:, s], at[:, s]).then_inc(score_free, 1)
                    done(nc.vector.tensor_tensor(
                        cand[:, :, :].rearrange("p t (a b) -> p t a b", a=TOPK),
                        top[:, 0].unsqueeze(3).to_broadcast([P, TT, TOPK, TOPK]),
                        top[:, 1].unsqueeze(2).to_broadcast([P, TT, TOPK, TOPK]), ALU.add))
                    after()
                    sixteen(cand, left, best, where)
                    after()
                    done(nc.vector.tensor_scalar(part[:, 0], where[:, :, :], 4, None, ALU.logical_shift_right))
                    done(nc.vector.tensor_scalar(part[:, 1], where[:, :, :], TOPK - 1, None, ALU.bitwise_and))
                    after()
                    done(nc.vector.tensor_copy(partf[:, :, :, :], part[:, :, :, :]))
                    after()
                    for s in range(2):
                        nc.vector.tensor_tensor(
                            hit[:, s], partf[:, s].unsqueeze(3).to_broadcast([P, TT, TOPK, TOPK]),
                            iota16.unsqueeze(1).unsqueeze(1).to_broadcast([P, TT, TOPK, TOPK]),
                            ALU.is_equal).then_inc(hit_ready, 1)
                    done(nc.vector.tensor_copy(tot[:, :], best[:, :, 0]))
                    after()
                    nc.vector.tensor_tensor(best[:, :, :], best[:, :, :],
                                            tot[:, :].unsqueeze(2).to_broadcast([P, TT, TOPK]),
                                            ALU.subtract).then_inc(exp_ready, 1)
                    for s in range(2):
                        dve.wait_ge(looked_up, i * 2 + s + 1)
                        done(nc.vector.tensor_reduce(res[:, s, :, bass.ds(i * TOPK, TOPK)], hit[:, s], AXX, ALU.add))
                    dve.wait_ge(exped, i + 1)
                    done(nc.vector.tensor_reduce(tot[:, :], best[:, :, :], AXX, ALU.add))
                    after()
                    done(nc.vector.reciprocal(tot[:, :], tot[:, :]))
                    after()
                    done(nc.vector.tensor_tensor(res[:, 2, :, bass.ds(i * TOPK, TOPK)], best[:, :, :],
                                                 tot[:, :].unsqueeze(2).to_broadcast([P, TT, TOPK]), ALU.mult))
                    after()
                    assert n[0] == STEPS, n[0]


STEPS = 3 * 4 * TT + 1 + 3 + 2 + 4


def gate_matrix(nc, k, f, d):
    GROUPS = P // GT
    with ExitStack() as ctx:
        hotJ = ctx.enter_context(nc.sbuf_tensor("hotJ", [P, 4, GT, NK], F32))
        hotI = ctx.enter_context(nc.sbuf_tensor("hotI", [P, 4, GT, NK], F32))
        stage = [ctx.enter_context(nc.sbuf_tensor(f"stage{j}", [P, NK, P], F32)) for j in range(2)]
        second, first, gated, used, copied, *stored = named_semaphores(
            nc, ctx, "gx", "second first gated used copied stored0 stored1")

        def chunks():
            return [(t, t * GROUPS, rows_of(t) // GT) for t in range(TT)]

        with nc.Block("gate_matrix") as block:
            @block.vector
            def _(dve):
                iota = k.const[:, C_IOTA:C_IOTA + NK].unsqueeze(1).to_broadcast([P, GT, NK])
                with dve.Fori(0, T // GT // 4) as i:
                    for s in range(4):
                        tokens = bass.ds(i * (4 * GT) + s * GT, GT)
                        dve.wait_ge(used, i * 4 + s + 1)
                        nc.vector.tensor_tensor(hotI[:, s], f.pick[:, 0, tokens].unsqueeze(2).to_broadcast([P, GT, NK]),
                                                iota, ALU.is_equal).then_inc(first, 1)
                        nc.vector.tensor_tensor(hotJ[:, s], f.pick[:, 1, tokens].unsqueeze(2).to_broadcast([P, GT, NK]),
                                                iota, ALU.is_equal).then_inc(second, 1)

            @block.gpsimd
            def _(pool):
                with pool.Fori(0, T // GT // 4) as i:
                    for s in range(4):
                        tokens = bass.ds(i * (4 * GT) + s * GT, GT)
                        pool.wait_ge(first, i * 4 + s + 1)
                        nc.gpsimd.tensor_tensor(hotI[:, s], hotI[:, s],
                                                f.pick[:, 2, tokens].unsqueeze(2).to_broadcast([P, GT, NK]),
                                                ALU.mult).then_inc(gated, 1)

            @block.tensor
            def _(pe):
                pe.sem_inc(used, 4)
                with pe.Fori(0, T // GT // 4) as i:
                    for s in range(4):
                        pe.wait_ge(second, i * 4 + s + 1)
                        pe.wait_ge(gated, i * 4 + s + 1)
                        pe.wait_ge(copied, i * 4 + s + 1)
                        for j in range(GT):
                            last = nc.tensor.matmul(k.ps[:, s, j * NK:(j + 1) * NK], hotJ[:, s, j, :], hotI[:, s, j, :],
                                                    start=True, stop=True)
                        last.then_inc(used, 1)

            @block.scalar
            def _(act):
                act.sem_inc(copied, 4)
                for t, g0, groups in chunks():
                    if t >= 2:
                        act.wait_ge(stored[t % 2], 16 * (t // 2))
                    with act.Fori(0, groups // 4) as i:
                        for s in range(4):
                            act.wait_ge(used, i * 4 + (g0 + s + 5))
                            nc.scalar.activation(stage[t % 2][:, :, bass.ds(i * (4 * GT) + s * GT, GT)],
                                                 k.ps[:, s, :].rearrange("p (t i) -> p i t", t=GT),
                                                 ACT.Copy).then_inc(copied, 1)

            @block.sync
            def _(sp):
                for t, g0, groups in chunks():
                    sp.wait_ge(copied, 4 + g0 + groups)
                    sp.dma_start(d["gates"][:, :, t * P:t * P + rows_of(t)].rearrange("i j t -> j i t"),
                                 stage[t % 2][:, :, 0:rows_of(t)]).then_inc(stored[t % 2], 16)
                for j in range(2):
                    sp.wait_ge(stored[j], 16 * len(range(j, TT, 2)))


def expert_pass(nc, k, d, f):
    n = NK // GB
    HU, YU = 2 * GB, 2 * KD
    with ExitStack() as ctx:
        u = ctx.enter_context(nc.sbuf_tensor("ex_u", [P, GB, D], F32))
        v = ctx.enter_context(nc.sbuf_tensor("ex_v", [P, GB, D], F32))
        gate = ctx.enter_context(nc.sbuf_tensor("ex_gate", [P, GB, T], F32))
        hid = ctx.enter_context(nc.sbuf_tensor("ex_hidden", [P, GB, T], F32))
        uH, uL, vH, vL = (ctx.enter_context(nc.sbuf_tensor(f"ex_{x}", [P, GB, D], F32R)) for x in ("uH", "uL", "vH", "vL"))
        wH, wL = (ctx.enter_context(nc.sbuf_tensor(f"ex_{x}", [P, 2, GB, T], F32R)) for x in ("wH", "wL"))
        (u0, u1, v0, v1, g0, g1, u_high, u_low, v_high, v_low, hidden, activated, gated, rounded, weighted,
         hidden_free, mixed, added) = named_semaphores(
            nc, ctx, "ex", "u0 u1 v0 v1 g0 g1 u_high u_low v_high v_low hidden activated gated rounded weighted "
            "hidden_free mixed added")
        u_in, v_in, g_in = (u0, u1), (v0, v1), (g0, g1)

        with nc.Block("expert_pass") as block:
            @block.sync
            def _(sp):
                def load(x, name, sem, b, s):
                    sp.dma_start(x[:, s, :], d[name][bass.ds(b * GB + s, 1)].rearrange("o p m -> p (o m)")
                                 ).then_inc(sem[s], 16)

                for x, name, sem in ((u, "u", u_in), (v, "v", v_in)):
                    for s in range(GB):
                        load(x, name, sem, 0, s)
                for s in range(GB):
                    load(gate, "gates", g_in, 0, s)
                with sp.Fori(0, n - 1) as b:
                    for s in range(GB):
                        sp.wait_ge(u_low, b * GB + s + 1)
                        load(u, "u", u_in, b + 1, s)
                    for s in range(GB):
                        sp.wait_ge(gated, b * GB + s + 1)
                        load(gate, "gates", g_in, b + 1, s)
                    for s in range(GB):
                        sp.wait_ge(v_low, b * GB + s + 1)
                        load(v, "v", v_in, b + 1, s)

            @block.scalar
            def _(act):
                def split_u(b, s):
                    act.wait_ge(u_in[s], b * 16 + 16)
                    nc.scalar.activation(uH[:, s, :], u[:, s, :], ACT.Copy).then_inc(u_high, 1)

                def split_v(b, s):
                    act.wait_ge(v_in[s], b * 16 + 16)
                    nc.scalar.activation(vH[:, s, :], v[:, s, :], ACT.Copy).then_inc(v_high, 1)

                def step(b, first=False, final=False):
                    for s in range(GB):
                        act.wait_ge(hidden_free, b * GB + s + 1)
                        for h in range(2):
                            act.wait_ge(hidden, b * HU + 2 * s + h + 1)
                            nc.scalar.activation(hid[:, s, halves(h)], k.ps[:, 2 * s + h, 0:H2],
                                                 ACT.Gelu).then_inc(activated, 1)
                        if not final:
                            split_u(b + 1, s)
                    if not first:
                        act.wait_ge(mixed, b * YU)
                        for s in range(GB):
                            split_v(b, s)

                for s in range(GB):
                    split_u(0, s)
                for s in range(GB):
                    split_v(0, s)
                act.sem_inc(hidden_free, GB)
                step(0, first=True)
                with act.Fori(1, n - 1) as b:
                    step(b)
                step(n - 1, final=True)

            @block.gpsimd
            def _(pool):
                def low(x, xH, xL, high, sem, b, s):
                    pool.wait_ge(high, b * GB + s + 1)
                    nc.gpsimd.tensor_tensor(xL[:, s, :], x[:, s, :], xH[:, s, :].bitcast(F32),
                                            ALU.subtract).then_inc(sem, 1)

                def low_u(b):
                    for s in range(GB):
                        low(u, uH, uL, u_high, u_low, b, s)

                def low_v(b):
                    for s in range(GB):
                        low(v, vH, vL, v_high, v_low, b, s)

                low_u(0)
                low_v(0)
                low_u(1)
                with pool.Fori(1, n - 1) as b:
                    low_u(b + 1)
                    low_v(b)
                low_v(n - 1)

            @block.tensor
            def _(pe):
                def hide(b, first=False):
                    for s in range(GB):
                        pe.wait_ge(u_low, b * GB + s + 1)
                        for h in range(2):
                            if not first:
                                pe.wait_ge(activated, b * HU + (2 * s + h + 1 - HU))
                            pairs = []
                            for c in range(KD):
                                rows = slice(c * P, (c + 1) * P)
                                pairs += [(uH[:, s, rows], k.h[0][:, c, halves(h)]), (uH[:, s, rows], k.h[1][:, c, halves(h)]),
                                          (uL[:, s, rows], k.h[0][:, c, halves(h)])]
                            accumulate(nc, k.ps[:, 2 * s + h, 0:H2], pairs).then_inc(hidden, 1)

                def mix(b, parity):
                    pe.wait_ge(weighted, b * GB + GB)
                    pe.wait_ge(v_low, b * GB + GB)
                    for c in range(KD):
                        rows = slice(c * P, (c + 1) * P)
                        for h in range(2):
                            y = 2 * c + h
                            pe.wait_ge(added, b * YU + y + 1)
                            pairs = []
                            for s in range(GB):
                                high, low = wH[:, parity, s, halves(h)], wL[:, parity, s, halves(h)]
                                pairs += [(vH[:, s, rows], high), (vH[:, s, rows], low), (vL[:, s, rows], high)]
                            accumulate(nc, k.ps[:, 4 + y % 4, 0:H2], pairs).then_inc(mixed, 1)

                pe.sem_inc(added, 4)
                hide(0, first=True)
                with pe.Fori(0, n - 2, 2) as b:
                    for j in range(2):
                        hide(b + (j + 1))
                        mix(b + j, j)
                hide(n - 1)
                mix(n - 2, 0)
                mix(n - 1, 1)

            @block.vector
            def _(dve):
                def weigh(b, parity, s):
                    dve.wait_ge(activated, b * HU + 2 * s + 2)
                    dve.wait_ge(g_in[s], b * 16 + 16)
                    nc.vector.tensor_tensor(hid[:, s, :], hid[:, s, :], gate[:, s, :], ALU.mult).then_inc(gated, 1)
                    dve.wait_ge(gated, b * GB + s + 1)
                    nc.vector.tensor_copy(wH[:, parity, s, :], hid[:, s, :]).then_inc(rounded, 1)
                    dve.wait_ge(rounded, b * GB + s + 1)
                    nc.vector.tensor_tensor(wL[:, parity, s, :], hid[:, s, :], wH[:, parity, s, :].bitcast(F32),
                                            ALU.subtract).then_inc(weighted, 1)
                    dve.wait_ge(weighted, b * GB + s + 1)
                    dve.sem_inc(hidden_free, 1)

                def add(b, units):
                    for y in units:
                        dve.wait_ge(mixed, b * YU + y + 1)
                        x = k.xT[:, y // 2, halves(y % 2)]
                        nc.vector.tensor_tensor(x, x, k.ps[:, 4 + y % 4, 0:H2], ALU.add).then_inc(added, 1)

                def turn(b, parity):
                    weigh(b + 1, 1 - parity, 0)
                    add(b, range(2))
                    weigh(b + 1, 1 - parity, 1)
                    add(b, range(2, YU))

                for s in range(GB):
                    weigh(0, 0, s)
                with dve.Fori(0, n - 2, 2) as b:
                    for j in range(2):
                        turn(b + j, j)
                turn(n - 2, 0)
                add(n - 1, range(YU))


def layer_embedding(nc, k, d):
    KP = 256 // P
    with ExitStack() as ctx:
        w = Stream(nc, ctx, "le", d["w_ple"], KD + KP, KD)
        pT = ctx.enter_context(nc.sbuf_tensor("le_p", [P, KP, T], F32))
        split = [ctx.enter_context(nc.sbuf_tensor(f"le_p{n}", [P, KP, T], F32R)) for n in ("high", "low")]
        gate = ctx.enter_context(nc.sbuf_tensor("le_gate", [P, 2, T], F32))
        p_in, p_high, p_low, gated, valued, gate_done, term, added = named_semaphores(
            nc, ctx, "le", "p_in p_high p_low gated valued gate_done term added")

        with nc.Block("layer_embedding") as block:
            @block.sync
            def _(sp):
                sp.dma_start(pT[:, :, :], d["pT"]).then_inc(p_in, 16)
                w.sync(sp)

            @block.gpsimd
            def _(pool):
                w.rest(pool)

            @block.tensor
            def _(pe):
                with pe.Fori(0, KD // 2) as i:
                    for s in range(2):
                        w.await_block(pe, i, s)
                        pe.wait_ge(gate_done, i * 2 + 1)
                        for h in range(2):
                            last = accumulate(nc, k.ps[:, 4 * s + h, 0:H2],
                                              [x for c in range(KD)
                                               for x in split_products(w.parts(s, c), both(k.h, c, halves(h)))])
                        last.then_inc(gated, 1)
                        pe.wait_ge(p_low, 1)
                        pe.wait_ge(term, i * 2 + 1)
                        for h in range(2):
                            last = accumulate(nc, k.ps[:, 4 * s + 2 + h, 0:H2],
                                              [x for c in range(KP)
                                               for x in split_products(w.parts(s, KD + c), both(split, c, halves(h)))])
                        last.then_inc(valued, 1)

            @block.scalar
            def _(act):
                def pair(i, more):
                    for s in range(2):
                        act.wait_ge(added, i * 2 + 1)
                        act.wait_ge(gated, i * 2 + s + 1)
                        nc.scalar.activation(gate[:, s, :].rearrange("p (h t) -> p h t", h=2),
                                             k.ps[:, 4 * s:4 * s + 2, 0:H2], ACT.Sigmoid).then_inc(gate_done, 1)
                        if more:
                            act.wait_ge(valued, i * 2 + s + 1)
                            w.round(act, i + 1, s)

                act.sem_inc(gate_done, 1)
                for s in range(2):
                    w.round(act, 0, s)
                act.wait_ge(p_in, 16)
                nc.scalar.activation(split[0][:, :, :], pT[:, :, :], ACT.Copy).then_inc(p_high, 1)
                with act.Fori(0, KD // 2 - 1) as i:
                    pair(i, True)
                pair(KD // 2 - 1, False)

            @block.vector
            def _(dve):
                dve.sem_inc(term, 1)
                dve.sem_inc(added, 1)
                dve.wait_ge(p_high, 1)
                nc.vector.tensor_tensor(split[1][:, :, :], pT[:, :, :], split[0][:, :, :].bitcast(F32),
                                        ALU.subtract).then_inc(p_low, 1)
                with dve.Fori(0, KD // 2) as i:
                    for s in range(2):
                        dve.wait_ge(gate_done, i * 2 + s + 2)
                        dve.wait_ge(valued, i * 2 + s + 1)
                        g = gate[:, s, :].rearrange("p (h t) -> p h t", h=2)
                        nc.vector.tensor_tensor(g, g, k.ps[:, 4 * s + 2:4 * s + 4, 0:H2], ALU.mult).then_inc(term, 1)
                        dve.wait_ge(term, i * 2 + s + 2)
                        x = k.xT[:, bass.ds(i * 2 + s, 1), :]
                        nc.vector.tensor_tensor(x, x, gate[:, s:s + 1, :], ALU.add).then_inc(added, 1)


def stream_step(nc, d):
    with ExitStack() as ctx:
        k = Core()

        def sb(name, shape, dtype=F32, c=ctx):
            return c.enter_context(nc.sbuf_tensor(name, shape, dtype))

        k.ps = ctx.enter_context(nc.psum_tensor("banks", [P, 8, 512], F32))
        k.xT = sb("xT", [P, KD, T])
        k.const = sb("const", [P, C_END])
        k.gain = sb("gain", [P, G_END])
        k.rstd = sb("rstd", [P, T])
        norm_sems = named_semaphores(nc, ctx, "norm", "squared summed rooted inverted normed high low stored")
        norms = {"uses": 0, "chunks": 0, "split": 0, "stores": 0}

        def norm(name, src, dst, chunks, gain, split=None, store=None):
            with nc.sbuf_tensor(f"{name}_square", [P, 2, T], F32) as k.square:
                rms_norm(nc, k, name, norm_sems, norms["uses"], norms["chunks"], src, dst, chunks, gain,
                         split and (*split, norms["split"]), store, norms["stores"])
            norms["uses"] += 1
            norms["chunks"] += chunks
            norms["split"] += chunks if split else 0
            norms["stores"] += len(store or [])

        def norm_h(name, gain):
            with nc.sbuf_tensor(f"{name}_whole", [P, 4, T], F32) as whole:
                norm(name, lambda c: k.xT[:, c, :], lambda c: whole[:, c % 4, :], KD, gain, k.h)

        load_inputs(nc, k, d)
        with ExitStack() as inner:
            k.h = [sb(f"h{n}", [P, KD, T], F32R, c=inner) for n in ("high", "low")]
            norm_h("norm_mix", G_MIX)
            with ExitStack() as mixer:
                a = Core()
                a.oA = sb("oA", [P, PAIRS, T], c=mixer)
                a.oB = sb("oB", [P, PAIRS, T], c=mixer)
                with ExitStack() as mla:
                    a.proj = sb("proj", [P, NQ + NC + 1, T], c=mla)
                    a.rope = sb("rope", [P, T], c=mla)
                    a.kdup = sb("kdup", [P, T], c=mla)
                    a.kdupS = sb("kdupS", [P, MLAK], c=mla)
                    a.keyS = sb("keyS", [P, NC, MLAK], c=mla)
                    a.valueS = sb("valueS", [P, PAST // P + 1, KVL], c=mla)
                    a.loaded, a.lift_in = named_semaphores(nc, mla, "mla", "loaded lift_in")
                    latent_projection(nc, k, d, a)
                    norm("norm_q", lambda c: a.proj[:, c, :], lambda c: a.proj[:, c, :], NQ, G_Q)
                    norm("norm_kv", lambda c: a.proj[:, NQ + c, :], lambda c: a.proj[:, NQ + c, :], NC, G_KV,
                         store=[(d["o_latent"], a.proj[:, NQ:NQ + NC, :])])
                    with nc.sbuf_tensor("turn", [P, T], F32) as a.turn:
                        rotary_key(nc, k, d, a)
                    a.wuv = sb("w_uv", [P, NC, HEADS * NOPE], c=mla)
                    a.wukT = sb("w_ukT", [P, PAIRS, KVL], c=mla)
                    a.qS = sb("qS", [P, HEADS, SAMP], c=mla)
                    latent_attention(nc, k, d, a)
                    latent_sample(nc, k, d, a)
                band_attention(nc, k, d, a)
                a.mergedH, a.mergedL = (sb(f"merged{n}", [P, KD, T], F32R, c=mixer) for n in ("high", "low"))
                with nc.sbuf_tensor("work", [P, 1, T], F32) as k.work:
                    gated_merge(nc, k, d, a)
                output_projection(nc, k, d, a)
            norm_h("norm_ffn", G_FFN)
            with ExitStack() as ffn:
                f = Core()
                f.pick = sb("pick", [P, 3, T], c=ffn)
                retrieve(nc, k, d, f)
                gate_matrix(nc, k, f, d)
                expert_pass(nc, k, d, f)
            norm_h("norm_ple", G_PLE)
            layer_embedding(nc, k, d)
        with nc.sbuf_tensor("y", [P, KD, T], F32) as y:
            norm("norm_final", lambda c: k.xT[:, c, :], lambda c: y[:, c, :], KD, G_FIN, store=[(d["o_y"], y[:, :, :])])


def kernel(**inputs):
    import concourse.bacc as bacc
    from concourse.bass_utils import run_bass_kernel_spmd

    x = {n: np.asarray(v) for n, v in inputs.items()}

    def blocks(w):
        kk, m = w.shape
        return np.ascontiguousarray(w.reshape(kk // P, P, m // P, P).transpose(2, 1, 0, 3))

    def feature_major(v):
        return np.ascontiguousarray(v.T.reshape(v.shape[1] // P, P, v.shape[0]).transpose(1, 0, 2))

    def columns(v):
        return v.reshape(-1, P).T

    def swapped(w):
        return np.concatenate([w[..., ROPE // 2:], w[..., :ROPE // 2]], -1)

    w_in = x["w_in"][0]
    o = np.cumsum([0, QL, KVL, ROPE, 512, 512, 512, D, D])
    kr = w_in[:, o[2]:o[3]]
    arrays = {}
    arrays["xT"] = feature_major(np.concatenate([x["x_prompt"][0], x["x_sample"][0]]))
    arrays["pT"] = feature_major(np.concatenate([x["p_prompt"][0, 0], x["p_sample"][0, 0]]))
    arrays["w_small"] = blocks(np.concatenate([w_in[:, :o[2]], kr, swapped(kr), np.zeros((D, 64), np.float32)], 1))
    for n, j in (("w_bq", 3), ("w_bk", 4), ("w_bv", 5)):
        arrays[n] = blocks(w_in[:, o[j]:o[j + 1]])
    values = np.concatenate([blocks(x["w_a_proj"][0]), blocks(x["w_b_proj"][0])], 2)
    arrays["w_merge"] = np.stack([blocks(w_in[:, o[6]:o[7]]), blocks(w_in[:, o[7]:o[8]]), values],
                                 1).reshape(3 * KD, P, KD, P)
    arrays["w_out"] = blocks(x["w_out"][0])
    arrays["w_query"] = blocks(x["w_query"][0])
    arrays["keys"] = x["sub_keys"][0].transpose(0, 3, 1, 2)
    arrays["w_ple"] = np.concatenate([blocks(x["w_ple_gate"][0]), blocks(x["w_ple_proj"][0])], 2)
    uq = x["w_uq"][0].reshape(QL, PAIRS, 2, NOPE + ROPE)
    nope, rot = uq[..., :NOPE], uq[..., NOPE:]
    rot = np.concatenate([rot, swapped(rot)], -1)
    uq = np.stack([np.concatenate([nope[:, :, 0], rot[:, :, 0]], -1),
                   np.concatenate([rot[:, :, 1], nope[:, :, 1]], -1)], 2)
    arrays["w_uq"] = uq.reshape(NQ, P, PAIRS, 2, P).transpose(2, 1, 3, 0, 4).reshape(PAIRS, P, -1)
    uk = x["w_uk"][0]
    arrays["w_uk"] = uk.reshape(NC, P, PAIRS, P).transpose(2, 1, 0, 3).reshape(PAIRS, P, -1)
    arrays["w_ukT"] = uk.reshape(KVL, PAIRS, P).transpose(2, 1, 0)
    arrays["w_uv"] = x["w_uv"][0].reshape(NC, P, HEADS * NOPE).transpose(1, 0, 2)
    lat = x["cache_latent"][0, 0]
    arrays["cache_latT"] = feature_major(lat)
    arrays["cache_lat"] = lat.reshape(PAST // P, P, KVL).transpose(1, 0, 2)
    arrays["cache_krT"] = np.concatenate([x["cache_krope"][0, 0].T] * 4)
    bk = x["cache_band_k"][0, 0].reshape(WIN, PAIRS, P)
    bv = x["cache_band_v"][0, 0].reshape(WIN, PAIRS, P)
    arrays["cache_bkT"] = bk.transpose(1, 2, 0)
    arrays["cache_bv"] = bv.reshape(QT, P, PAIRS, P).transpose(2, 1, 0, 3)
    arrays["cache_bv_kept"] = bv[SAMP:].reshape(WIN - SAMP, PAIRS * P)
    rel = x["rel_bias"][0]
    clip = (rel.shape[1] - 1) // 2
    dist = np.arange(P)[:, None] - (np.arange(WIN + P) - WIN)[None]
    bias = rel[:, np.clip(dist, -clip, clip) + clip]
    bias[:, :64, WIN + 64:] = NEG
    arrays["bias"] = bias.reshape(PAIRS, 2, P, WIN + P).transpose(0, 2, 1, 3)
    dist = (WIN + np.arange(SAMP))[:, None] - np.arange(BANDK)[None]
    arrays["biasS"] = rel[:, np.clip(dist, -clip, clip) + clip].reshape(PAIRS, 2 * SAMP, BANDK)
    arrays["u"] = x["expert_u"][0].reshape(NK, NK, KD, P).transpose(0, 3, 2, 1).reshape(NK, P, D)
    arrays["v"] = x["expert_v"][0].reshape(NK, NK, D)
    arrays["gains"] = np.concatenate([columns(x[n].reshape(-1)) for n in
                                      ("g_mix", "g_ffn", "g_ple", "g_final", "g_q_lora", "g_kv_lora")], 1)
    half = ROPE // 2
    freqs = (np.float32(10000.0) ** (-np.arange(half, dtype=np.float32) / np.float32(half))).astype(np.float32)
    pos = np.concatenate([np.arange(SEQ), PAST + np.arange(SAMP)]).astype(np.float32)
    ang = (freqs[:, None] * pos[None]).astype(np.float32)
    cos, sin = np.cos(ang), np.sin(ang)
    arrays["rope"] = np.concatenate([cos, cos, -sin, sin] * 2).astype(np.float32)
    const = np.zeros((P, C_END), np.float32)
    const[:, C_IDENT:C_IDENT + P] = np.eye(P)
    const[:, C_ONES:C_ONES + P] = 1.0
    const[:, C_IOTA:C_IOTA + P] = np.arange(P)
    const[:, C_DUP:C_DUP + P] = np.arange(P)[:, None] % ROPE == np.arange(P)[None] % ROPE
    const[0, C_MASKL:C_MASKL + 64] = 1.0
    const[0, C_MASKR + 64:C_MASKR + P] = NEG
    const[:, C_EPS] = EPS
    arrays["consts"] = const

    outs = {"o_y": [P, KD, T], "o_latent": [P, NC, T], "o_krope": [ROPE, T], "o_bkT": [PAIRS, P, SEQ],
            "o_bkS": [PAIRS, P, WIN], "o_bv": [PAIRS, P, QT, P], "o_bvS": [PAIRS, SAMP, P],
            "o_bvold": [WIN - SAMP, PAIRS * P]}
    nc = bacc.Bacc("TRN2", target_bir_lowering=False, num_devices=1)
    arrays = {n: np.ascontiguousarray(v) for n, v in arrays.items()}
    d = {n: nc.dram_tensor(f"in_{n}", v.shape, mybir.dt.from_np(v.dtype), kind="ExternalInput").ap()
         for n, v in arrays.items()}
    for n, shape in outs.items():
        d[n] = nc.dram_tensor(n, shape, F32, kind="ExternalOutput").ap()
    d["gates"] = nc.dram_tensor("gates_scratch", [NK, NK, T], F32, kind="Internal").ap()
    stream_step(nc, d)
    r = run_bass_kernel_spmd(nc, [{f"in_{n}": v for n, v in arrays.items()}], core_ids=[0]).results[0]

    def token_major(v):
        return v.transpose(2, 1, 0).reshape(v.shape[2], -1)

    y, latent = token_major(r["o_y"]), token_major(r["o_latent"])
    krope = r["o_krope"].T
    band_k = r["o_bkT"].transpose(2, 0, 1).reshape(1, 1, SEQ, HEADS, 64)
    band_kS = r["o_bkS"].transpose(2, 0, 1).reshape(1, 1, WIN, HEADS, 64)
    band_v = r["o_bv"].transpose(2, 1, 0, 3).reshape(1, 1, SEQ, HEADS, 64)
    band_vS = np.concatenate([r["o_bvold"], r["o_bvS"].transpose(1, 0, 2).reshape(SAMP, PAIRS * P)])
    return (y[None, :SEQ], y[None, SEQ:], latent[None, None, :SEQ], krope[None, None, :SEQ], band_k, band_v,
            latent[None, None, SEQ:], krope[None, None, SEQ:], band_kS, band_vS.reshape(1, 1, WIN, HEADS, 64))
```

```python
from contextlib import ExitStack

import numpy as np

import concourse.bass as bass
from concourse import mybir

F32 = mybir.dt.float32
F32R = mybir.dt.float32r
U32 = mybir.dt.uint32
ALU = mybir.AluOpType
ACT = mybir.ActivationFunctionType
AXX = mybir.AxisListType.X
AXXY = mybir.AxisListType.XY

P = 128
D = 1024
KD = D // P
SEQ, SAMP, PAST = 512, 32, 1024
T = SEQ + SAMP
H2 = T // 2
QL, KVL, NOPE, ROPE = 384, 256, 64, 32
HEADS, PAIRS = 8, 4
NQ, NC = QL // P, KVL // P
MLA_SCALE = float(NOPE + ROPE) ** -0.5
BAND_SCALE = 0.125
WIN = 512
BANDK = WIN + SAMP
MLAK = PAST + SAMP
MLA3 = MLAK // 3
NEG = -1e30
REMOVED = -3e38
EPS = 1e-6
QT = SEQ // P
TT = QT + 1
NK = 128
TOPK = 16
GB = 2
GT = 4
ROUNDS = HEADS + 2
PRE = 2 * ROUNDS
EARLY = GB * PRE

C_IDENT, C_ONES, C_IOTA, C_DUP, C_MASKL, C_MASKR, C_EPS, C_END = 0, 128, 256, 384, 512, 640, 768, 769
G_MIX, G_FFN, G_PLE, G_FIN, G_Q, G_KV, G_END = 0, 8, 16, 24, 32, 35, 37


def tensor_wait(nc, k, pe, bank, sem, value):
    pe.wait_ge(sem, value)
    nc.tensor.matmul(k.ps[:, bank, 511:512], k.const[:, C_ONES:C_ONES + P], k.const[:, C_ONES:C_ONES + 1],
                     start=True, stop=True)


def rows_of(tile):
    return P if tile < QT else SAMP


def halves(h):
    return slice(h * H2, (h + 1) * H2)


class Core:
    pass


def named_semaphores(nc, ctx, prefix, names):
    return [ctx.enter_context(nc.semaphore(f"{prefix}_{n}")) for n in names.split()]


def rms_norm(nc, k, name, sems, counts, parts, split=None, ahead=None, store=None, hold=True):
    squared, summed, rooted, inverted, normed, high, stored = sems
    use, base, was_split, stores = counts
    chunks = [(j, c) for j, part in enumerate(parts) for c in range(part[2])]
    with nc.Block(name) as block:
        @block.scalar
        def _(act):
            for n, (j, c) in enumerate(chunks):
                if n >= 2:
                    act.wait_ge(summed, base + n - 1)
                nc.scalar.activation(k.square[:, n % 2, :], parts[j][0](c), ACT.Square).then_inc(squared, 1)
            for j, part in enumerate(parts):
                act.wait_ge(summed, base + sum(x[2] for x in parts[:j + 1]))
                nc.scalar.activation(k.rstd[:, j, :].rearrange("p (h t) -> p h t", h=2), k.ps[:, 2 * j:2 * j + 2, 0:H2],
                                     ACT.Sqrt, bias=k.const[:, C_EPS:C_EPS + 1], scale=1.0 / (part[2] * P)
                                     ).then_inc(rooted, 1)
            if ahead is not None:
                ahead.round_first(act)
            if split is not None:
                for n, (j, c) in enumerate(chunks):
                    act.wait_ge(normed, base + n + 1)
                    nc.scalar.activation(split[0][:, n, :], parts[j][1](c), ACT.Copy).then_inc(high, 1)

        @block.tensor
        def _(pe):
            for n, (j, c) in enumerate(chunks):
                pe.wait_ge(squared, base + n + 1)
                for h in range(2):
                    last = nc.tensor.matmul(k.ps[:, 2 * j + h, 0:H2], k.const[:, C_ONES:C_ONES + P],
                                            k.square[:, n % 2, halves(h)], start=c == 0, stop=c == parts[j][2] - 1)
                last.then_inc(summed, 1)

        def low(engine, n):
            j, c = chunks[n]
            engine.wait_ge(high, was_split + n + 1)
            return engine.tensor_tensor(split[1][:, n, :], parts[j][1](c), split[0][:, n, :].bitcast(F32), ALU.subtract)

        @block.vector
        def _(dve):
            for j, (src, dst, count, gain) in enumerate(parts):
                dve.wait_ge(rooted, use + j + 1)
                nc.vector.reciprocal(k.rstd[:, j, :], k.rstd[:, j, :]).then_inc(inverted, 1)
                dve.wait_ge(inverted, use + j + 1)
                for c in range(count):
                    nc.vector.scalar_tensor_tensor(out=dst(c), in0=src(c), scalar=k.gain[:, gain + c:gain + c + 1],
                                                   in1=k.rstd[:, j, :], op0=ALU.mult, op1=ALU.mult).then_inc(normed, 1)
                    if split is not None and c >= 3 and c % 2 == 1:
                        low(nc.vector, c - 2)
            if split is not None:
                low(nc.vector, len(chunks) - 1)

        if split is not None:
            @block.gpsimd
            def _(pool):
                if ahead is not None:
                    ahead.rest_first(pool)
                for n in range(0, len(chunks), 2):
                    low(nc.gpsimd, n)

        if store is not None or ahead is not None:
            @block.sync
            def _(sp):
                if ahead is not None:
                    ahead.load_first(sp)
                if store is not None:
                    sp.wait_ge(normed, base + len(chunks))
                    for out, tile in store:
                        sp.dma_start(out, tile).then_inc(stored, 16)
                    if hold:
                        sp.wait_ge(stored, 16 * (stores + len(store)))


def accumulate(nc, out, pairs):
    n = len(pairs)
    for j, (lhs, rhs) in enumerate(pairs):
        last = nc.tensor.matmul(out, lhs, rhs, start=j == 0, stop=j == n - 1)
    return last


def split_products(weights, activations):
    (wh, wl), (xh, xl) = weights, activations
    return [(wh, xh), (wh, xl), (wl, xh)]


class Stream:

    def __init__(self, nc, ctx, name, dram, kc, blocks, body=2):
        self.nc, self.dram, self.kc, self.blocks, self.body = nc, dram, kc, blocks, body
        self.raw = ctx.enter_context(nc.sbuf_tensor(f"{name}_raw", [P, 2, kc * P], F32))
        self.high = ctx.enter_context(nc.sbuf_tensor(f"{name}_high", [P, 2, kc * P], F32R))
        self.low = ctx.enter_context(nc.sbuf_tensor(f"{name}_low", [P, 2, kc * P], F32R))
        in0, in1, self.high_done, self.low_done = named_semaphores(nc, ctx, name, "in0 in1 high_done low_done")
        self.loaded = (in0, in1)

    def load(self, sp, s, m):
        sp.dma_start(self.raw[:, s, :], self.dram[bass.ds(m, 1)].rearrange("o p k m -> p (o k m)")
                     ).then_inc(self.loaded[s], 16)

    def load_first(self, sp):
        for s in range(2):
            self.load(sp, s, s)

    def round_first(self, act):
        for q in range(2):
            self.round(act, 0, q)

    def rest_first(self, pool):
        for s in range(2):
            self.low_part(pool, s, s)

    def sync(self, sp):
        with sp.Fori(0, self.blocks // 2 - 1) as i:
            for s in range(2):
                sp.wait_ge(self.low_done, i * 2 + s + 1)
                self.load(sp, s, i * 2 + (s + 2))

    def round(self, act, i, q):
        s = q % 2
        act.wait_ge(self.loaded[s], i * (8 * self.body) + (q // 2 + 1) * 16)
        self.nc.scalar.activation(self.high[:, s, :], self.raw[:, s, :], ACT.Copy).then_inc(self.high_done, 1)

    def low_part(self, pool, s, m):
        pool.wait_ge(self.high_done, m + 1)
        self.nc.gpsimd.tensor_tensor(self.low[:, s, :], self.raw[:, s, :], self.high[:, s, :].bitcast(F32),
                                     ALU.subtract).then_inc(self.low_done, 1)

    def rest(self, pool):
        with pool.Fori(1, self.blocks // 2) as i:
            for s in range(2):
                self.low_part(pool, s, i * 2 + s)

    def await_block(self, pe, i, q):
        pe.wait_ge(self.low_done, i * self.body + q + 1)

    def parts(self, q, c):
        cols = slice(c * P, (c + 1) * P)
        return self.high[:, q % 2, cols], self.low[:, q % 2, cols]


def both(pair, c, cols):
    return pair[0][:, c, cols], pair[1][:, c, cols]


def load_inputs(nc, k, d):
    with nc.Block("load") as block, nc.semaphore("load_done") as loaded:
        @block.sync
        def _(sp):
            sp.dma_start(k.xT[:, :, :], d["xT"]).then_inc(loaded, 16)
            sp.dma_start(k.const[:, :], d["consts"]).then_inc(loaded, 16)
            sp.dma_start(k.gain[:, :], d["gains"]).then_inc(loaded, 16)
            sp.wait_ge(loaded, 48)


def latent_projection(nc, k, d, a, w):
    blocks = NQ + NC + 1
    with ExitStack() as ctx:
        product, bank_free = named_semaphores(nc, ctx, "lp", "product bank_free")
        with nc.Block("latent_projection") as block:
            @block.sync
            def _(sp):
                w.sync(sp)
                sp.dma_start(a.rope[:, :], d["rope"]).then_inc(a.loaded, 16)
                sp.dma_start(a.keyS[:, :, 0:PAST], d["cache_latT"]).then_inc(a.loaded, 16)
                sp.dma_start(a.kdupS[:, 0:PAST], d["cache_krT"]).then_inc(a.loaded, 16)
                sp.dma_start(a.valueS[:, 0:PAST // P, :], d["cache_lat"]).then_inc(a.loaded, 16)

            @block.gpsimd
            def _(pool):
                w.rest(pool)

            @block.tensor
            def _(pe):
                pe.sem_inc(bank_free, 4)
                with pe.Fori(0, blocks // 2) as i:
                    for s in range(2):
                        w.await_block(pe, i, s)
                        for h in range(2):
                            pe.wait_ge(bank_free, i * 4 + 2 * s + h + 1)
                            accumulate(nc, k.ps[:, 2 * s + h, 0:H2],
                                       [x for c in range(KD)
                                        for x in split_products(w.parts(s, c), both(k.h, c, halves(h)))]
                                       ).then_inc(product, 1)

            @block.scalar
            def _(act):
                def pair(i, more):
                    for s in range(2):
                        for h in range(2):
                            u = 2 * s + h
                            act.wait_ge(product, i * 4 + u + 1)
                            nc.scalar.activation(a.proj[:, bass.ds(i * 2 + s, 1), halves(h)],
                                                 k.ps[:, u:u + 1, 0:H2], ACT.Copy).then_inc(bank_free, 1)
                        if more:
                            w.round(act, i + 1, s)

                with act.Fori(0, blocks // 2 - 1) as i:
                    pair(i, True)
                pair(blocks // 2 - 1, False)


def rotary_key(nc, k, d, a):
    with ExitStack() as ctx:
        turned, summed, copied, flipped, kept = named_semaphores(nc, ctx, "rk", "turned summed copied flipped kept")
        with nc.Block("rotary_key") as block:
            @block.sync
            def _(sp):
                sp.wait_ge(copied, 2)
                sp.dma_start(d["o_krope"], a.kdup[0:ROPE, :]).then_inc(a.key_stored, 16)

            @block.vector
            def _(dve):
                dve.wait_ge(a.loaded, 64)
                nc.vector.tensor_tensor(a.turn[0:NOPE, :], a.proj[0:NOPE, NQ + NC, :], a.rope[0:NOPE, :],
                                        ALU.mult).then_inc(turned, 1)
                for c in range(NC):
                    nc.vector.tensor_copy(a.keyS[:, c, PAST:MLAK], a.proj[:, NQ + c, SEQ:T])
                dve.wait_ge(copied, 2)
                nc.vector.tensor_copy(a.kdupS[:, PAST:MLAK], a.kdup[:, SEQ:T]).then_inc(kept, 1)

            @block.tensor
            def _(pe):
                for c in range(NC):
                    last = nc.tensor.transpose(k.ps[0:SAMP, 2, c * P:(c + 1) * P], a.proj[:, NQ + c, SEQ:T],
                                               k.const[:, C_IDENT:C_IDENT + P])
                last.then_inc(flipped, 1)
                pe.wait_ge(turned, 1)
                for h in range(2):
                    nc.tensor.matmul(k.ps[:, h, 0:H2], k.const[0:NOPE, C_DUP:C_DUP + P],
                                     a.turn[0:NOPE, halves(h)], start=True, stop=True).then_inc(summed, 1)

            @block.scalar
            def _(act):
                act.wait_ge(flipped, 1)
                nc.scalar.activation(a.valueS[0:SAMP, PAST // P, :], k.ps[0:SAMP, 2, 0:KVL], ACT.Copy).then_inc(kept, 1)
                for h in range(2):
                    act.wait_ge(summed, h + 1)
                    nc.scalar.activation(a.kdup[:, halves(h)], k.ps[:, h, 0:H2], ACT.Copy).then_inc(copied, 1)


def pair_count(i, par, per, done):
    return i * (2 * per) + (par * per + done)


def pair_after(i, par):
    return (i, 1) if par == 0 else (i + 1, 0)


def over_units(engine, units, step):
    with engine.Fori(0, PAIRS // 2 - 1) as i:
        for par in range(2):
            for u in range(units):
                step(i, par, u, True, True)
    for par in range(2):
        for u in range(units):
            step(PAIRS // 2 - 1, par, u, par == 0, False)


class Softmax:

    def __init__(self, nc, k, sems, units, before=0, sample_keys=0):
        self.nc, self.k, self.units, self.band, self.sample_keys = nc, k, units, units > 2 * QT, sample_keys
        self.before = before
        (self.scored, self.biased, self.peaked, self.exped, self.scaled, self.turned, self.probT, self.mixed,
         self.kept, self.inv_done) = sems

    def rows(self, u):
        return P if u < 2 * QT else 2 * SAMP

    def keys(self, u):
        return P * (u % QT + 1) if u < 2 * QT else self.sample_keys

    def blocks(self, u):
        n = self.keys(u)
        return [(b, min(P, n - b)) for b in range(0, n, P)]

    def slot(self, par, u):
        return (par * self.units + u) % 2

    def count(self, i, par, u):
        return pair_count(i, par, self.units, self.before + u + 1)

    def ahead(self, i, par, u, n, more):
        if u + n < self.units:
            return i, par, u + n
        return (*pair_after(i, par), u + n - self.units) if more else None

    def tensor(self, pe, i, par, u, more, scores, project, values):
        nc, k = self.nc, self.k
        further = self.ahead(i, par, u, 2, more)
        if further is not None:
            pe.wait_ge(self.biased if self.band else self.exped, self.count(i, par, u))
            scores(*further)
        s = self.slot(par, u)
        if u < 2 * QT:
            pe.wait_ge(self.scaled, self.count(i, par, u))
        else:
            tensor_wait(nc, k, pe, 2, self.scaled, self.count(i, par, u))
        r = self.rows(u)
        for j, (b, n) in enumerate(self.blocks(u)):
            last = nc.tensor.transpose(k.ps[0:n, 3 + s, j * r:j * r + r], k.prob[0:r, s, b:b + n],
                                       k.const[0:r, C_IDENT:C_IDENT + r])
        last.then_inc(self.turned, 1)
        if more:
            project(*pair_after(i, par), u)
        pe.wait_ge(self.probT, self.count(i, par, u))
        pe.wait_ge(self.kept, self.count(i, par, u))
        values(i, par, u).then_inc(self.mixed, 1)

    def exponential(self, act, i, par, u):
        nc, k, s = self.nc, self.k, self.slot(par, u)
        r, n = self.rows(u), self.keys(u)
        act.wait_ge(self.peaked, self.count(i, par, u))
        src = k.biased[0:r, s, 0:n] if self.band else k.ps[0:r, s, 0:n]
        nc.scalar.activation(k.prob[0:r, s, 0:n], src, ACT.Exp, bias=k.peak[0:r, s:s + 1],
                             scale=1.0 if self.band else MLA_SCALE,
                             accum_out=k.total[0:r, s:s + 1]).then_inc(self.exped, 1)

    def transposed(self, act, i, par, u):
        nc, k, s = self.nc, self.k, self.slot(par, u)
        act.wait_ge(self.turned, self.count(i, par, u))
        r, blocks = self.rows(u), self.blocks(u)
        full = len([b for b in blocks if b[1] == P])
        last = nc.scalar.activation(k.probT[:, s, 0:full * r], k.ps[:, 3 + s, 0:full * r], ACT.Copy)
        for j in range(full, len(blocks)):
            n = blocks[j][1]
            last = nc.scalar.activation(k.probT[0:n, s, j * r:j * r + r], k.ps[0:n, 3 + s, j * r:j * r + r], ACT.Copy)
        last.then_inc(self.probT, 1)

    def scalar(self, act, i, par, u, more, collect, keep):
        unit = self.ahead(i, par, u, 2, more)
        if unit is not None:
            self.exponential(act, *unit)
        if more:
            collect(*pair_after(i, par), u)
        unit = self.ahead(i, par, u, 1, more)
        if unit is not None:
            self.transposed(act, *unit)
        act.wait_ge(self.mixed, self.count(i, par, u))
        keep(i, par, u).then_inc(self.kept, 1)

    def maxima(self, dve, i, par, u):
        nc, k, s = self.nc, self.k, self.slot(par, u)
        r, n = self.rows(u), self.keys(u)
        dve.wait_ge(self.scored, self.count(i, par, u))
        if not self.band:
            nc.vector.tensor_reduce(k.rawpeak[0:r, s:s + 1], k.ps[0:r, s, 0:n], AXX, ALU.max,
                                    negate=True).then_inc(self.biased, 1)
            dve.wait_ge(self.biased, self.count(i, par, u))
            nc.vector.tensor_scalar(k.peak[0:r, s:s + 1], k.rawpeak[0:r, s:s + 1], MLA_SCALE,
                                    None, ALU.mult).then_inc(self.peaked, 1)
            return
        if u < 2 * QT:
            q0 = P * (u % QT)
            nc.vector.tensor_tensor(k.biased[0:r, s, 0:n], k.ps[0:r, s, 0:n],
                                    k.bias[:, par, u // QT, WIN - q0:WIN - q0 + n], ALU.add).then_inc(self.biased, 1)
        else:
            nc.vector.tensor_tensor(k.biased[0:r, s, 0:WIN], k.ps[0:r, s, 0:WIN], k.biasS[:, par, 0:WIN], ALU.add)
            nc.vector.tensor_tensor(k.biased[0:r, s, WIN:n], k.ps[0:r, 2, 0:SAMP],
                                    k.biasS[:, par, WIN:n], ALU.add).then_inc(self.biased, 1)
        dve.wait_ge(self.biased, self.count(i, par, u))
        nc.vector.tensor_reduce(k.peak[0:r, s:s + 1], k.biased[0:r, s, 0:n], AXX, ALU.max,
                                negate=True).then_inc(self.peaked, 1)

    def vector(self, dve, i, par, u, more, await_bias=None):
        nc, k, s = self.nc, self.k, self.slot(par, u)
        unit = self.ahead(i, par, u, 1, more)
        if unit is not None:
            if unit[2] == 0 and await_bias is not None:
                await_bias(*unit[:2])
            self.maxima(dve, *unit)
        r, n = self.rows(u), self.keys(u)
        dve.wait_ge(self.exped, self.count(i, par, u))
        nc.vector.reciprocal(k.inverse[0:r, s:s + 1], k.total[0:r, s:s + 1]).then_inc(self.inv_done, 1)
        dve.wait_ge(self.inv_done, self.count(i, par, u))
        nc.vector.tensor_scalar(k.prob[0:r, s, 0:n], k.prob[0:r, s, 0:n], k.inverse[0:r, s:s + 1],
                                None, ALU.mult).then_inc(self.scaled, 1)


SOFTMAX_SEMS = "scored biased peaked exped scaled turned probT mixed kept inv_done"


def softmax_buffers(nc, k, ctx, p, keys, rows):
    k.prob = ctx.enter_context(nc.sbuf_tensor(f"{p}_prob", [P, 2, keys], F32))
    k.probT = ctx.enter_context(nc.sbuf_tensor(f"{p}_probT", [P, 2, rows], F32))
    k.peak, k.rawpeak, k.total, k.inverse = (
        ctx.enter_context(nc.sbuf_tensor(f"{p}_{n}", [P, 2], F32)) for n in ("peak", "rawpeak", "total", "inverse"))


def latent_attention(nc, k, d, a):
    UNITS, GROUPS = 2 * QT, 6
    with ExitStack() as ctx:
        softmax_buffers(nc, k, ctx, "ma", SEQ, SEQ)
        wq = ctx.enter_context(nc.sbuf_tensor("m_wq", [P, 2, 2, NQ, P], F32))
        wk = ctx.enter_context(nc.sbuf_tensor("m_wk", [P, 2, NC, P], F32))
        q = ctx.enter_context(nc.sbuf_tensor("m_q", [P, 2, 2, T], F32))
        kk = ctx.enter_context(nc.sbuf_tensor("m_k", [P, 2, 2, SEQ], F32))
        v = ctx.enter_context(nc.sbuf_tensor("m_v", [P, 2, QT, P], F32))
        w_in0, w_in1, wide_in, projected, collected, rotated, spread = named_semaphores(
            nc, ctx, "ma", "w_in0 w_in1 wide_in projected collected rotated spread")
        w_in = (w_in0, w_in1)
        sm = Softmax(nc, k, a.softmax, UNITS)

        def load(sp, i, par):
            p = i * 2 + par
            sp.dma_start(wq[:, par].rearrange("p a k m -> p (a k m)"),
                         d["w_uq"][bass.ds(p, 1)].rearrange("o p m -> p (o m)")).then_inc(w_in[par], 16)
            sp.dma_start(wk[:, par].rearrange("p k m -> p (k m)"),
                         d["w_uk"][bass.ds(p, 1)].rearrange("o p m -> p (o m)")).then_inc(w_in[par], 16)

        def rows(hh):
            return slice(NOPE * hh, NOPE * (hh + 1))

        with nc.Block("latent_attention") as block:
            @block.sync
            def _(sp):
                load(sp, 0, 0)
                sp.dma_start(a.wuv[:, :, :], d["w_uv"]).then_inc(wide_in, 16)
                load(sp, 0, 1)
                sp.dma_start(a.wukT[:, :, :], d["w_ukT"]).then_inc(a.lift_in, 16)
                with sp.Fori(1, PAIRS // 2) as i:
                    for par in range(2):
                        sp.wait_ge(projected, i * (2 * GROUPS) + (par - 1) * GROUPS)
                        load(sp, i, par)
                sp.wait_ge(a.latent_stored, 16)
                sp.wait_ge(a.key_stored, 16)

            @block.tensor
            def _(pe):
                def project(i, par, g):
                    if g >= GROUPS:
                        return
                    if g == 0:
                        pe.wait_ge(w_in[par], i * 32 + 32)
                    bank = (2, 7)[g % 2]
                    pe.wait_ge(collected, pair_count(i, par, GROUPS, g + 1))
                    pe.wait_ge(rotated, pair_count(i, par, 4, g + 1))
                    if g < 4:
                        last = accumulate(nc, k.ps[:, bank, 0:H2],
                                          [(wq[:, par, g // 2, c, :], a.proj[:, c, halves(g % 2)]) for c in range(NQ)])
                    elif g == 4:
                        last = accumulate(nc, k.ps[:, bank, 0:SEQ],
                                          [(wk[:, par, c, :], a.proj[:, NQ + c, 0:SEQ]) for c in range(NC)])
                    else:
                        for t in range(QT):
                            last = accumulate(nc, k.ps[:, bank, t * P:(t + 1) * P],
                                              [(a.proj[:, NQ + c, t * P:(t + 1) * P],
                                                a.wuv[:, c, bass.ds((i * 2 + par) * P, P)]) for c in range(NC)])
                    last.then_inc(projected, 1)

                def scores(i, par, u):
                    if u == 0:
                        pe.wait_ge(collected, pair_count(i, par, GROUPS, GROUPS + 2))
                        pe.wait_ge(rotated, pair_count(i, par, 4, 4 + 2))
                    hh, q0, n, s = u // QT, P * (u % QT), sm.keys(u), sm.slot(par, u)
                    nc.tensor.matmul(k.ps[:, s, 0:n], q[:, par, hh, q0:q0 + P], kk[:, par, hh, 0:n],
                                     start=True, stop=False)
                    nc.tensor.matmul(k.ps[:, s, q0:q0 + P], k.const[0:1, C_MASKL:C_MASKL + P],
                                     k.const[0:1, C_MASKR:C_MASKR + P], start=False, stop=True).then_inc(sm.scored, 1)

                def values(i, par, u):
                    s, r = sm.slot(par, u), rows(u // QT)
                    return accumulate(nc, k.ps[r, 5 + s, 0:P],
                                      [(v[:, par, j, r], k.probT[:, s, j * P:(j + 1) * P]) for j in range(u % QT + 1)])

                pe.wait_ge(wide_in, 16)
                for g in range(GROUPS):
                    project(0, 0, g)
                pe.wait_ge(spread, 4)
                for u in range(2):
                    scores(0, 0, u)
                over_units(pe, UNITS, lambda i, par, u, more, more2:
                           sm.tensor(pe, i, par, u, more, scores, project, values))

            @block.scalar
            def _(act):
                def collect(i, par, g):
                    if g >= GROUPS:
                        return
                    act.wait_ge(projected, pair_count(i, par, GROUPS, g + 1))
                    bank = (2, 7)[g % 2]
                    if g < 4:
                        hh, h = g // 2, g % 2
                        r = rows(hh)
                        if h == 1:
                            nc.scalar.activation(a.qS[r, bass.ds((i * 2 + par) * 2 + hh, 1), :],
                                                 k.ps[r, bank:bank + 1, H2 - SAMP:H2], ACT.Copy)
                        last = nc.scalar.activation(q[r, par, hh, halves(h)], k.ps[r, bank, 0:H2], ACT.Copy)
                    elif g == 4:
                        for hh in range(2):
                            last = nc.scalar.activation(kk[rows(hh), par, hh, :], k.ps[rows(hh), bank, 0:SEQ], ACT.Copy)
                    else:
                        last = nc.scalar.activation(v[:, par].rearrange("p t c -> p (t c)"), k.ps[:, bank, :], ACT.Copy)
                    last.then_inc(collected, 1)

                def keep(i, par, u):
                    s, r, q0 = sm.slot(par, u), rows(u // QT), P * (u % QT)
                    return nc.scalar.activation(a.oA[r, bass.ds(i * 2 + par, 1), q0:q0 + P],
                                                k.ps[r, 5 + s:6 + s, 0:P], ACT.Copy)

                act.sem_inc(collected, 2)
                act.sem_inc(sm.kept, 2)
                for g in range(GROUPS):
                    collect(0, 0, g)
                for u in range(2):
                    sm.exponential(act, 0, 0, u)
                sm.transposed(act, 0, 0, 0)
                over_units(act, UNITS, lambda i, par, u, more, more2:
                           sm.scalar(act, i, par, u, more, collect, keep))

            @block.vector
            def _(dve):
                def rotate(i, par, g):
                    if g >= 4:
                        return
                    dve.wait_ge(projected, pair_count(i, par, GROUPS, g + 1))
                    hh, h, bank = g // 2, g % 2, (2, 7)[g % 2]
                    r = rows(1 - hh)
                    if h == 1:
                        nc.vector.tensor_tensor(a.qS[r, bass.ds((i * 2 + par) * 2 + hh, 1), :],
                                                k.ps[r, bank:bank + 1, H2 - SAMP:H2],
                                                a.rope[r, SEQ:T].unsqueeze(1), ALU.mult)
                    nc.vector.tensor_tensor(q[r, par, hh, halves(h)], k.ps[r, bank, 0:H2], a.rope[r, halves(h)],
                                            ALU.mult).then_inc(rotated, 1)

                def step(i, par, u, more, more2):
                    sm.vector(dve, i, par, u, more)
                    if more:
                        rotate(*pair_after(i, par), u)

                dve.sem_inc(rotated, 2)
                for par in range(2):
                    for hh in range(2):
                        r = rows(1 - hh)
                        nc.vector.tensor_copy(kk[r, par, hh, :], a.kdup[r, 0:SEQ]).then_inc(spread, 1)
                for g in range(4):
                    rotate(0, 0, g)
                sm.maxima(dve, 0, 0, 0)
                over_units(dve, UNITS, step)


def latent_sample(nc, k, d, a):
    TILES = HEADS * SAMP // P
    PER = HEADS // TILES
    KB = PAST // P + 1
    with ExitStack() as ctx:
        prob = ctx.enter_context(nc.sbuf_tensor("s_prob", [P, TILES, MLAK], F32))
        probT = ctx.enter_context(nc.sbuf_tensor("s_probT", [P, TILES, KB * P], F32))
        ql = ctx.enter_context(nc.sbuf_tensor("s_ql", [P, NC, HEADS, SAMP], F32))
        qr = ctx.enter_context(nc.sbuf_tensor("s_qr", [P, HEADS, SAMP], F32))
        ol = ctx.enter_context(nc.sbuf_tensor("s_ol", [P, NC, HEADS, SAMP], F32))
        rawpeak, peak, total, inverse = (ctx.enter_context(nc.sbuf_tensor(f"s_{n}", [P, TILES], F32))
                                         for n in ("rawpeak", "peak", "total", "inverse"))
        (lifted, in_sbuf, cleared, packed, scored, maximal, peaked, exped, inverted, scaled, turned, copied, mixed,
         kept, lowered, stored) = named_semaphores(
            nc, ctx, "ls", "lifted in_sbuf cleared packed scored maximal peaked exped inverted scaled turned copied "
            "mixed kept lowered stored")

        def rows(hh):
            return slice(NOPE * hh, NOPE * (hh + 1))

        with nc.Block("latent_sample") as block:
            @block.gpsimd
            def _(pool):
                nc.gpsimd.memset(qr[:, :, :], 0.0).then_inc(cleared, 1)

            @block.tensor
            def _(pe):
                pe.wait_ge(a.lift_in, 16)
                for hh in range(2):
                    for c in range(NC):
                        for p in range(PAIRS):
                            last = nc.tensor.matmul(k.ps[:, 4 + 2 * hh + c, p * SAMP:(p + 1) * SAMP],
                                                    a.wukT[rows(hh), p, c * P:(c + 1) * P],
                                                    a.qS[rows(hh), 2 * p + hh, :], start=True, stop=True)
                    last.then_inc(lifted, 1)
                pe.wait_ge(in_sbuf, 2)
                pe.wait_ge(packed, 2)
                for t in range(TILES):
                    heads = slice(t * PER, (t + 1) * PER)
                    for j in range(3):
                        keys = slice(j * MLA3, (j + 1) * MLA3)
                        last = accumulate(nc, k.ps[:, 3 * t + j, 0:MLA3],
                                          [(ql[:, c, heads, :].rearrange("p h t -> p (h t)"), a.keyS[:, c, keys])
                                           for c in range(NC)]
                                          + [(qr[:, heads, :].rearrange("p h t -> p (h t)"), a.kdupS[:, keys])])
                    last.then_inc(scored, 1)
                for t in range(TILES):
                    pe.wait_ge(scaled, t + 1)
                    for j in range(KB):
                        n = min(P, MLAK - j * P)
                        last = nc.tensor.transpose(k.ps[0:n, 3 * t + j // 4, (j % 4) * P:(j % 4 + 1) * P],
                                                   prob[:, t, j * P:j * P + n], k.const[:, C_IDENT:C_IDENT + P])
                        if j % 4 == 3 or j == KB - 1:
                            last.then_inc(turned, 1)
                for t in range(TILES):
                    pe.wait_ge(copied, 3 * t + 3)
                    for c in range(NC):
                        last = accumulate(nc, k.ps[:, 6 + t, c * P:(c + 1) * P],
                                          [(a.valueS[0:min(P, MLAK - j * P), j, c * P:(c + 1) * P],
                                            probT[0:min(P, MLAK - j * P), t, j * P:(j + 1) * P]) for j in range(KB)])
                    last.then_inc(mixed, 1)
                pe.wait_ge(kept, TILES)
                for head in range(HEADS):
                    last = accumulate(nc, k.ps[rows(head % 2), 0, (head // 2) * SAMP:(head // 2 + 1) * SAMP],
                                      [(a.wuv[:, c, head * NOPE:(head + 1) * NOPE], ol[:, c, head, :])
                                       for c in range(NC)])
                last.then_inc(lowered, 1)

            @block.scalar
            def _(act):
                for hh in range(2):
                    act.wait_ge(lifted, hh + 1)
                    for c in range(NC):
                        last = nc.scalar.activation(
                            ql[:, c].rearrange("p (g h) t -> p g h t", h=2)[:, :, hh, :],
                            k.ps[:, 4 + 2 * hh + c, 0:PAIRS * SAMP].rearrange("p (g t) -> p g t", g=PAIRS), ACT.Copy)
                    last.then_inc(in_sbuf, 1)
                for t in range(TILES):
                    act.wait_ge(peaked, t + 1)
                    nc.scalar.activation(prob[:, t, :].rearrange("p (a b) -> p a b", a=3),
                                         k.ps[:, 3 * t:3 * t + 3, 0:MLA3], ACT.Exp, bias=peak[:, t:t + 1],
                                         scale=MLA_SCALE, accum_out=total[:, t:t + 1]).then_inc(exped, 1)
                for t in range(TILES):
                    for j in range(3):
                        act.wait_ge(turned, 3 * t + j + 1)
                        n = P if j < 2 else MLAK - 8 * P
                        w = 4 * P if j < 2 else P
                        nc.scalar.activation(probT[0:n, t, 4 * j * P:4 * j * P + w], k.ps[0:n, 3 * t + j, 0:w],
                                             ACT.Copy).then_inc(copied, 1)
                for t in range(TILES):
                    act.wait_ge(mixed, t + 1)
                    nc.scalar.activation(ol[:, :, t * PER:(t + 1) * PER, :].rearrange("p c h t -> p c (h t)"),
                                         k.ps[:, 6 + t, 0:NC * P].rearrange("p (c m) -> p c m", c=NC),
                                         ACT.Copy).then_inc(kept, 1)
                act.wait_ge(lowered, 1)
                nc.scalar.activation(a.oA[:, :, SEQ:T], k.ps[:, 0, 0:PAIRS * SAMP].rearrange("p (c t) -> p c t", c=PAIRS),
                                     ACT.Copy).then_inc(stored, 1)

            @block.vector
            def _(dve):
                dve.wait_ge(cleared, 1)
                for hh in range(2):
                    r = rows(1 - hh)
                    nc.vector.tensor_copy(qr[r].rearrange("p (c h) t -> p c h t", h=2)[:, :, hh, :],
                                          a.qS[r].rearrange("p (c h) t -> p c h t", h=2)[:, :, hh, :]).then_inc(packed, 1)
                for t in range(TILES):
                    dve.wait_ge(scored, t + 1)
                    nc.vector.tensor_reduce(rawpeak[:, t:t + 1], k.ps[:, 3 * t:3 * t + 3, 0:MLA3], AXXY, ALU.max,
                                            negate=True).then_inc(maximal, 1)
                    dve.wait_ge(maximal, t + 1)
                    nc.vector.tensor_scalar(peak[:, t:t + 1], rawpeak[:, t:t + 1], MLA_SCALE, None,
                                            ALU.mult).then_inc(peaked, 1)
                for t in range(TILES):
                    dve.wait_ge(exped, t + 1)
                    nc.vector.reciprocal(inverse[:, t:t + 1], total[:, t:t + 1]).then_inc(inverted, 1)
                    dve.wait_ge(inverted, t + 1)
                    nc.vector.tensor_scalar(prob[:, t, :], prob[:, t, :], inverse[:, t:t + 1], None,
                                            ALU.mult).then_inc(scaled, 1)


def band_attention(nc, k, d, a, ahead):
    UNITS, GROUPS = 2 * QT + 1, 7
    with ExitStack() as ctx:
        softmax_buffers(nc, k, ctx, "ba", BANDK, SEQ)
        k.biased = ctx.enter_context(nc.sbuf_tensor("biased", [P, 2, BANDK], F32))
        k.bias = ctx.enter_context(nc.sbuf_tensor("bias", [P, 2, 2, WIN + P], F32))
        k.biasS = ctx.enter_context(nc.sbuf_tensor("biasS", [2 * SAMP, 2, BANDK], F32))
        raw = [ctx.enter_context(nc.sbuf_tensor(f"bw_{n}", [P, KD * P], F32)) for n in "qkv"]
        high = [ctx.enter_context(nc.sbuf_tensor(f"bw_high_{n}", [P, KD * P], F32R)) for n in "qkv"]
        low = [ctx.enter_context(nc.sbuf_tensor(f"bw_low_{n}", [P, KD * P], F32R)) for n in "qkv"]
        q = ctx.enter_context(nc.sbuf_tensor("b_q", [P, 2, T], F32))
        kk = ctx.enter_context(nc.sbuf_tensor("b_k", [P, 2, SEQ + BANDK], F32))
        v = ctx.enter_context(nc.sbuf_tensor("b_v", [P, 2, 2 * QT + 1, P], F32))
        sample = [ctx.enter_context(nc.sbuf_tensor(f"b_sample_{n}", [P, KD, P], F32R)) for n in ("high", "low")]
        (wq_in, wk_in, wv_in, cache_in0, cache_in1, bias_in0, bias_in1, stored0, stored1, moved, w_high, w_low,
         projected, collected, sampled) = named_semaphores(
            nc, ctx, "ba", "wq_in wk_in wv_in cache_in0 cache_in1 bias_in0 bias_in1 stored0 stored1 moved w_high w_low "
            "projected collected sampled")
        w_in, cache_in, bias_in = (wq_in, wk_in, wv_in), (cache_in0, cache_in1), (bias_in0, bias_in1)
        stored = (stored0, stored1)
        sm = Softmax(nc, k, a.softmax, UNITS, PAIRS * 2 * QT, BANDK)

        def one(name, i, par):
            return d[name][bass.ds(i * 2 + par, 1)]

        def load_weight(sp, j, i, par):
            sp.dma_start(raw[j][:, :], one(("w_bq", "w_bk", "w_bv")[j], i, par).rearrange("o p k m -> p (o k m)")
                         ).then_inc(w_in[j], 16)

        def load_cache(sp, i, par):
            sp.dma_start(kk[:, par, SEQ:SEQ + WIN], one("cache_bkT", i, par).rearrange("o p t -> p (o t)")
                         ).then_inc(cache_in[par], 16)
            sp.dma_start(v[:, par, QT:2 * QT, :], one("cache_bv", i, par).rearrange("o p n c -> p (o n) c")
                         ).then_inc(cache_in[par], 16)
            sp.dma_start(k.bias[:, par], one("bias", i, par).rearrange("o p h m -> p (o h) m")).then_inc(bias_in[par], 16)
            sp.dma_start(k.biasS[:, par, :], one("biasS", i, par).rearrange("o p m -> p (o m)")
                         ).then_inc(bias_in[par], 16)

        def store(sp, i, par):
            sp.wait_ge(collected, pair_count(i, par, GROUPS, GROUPS + 1))
            sp.wait_ge(cache_in[par], i * 32 + 32)
            for name, dims, tile in (("o_bkT", "o p t -> p (o t)", kk[:, par, 0:SEQ]),
                                     ("o_bkS", "o p t -> p (o t)", kk[:, par, SEQ + SAMP:SEQ + BANDK]),
                                     ("o_bv", "o p n c -> p (o n) c", v[:, par, 0:QT, :]),
                                     ("o_bvS", "o p c -> p (o c)", v[0:SAMP, par, 2 * QT, :])):
                sp.dma_start(one(name, i, par).rearrange(dims), tile).then_inc(stored[par], 16)

        with nc.Block("band_attention") as block:
            @block.sync
            def _(sp):
                for j in range(3):
                    load_weight(sp, j, 0, 0)
                load_cache(sp, 0, 0)
                for j in range(3):
                    sp.wait_ge(w_low, j + 1)
                    load_weight(sp, j, 0, 1)
                load_cache(sp, 0, 1)
                sp.dma_start(d["o_bvold"], d["cache_bv_kept"]).then_inc(moved, 16)
                with sp.Fori(0, PAIRS // 2 - 1) as i:
                    for par in range(2):
                        store(sp, i, par)
                        for j in range(3):
                            sp.wait_ge(w_low, pair_count(i, par, 3, 3 + j + 1))
                            load_weight(sp, j, i + 1, par)
                        sp.wait_ge(sm.mixed, sm.count(i, par, UNITS - 1))
                        sp.wait_ge(stored[par], i * 64 + 64)
                        load_cache(sp, i + 1, par)
                ahead.load_first(sp)
                for par in range(2):
                    store(sp, PAIRS // 2 - 1, par)
                    sp.wait_ge(stored[par], PAIRS // 2 * 64)
                sp.wait_ge(moved, 16)

            @block.gpsimd
            def _(pool):
                with pool.Fori(0, PAIRS) as p:
                    for j in range(3):
                        pool.wait_ge(w_high, p * 3 + j + 1)
                        nc.gpsimd.tensor_tensor(low[j][:, :], raw[j][:, :], high[j][:, :].bitcast(F32),
                                                ALU.subtract).then_inc(w_low, 1)
                ahead.rest_first(pool)

            @block.tensor
            def _(pe):
                def project(i, par, g):
                    if g >= GROUPS:
                        return
                    j = min(g // 2, 2)
                    if g == 6:
                        pe.wait_ge(sampled, 2)
                    if g % 2 == 0 and g < 6:
                        pe.wait_ge(w_low, pair_count(i, par, 3, j + 1))
                    pe.wait_ge(collected, pair_count(i, par, GROUPS, g + 1))

                    def w(c):
                        return high[j][:, c * P:(c + 1) * P], low[j][:, c * P:(c + 1) * P]

                    if g < 4:
                        last = accumulate(nc, k.ps[:, 7, 0:H2],
                                          [x for c in range(KD) for x in split_products(w(c), both(k.h, c, halves(g % 2)))])
                    else:
                        for t in range(2 * (g - 4), min(2 * (g - 3), TT)):
                            o, cols = (t % 2) * P, slice(t * P, (t + 1) * P)
                            last = accumulate(nc, k.ps[:, 7, o:o + P],
                                              [x for c in range(KD) for x in split_products(
                                                  both(k.h, c, cols) if t < QT else both(sample, c, slice(0, P)), w(c))])
                    last.then_inc(projected, 1)

                def scores(i, par, u):
                    if u == 0:
                        pe.wait_ge(collected, pair_count(i, par, GROUPS, GROUPS + 1))
                    s = sm.slot(par, u)
                    if u < 2 * QT:
                        a0, q0 = 64 * (u // QT), P * (u % QT)
                        last = nc.tensor.matmul(k.ps[:, s, 0:sm.keys(u)], q[a0:a0 + 64, par, q0:q0 + P],
                                                kk[a0:a0 + 64, par, 0:sm.keys(u)], start=True, stop=True)
                    else:
                        tensor_wait(nc, k, pe, 2, cache_in[par], i * 32 + 32)
                        for hh in range(2):
                            a0 = 64 * hh
                            for bank, k0, n in ((s, SEQ, WIN), (2, SEQ + WIN, SAMP)):
                                last = nc.tensor.matmul(k.ps[SAMP * hh:SAMP * (hh + 1), bank, 0:n],
                                                        q[a0:a0 + 64, par, SEQ:T], kk[a0:a0 + 64, par, k0:k0 + n],
                                                        start=True, stop=True)
                    last.then_inc(sm.scored, 1)

                def values(i, par, u):
                    s = sm.slot(par, u)
                    if u < 2 * QT:
                        a0 = 64 * (u // QT)
                        return accumulate(nc, k.ps[a0:a0 + 64, 5 + s, 0:P],
                                          [(v[:, par, j, a0:a0 + 64], k.probT[:, s, j * P:(j + 1) * P])
                                           for j in range(u % QT + 1)])
                    for hh in range(2):
                        a0, r = 64 * hh, 2 * SAMP
                        last = accumulate(nc, k.ps[a0:a0 + 64, 5 + s, 0:SAMP],
                                          [(v[0:n, par, QT + j, a0:a0 + 64],
                                            k.probT[0:n, s, j * r + SAMP * hh:j * r + SAMP * (hh + 1)])
                                           for j, (_, n) in enumerate(sm.blocks(u))])
                    return last

                for g in range(GROUPS):
                    project(0, 0, g)
                for u in range(2):
                    scores(0, 0, u)
                over_units(pe, UNITS, lambda i, par, u, more, more2:
                           sm.tensor(pe, i, par, u, more, scores, project, values))

            @block.scalar
            def _(act):
                def round_weight(j, i, par):
                    act.wait_ge(w_in[j], pair_count(i, par, 16, 16))
                    nc.scalar.activation(high[j][:, :], raw[j][:, :], ACT.Copy).then_inc(w_high, 1)

                def collect(i, par, g, further):
                    if g >= GROUPS:
                        return
                    act.wait_ge(projected, pair_count(i, par, GROUPS, g + 1))
                    if g < 2:
                        last = nc.scalar.activation(q[:, par, halves(g)], k.ps[:, 7, 0:H2], ACT.Copy, scale=BAND_SCALE)
                    elif g == 2:
                        act.wait_ge(cache_in[par], i * 32 + 32)
                        last = nc.scalar.activation(kk[:, par, 0:H2], k.ps[:, 7, 0:H2], ACT.Copy)
                    elif g == 3:
                        nc.scalar.activation(kk[:, par, H2:SEQ], k.ps[:, 7, 0:SEQ - H2], ACT.Copy)
                        last = nc.scalar.activation(kk[:, par, SEQ + WIN:SEQ + BANDK], k.ps[:, 7, SEQ - H2:H2], ACT.Copy)
                    elif g < 6:
                        t = 2 * (g - 4)
                        last = nc.scalar.activation(v[:, par, t:t + 2, :].rearrange("p t c -> p (t c)"),
                                                    k.ps[:, 7, 0:2 * P], ACT.Copy)
                    else:
                        last = nc.scalar.activation(v[0:SAMP, par, 2 * QT, :], k.ps[0:SAMP, 7, 0:P], ACT.Copy)
                    last.then_inc(collected, 1)
                    if further and g in (1, 3, 6):
                        round_weight(min(g // 2, 2), *pair_after(i, par))

                def keep(i, par, u):
                    s, p = sm.slot(par, u), bass.ds(i * 2 + par, 1)
                    if u < 2 * QT:
                        a0, q0 = 64 * (u // QT), P * (u % QT)
                        return nc.scalar.activation(a.oB[a0:a0 + 64, p, q0:q0 + P],
                                                    k.ps[a0:a0 + 64, 5 + s:6 + s, 0:P], ACT.Copy)
                    return nc.scalar.activation(a.oB[:, p, SEQ:T], k.ps[:, 5 + s:6 + s, 0:SAMP], ACT.Copy)

                act.sem_inc(collected, 1)
                for j in range(3):
                    round_weight(j, 0, 0)
                for g in range(GROUPS):
                    collect(0, 0, g, True)
                for u in range(2):
                    sm.exponential(act, 0, 0, u)
                sm.transposed(act, 0, 0, 0)
                over_units(act, UNITS, lambda i, par, u, more, more2:
                           sm.scalar(act, i, par, u, more, lambda i, par, g: collect(i, par, g, more2), keep))
                ahead.round_first(act)

            @block.vector
            def _(dve):
                def await_bias(i, par):
                    dve.wait_ge(bias_in[par], i * 32 + 32)

                for x, out in zip(k.h, sample):
                    nc.vector.tensor_copy(out[:, :, :].rearrange("p c (n t) -> p c n t", t=SAMP),
                                          x[:, :, SEQ:T].unsqueeze(2).to_broadcast([P, KD, P // SAMP, SAMP])
                                          ).then_inc(sampled, 1)
                await_bias(0, 0)
                sm.maxima(dve, 0, 0, 0)
                over_units(dve, UNITS, lambda i, par, u, more, more2:
                           sm.vector(dve, i, par, u, more, await_bias))


def gated_merge(nc, k, d, a, w, ahead):
    with ExitStack() as ctx:
        o = [[ctx.enter_context(nc.sbuf_tensor(f"gm_o{b}{p}", [P, PAIRS, T], F32R)) for p in ("high", "low")]
             for b in range(2)]
        gate = ctx.enter_context(nc.sbuf_tensor("gm_gate", [P, 2, T], F32))
        gated, valued, gate_done, term, merged, o_high, o_low, m_high, m_low = named_semaphores(
            nc, ctx, "gm", "gated valued gate_done term merged o_high o_low m_high m_low")

        with nc.Block("gated_merge") as block:
            @block.sync
            def _(sp):
                w.sync(sp)
                ahead.load_first(sp)

            @block.gpsimd
            def _(pool):
                w.rest(pool)
                ahead.rest_first(pool)

            @block.tensor
            def _(pe):
                with pe.Fori(0, KD // 2) as i:
                    for s in range(2):
                        for b in range(2):
                            w.await_block(pe, i, 3 * s + b)
                            pe.wait_ge(gate_done, i * 4 + 2 * s + 1)
                            for h in range(2):
                                last = accumulate(nc, k.ps[:, 2 * b + h, 0:H2],
                                                  [x for c in range(KD)
                                                   for x in split_products(w.parts(3 * s + b, c), both(k.h, c, halves(h)))])
                            last.then_inc(gated, 1)
                        w.await_block(pe, i, 3 * s + 2)
                        pe.wait_ge(o_low, 2 * PAIRS)
                        pe.wait_ge(term, i * 4 + 2 * s + 1)
                        for b in range(2):
                            for h in range(2):
                                last = accumulate(nc, k.ps[:, 4 + 2 * b + h, 0:H2],
                                                  [x for c in range(PAIRS)
                                                   for x in split_products(w.parts(3 * s + 2, b * PAIRS + c),
                                                                           both(o[b], c, halves(h)))])
                            last.then_inc(valued, 1)

            @block.scalar
            def _(act):
                def pair(i, more):
                    for s in range(2):
                        act.wait_ge(merged, i * 2 + s + 1)
                        for b in range(2):
                            act.wait_ge(gated, i * 4 + 2 * s + b + 1)
                            nc.scalar.activation(gate[:, b, :].rearrange("p (h t) -> p h t", h=2),
                                                 k.ps[:, 2 * b:2 * b + 2, 0:H2], ACT.Sigmoid).then_inc(gate_done, 1)
                            round_next(i, 3 * s + b, more)
                        act.wait_ge(valued, i * 4 + 2 * s + 2)
                        round_next(i, 3 * s + 2, more)

                def round_next(i, q, more):
                    if q < 4:
                        w.round(act, i, q + 2)
                    elif more:
                        w.round(act, i + 1, q - 4)

                act.sem_inc(gate_done, 1)
                for b, x in enumerate((a.oA, a.oB)):
                    for c in range(PAIRS):
                        nc.scalar.activation(o[b][0][:, c, :], x[:, c, :], ACT.Copy).then_inc(o_high, 1)
                with act.Fori(0, KD // 2 - 1) as i:
                    pair(i, True)
                pair(KD // 2 - 1, False)
                ahead.round_first(act)

            @block.vector
            def _(dve):
                dve.sem_inc(term, 1)
                dve.sem_inc(merged, 1)
                for b, x in enumerate((a.oA, a.oB)):
                    for c in range(PAIRS):
                        dve.wait_ge(o_high, b * PAIRS + c + 1)
                        nc.vector.tensor_tensor(o[b][1][:, c, :], x[:, c, :], o[b][0][:, c, :].bitcast(F32),
                                                ALU.subtract).then_inc(o_low, 1)
                with dve.Fori(0, KD // 2) as i:
                    for s in range(2):
                        for b in range(2):
                            dve.wait_ge(gate_done, i * 4 + 2 * s + b + 2)
                            dve.wait_ge(valued, i * 4 + 2 * s + b + 1)
                            g = gate[:, b, :].rearrange("p (h t) -> p h t", h=2)
                            nc.vector.tensor_tensor(g, g, k.ps[:, 4 + 2 * b:6 + 2 * b, 0:H2], ALU.mult).then_inc(term, 1)
                        dve.wait_ge(term, i * 4 + 2 * s + 3)
                        nc.vector.tensor_tensor(k.work[:, 0, :], gate[:, 0, :], gate[:, 1, :], ALU.add).then_inc(merged, 1)
                        dve.wait_ge(merged, i * 2 + s + 2)
                        m = bass.ds(i * 2 + s, 1)
                        nc.vector.tensor_copy(a.mergedH[:, m, :], k.work[:, 0:1, :]).then_inc(m_high, 1)
                        dve.wait_ge(m_high, i * 2 + s + 1)
                        nc.vector.tensor_tensor(a.mergedL[:, m, :], k.work[:, 0:1, :],
                                                a.mergedH[:, m, :].bitcast(F32), ALU.subtract).then_inc(m_low, 1)
                        dve.wait_ge(m_low, i * 2 + s + 1)


def output_projection(nc, k, d, a, w):
    with ExitStack() as ctx:
        product, bank_free = named_semaphores(nc, ctx, "op", "product bank_free")
        with nc.Block("output_projection") as block:
            @block.sync
            def _(sp):
                w.sync(sp)

            @block.gpsimd
            def _(pool):
                w.rest(pool)

            @block.tensor
            def _(pe):
                pe.sem_inc(bank_free, 4)
                with pe.Fori(0, KD // 2) as i:
                    for s in range(2):
                        w.await_block(pe, i, s)
                        for h in range(2):
                            pe.wait_ge(bank_free, i * 4 + 2 * s + h + 1)
                            accumulate(nc, k.ps[:, 2 * s + h, 0:H2],
                                       [x for c in range(KD)
                                        for x in split_products(w.parts(s, c), both((a.mergedH, a.mergedL), c, halves(h)))]
                                       ).then_inc(product, 1)

            @block.scalar
            def _(act):
                with act.Fori(0, KD // 2 - 1) as i:
                    for s in range(2):
                        act.wait_ge(product, i * 4 + 2 * s + 2)
                        w.round(act, i + 1, s)

            @block.vector
            def _(dve):
                with dve.Fori(0, KD // 2) as i:
                    for s in range(2):
                        for h in range(2):
                            u = 2 * s + h
                            dve.wait_ge(product, i * 4 + u + 1)
                            x = k.xT[:, bass.ds(i * 2 + s, 1), halves(h)]
                            nc.vector.tensor_tensor(x, x, k.ps[:, u:u + 1, 0:H2], ALU.add).then_inc(bank_free, 1)


def retrieve(nc, k, d, f, w):
    with ExitStack() as ctx:
        keys = ctx.enter_context(nc.sbuf_tensor("r_keys", [P, 2, 2, P], F32))
        qT = ctx.enter_context(nc.sbuf_tensor("r_q", [P, 2, T], F32))
        score = ctx.enter_context(nc.sbuf_tensor("r_score", [P, 2, TT, NK], F32))
        rest = ctx.enter_context(nc.sbuf_tensor("r_rest", [P, TT, NK], F32))
        top = ctx.enter_context(nc.sbuf_tensor("r_top", [P, 2, TT, TOPK], F32))
        at = ctx.enter_context(nc.sbuf_tensor("r_at", [P, 2, TT, TOPK], U32))
        atf = ctx.enter_context(nc.sbuf_tensor("r_atf", [P, 2, TT, TOPK], F32))
        cand = ctx.enter_context(nc.sbuf_tensor("r_cand", [P, TT, TOPK * TOPK], F32))
        left = ctx.enter_context(nc.sbuf_tensor("r_left", [P, TT, TOPK * TOPK], F32))
        best = ctx.enter_context(nc.sbuf_tensor("r_best", [P, TT, TOPK], F32))
        where = ctx.enter_context(nc.sbuf_tensor("r_where", [P, TT, TOPK], U32))
        part = ctx.enter_context(nc.sbuf_tensor("r_part", [P, 2, TT, TOPK], U32))
        partf = ctx.enter_context(nc.sbuf_tensor("r_partf", [P, 2, TT, TOPK], F32))
        hit = ctx.enter_context(nc.sbuf_tensor("r_hit", [P, 2, TT, TOPK, TOPK], F32))
        tot = ctx.enter_context(nc.sbuf_tensor("r_tot", [P, TT], F32))
        res = ctx.enter_context(nc.sbuf_tensor("r_res", [P, 3, TT, HEADS * TOPK], F32))
        (keys_in0, keys_in1, queried, q_in_sbuf, scored, score_in, score_free, step, hit_ready, looked_up, exp_ready, exped,
         reset, turned, turn_free) = named_semaphores(
            nc, ctx, "re", "keys_in0 keys_in1 queried q_in_sbuf scored score_in score_free step hit_ready looked_up "
            "exp_ready exped reset turned turn_free")
        keys_in = (keys_in0, keys_in1)
        u, hid = (ctx.enter_context(nc.sbuf_tensor(n, [P, 2, m], F32)) for n, m in (("r_u", D), ("r_hidden", T)))
        uH, uL = (ctx.enter_context(nc.sbuf_tensor(n, [P, 2, D], F32R)) for n in ("r_uH", "r_uL"))
        (u0, u1, u_high, u_low, hidden, activated, *hidden_out) = named_semaphores(
            nc, ctx, "rh", "u0 u1 u_high u_low hidden activated hidden_out0 hidden_out1")
        u_in = (u0, u1)
        scratch = ctx.enter_context(nc.sbuf_tensor("r_scratch", [P, 64], F32))
        iota16 = k.const[:, C_IOTA:C_IOTA + TOPK]

        def load_keys(sp, j, i):
            sp.dma_start(keys[:, j], d["keys"][bass.ds(i, 1)].rearrange("o p s m -> p (o s) m")).then_inc(keys_in[j], 16)

        with nc.Block("retrieve") as block:
            @block.sync
            def _(sp):
                def load_u(i, s):
                    sp.dma_start(u[:, s, :], d["u"][bass.ds(i * (2 * GB) + s * GB, 1)].rearrange("o p m -> p (o m)")
                                 ).then_inc(u_in[s], 16)

                def store_hidden(i, s):
                    sp.wait_ge(activated, i * 4 + (2 * s + 6))
                    sp.dma_start(d["hidden"][bass.ds(i * 2 + s, 1)].rearrange("o p t -> p (o t)"), hid[:, s, :]
                                 ).then_inc(hidden_out[s], 16)

                for j in range(2):
                    load_keys(sp, j, j)
                for s in range(2):
                    load_u(0, s)
                for s in range(2):
                    sp.wait_ge(w.low_done, s + 1)
                    w.load(sp, s, s + 2)
                for s in range(2):
                    sp.wait_ge(u_low, s + 1)
                    load_u(1, s)
                for s in range(2):
                    store_hidden(0, s)
                with sp.Fori(1, HEADS // 2) as i:
                    for j in range(2):
                        sp.wait_ge(scored, i * 4 + (2 * j - 1))
                        load_keys(sp, j, i * 2 + j)
                        m = i * 2 + j
                        for s in range(2):
                            sp.wait_ge(w.low_done, m * 2 + (s - 1))
                            w.load(sp, s, m * 2 + s)
                        for s in range(2):
                            sp.wait_ge(u_low, m * 2 + (s - 1))
                            load_u(m, s)
                        for s in range(2):
                            store_hidden(m - 1, s)
                for m in range(HEADS, ROUNDS):
                    for s in range(2):
                        sp.wait_ge(u_low, m * 2 + (s - 1))
                        load_u(m, s)
                    for s in range(2):
                        store_hidden(m - 1, s)
                for s in range(2):
                    store_hidden(ROUNDS - 1, s)
                    sp.wait_ge(hidden_out[s], 16 * ROUNDS)

            @block.gpsimd
            def _(pool):
                def look_up(i):
                    for s in range(2):
                        pool.wait_ge(hit_ready, i * 2 + s + 1)
                        nc.gpsimd.tensor_tensor(hit[:, s], hit[:, s],
                                                atf[:, s].unsqueeze(2).to_broadcast([P, TT, TOPK, TOPK]),
                                                ALU.mult).then_inc(looked_up, 1)

                def low_u(i):
                    for s in range(2):
                        pool.wait_ge(u_high, i * 2 + s + 1)
                        nc.gpsimd.tensor_tensor(uL[:, s, :], u[:, s, :], uH[:, s, :].bitcast(F32),
                                                ALU.subtract).then_inc(u_low, 1)

                low_u(0)
                with pool.Fori(0, HEADS - 1) as i:
                    for s in range(2):
                        w.low_part(pool, s, i * 2 + (s + 2))
                    low_u(i + 1)
                    look_up(i)
                for m in range(HEADS, ROUNDS):
                    low_u(m)
                look_up(HEADS - 1)

            @block.tensor
            def _(pe):
                pe.sem_inc(scored, 1)
                def head(i, j):
                    m = i * 2 + j
                    for s in range(2):
                        pe.wait_ge(w.low_done, m * 2 + s + 1)
                        pe.wait_ge(q_in_sbuf, m * 2 + 1)
                        pe.wait_ge(activated, m * 4 + (2 * s + 2))
                        for h in range(2):
                            last = accumulate(nc, k.ps[:, 2 * s + h, 0:H2],
                                              [x for c in range(KD)
                                               for x in split_products(w.parts(s, c), both(k.h, c, halves(h)))])
                        last.then_inc(queried, 1)
                    pe.wait_ge(keys_in[j], i * 16 + 16)
                    for s in range(2):
                        pe.wait_ge(q_in_sbuf, m * 2 + s + 2)
                        pe.wait_ge(score_in, m * 2 + 1)
                        for t in range(TT):
                            r = rows_of(t)
                            out = k.ps[0:r, 4 + 2 * s, t * P:(t + 1) * P] if t < QT else k.ps[0:r, 5 + 2 * s, 0:P]
                            last = nc.tensor.matmul(out, qT[:, s, t * P:t * P + r], keys[:, j, s, :],
                                                    start=True, stop=True)
                        last.then_inc(scored, 1)

                    hide(m)

                def hide(m, awaited=True):
                    for s in range(2):
                        if not awaited:
                            pe.wait_ge(activated, m * 4 + (2 * s + 2))
                        pe.wait_ge(u_low, m * 2 + s + 1)
                        for h in range(2):
                            accumulate(nc, k.ps[:, 2 * s + h, 0:H2],
                                       [x for c in range(KD) for x in split_products(
                                           (uH[:, s, c * P:(c + 1) * P], uL[:, s, c * P:(c + 1) * P]),
                                           both(k.h, c, halves(h)))]).then_inc(hidden, 1)

                with pe.Fori(0, HEADS // 2) as i:
                    for j in range(2):
                        head(i, j)
                for m in range(HEADS, ROUNDS):
                    hide(m, awaited=False)
                pe.wait_ge(step, HEADS * STEPS)
                for j in range(3 * TT):
                    a, t = j // TT, j % TT
                    r = rows_of(t)
                    if j >= 4:
                        pe.wait_ge(turn_free, j - 3)
                    nc.tensor.transpose(k.ps[:, j % 4, 0:r], res[0:r, a, t, :],
                                        k.const[0:r, C_IDENT:C_IDENT + r]).then_inc(turned, 1)

            @block.scalar
            def _(act):
                def copies(i, more=True):
                    for s in range(2):
                        act.wait_ge(queried, i * 2 + s + 1)
                        act.wait_ge(scored, i * 2 + 1)
                        nc.scalar.activation(qT[:, s, :].rearrange("p (h t) -> p h t", h=2),
                                             k.ps[:, 2 * s:2 * s + 2, 0:H2], ACT.Copy).then_inc(q_in_sbuf, 1)
                        if more:
                            w.round(act, i + 1, s)
                    for s in range(2):
                        act.wait_ge(scored, i * 2 + s + 2)
                        act.wait_ge(score_free, i * 2 + s + 1)
                        nc.scalar.activation(score[:, s, 0:QT, :], k.ps[:, 4 + 2 * s, :].rearrange("p (t c) -> p t c", t=QT),
                                             ACT.Copy)
                        nc.scalar.activation(score[0:SAMP, s, QT, :], k.ps[0:SAMP, 5 + 2 * s, 0:P],
                                             ACT.Copy).then_inc(score_in, 1)

                def exponentials(i):
                    act.wait_ge(exp_ready, i + 1)
                    nc.scalar.activation(best[:, :, :], best[:, :, :], ACT.Exp).then_inc(exped, 1)

                act.sem_inc(q_in_sbuf, 1)
                act.sem_inc(score_in, 1)
                def round_u(i, s):
                    act.wait_ge(u_in[s], i * 16 + 16)
                    nc.scalar.activation(uH[:, s, :], u[:, s, :], ACT.Copy).then_inc(u_high, 1)

                def activate(i, first=False, more=True):
                    for s in range(2):
                        if not first:
                            act.wait_ge(hidden_out[s], i * 16)
                        for h in range(2):
                            act.wait_ge(hidden, i * 4 + (2 * s + h + 1))
                            nc.scalar.activation(hid[:, s, halves(h)], k.ps[:, 2 * s + h, 0:H2],
                                                 ACT.Gelu).then_inc(activated, 1)
                        if more:
                            round_u(i + 1, s)

                act.sem_inc(activated, 4)
                for s in range(2):
                    round_u(0, s)
                copies(0)
                activate(0, first=True)
                with act.Fori(0, HEADS - 2) as i:
                    copies(i + 1)
                    activate(i + 1)
                    exponentials(i)
                copies(HEADS - 1, more=False)
                activate(HEADS - 1)
                exponentials(HEADS - 2)
                for m in range(HEADS, ROUNDS):
                    activate(m, more=m < ROUNDS - 1)
                exponentials(HEADS - 1)
                for j in range(3 * TT):
                    a, t = j // TT, j % TT
                    act.wait_ge(turned, j + 1)
                    nc.scalar.activation(f.pick[:, a, t * P:t * P + rows_of(t)], k.ps[:, j % 4, 0:rows_of(t)],
                                         ACT.Copy).then_inc(turn_free, 1)

            @block.vector
            def _(dve):
                nc.vector.memset(score[:, :, QT, :], 0.0).then_inc(reset, 1)
                dve.wait_ge(reset, 1)
                dve.sem_inc(score_free, 2)

                def head(i, first=False, last=False):
                    n, waits = [0 if first else -FINISH], [0]

                    def done(ins):
                        n[0] += 1
                        ins.then_inc(step, 1)

                    def after():
                        vector_wait(step, i * STEPS + n[0])

                    def vector_wait(sem, value):
                        dve.wait_ge(sem, value)
                        nc.vector.memset(scratch[:, waits[0]:waits[0] + 1], 0.0)
                        waits[0] += 1

                    def sixteen(value, spare, tops, index):
                        for t in range(TT):
                            done(nc.vector.max(tops[:, t, 0:8], value[:, t, :]))
                        after()
                        for t in range(TT):
                            nc.vector.max_index(index[:, t, 0:8], tops[:, t, 0:8], value[:, t, :])
                            done(nc.vector.match_replace(spare[:, t, :], tops[:, t, 0:8], value[:, t, :], REMOVED))
                        after()
                        for t in range(TT):
                            done(nc.vector.max(tops[:, t, 8:16], spare[:, t, :]))
                        after()
                        for t in range(TT):
                            last = nc.vector.max_index(index[:, t, 8:16], tops[:, t, 8:16], spare[:, t, :])
                            done(last)

                    def finish(i):
                        for s in range(2):
                            dve.wait_ge(looked_up, i * 2 + s + 1)
                            done(nc.vector.tensor_reduce(res[:, s, :, bass.ds(i * TOPK, TOPK)], hit[:, s], AXX, ALU.add))
                        dve.wait_ge(exped, i + 1)
                        done(nc.vector.tensor_reduce(tot[:, :], best[:, :, :], AXX, ALU.add))
                        after()
                        done(nc.vector.reciprocal(tot[:, :], tot[:, :]))
                        after()
                        done(nc.vector.tensor_tensor(res[:, 2, :, bass.ds(i * TOPK, TOPK)], best[:, :, :],
                                                     tot[:, :].unsqueeze(2).to_broadcast([P, TT, TOPK]), ALU.mult))

                    if last:
                        finish(i - 1)
                        return
                    for s in range(2):
                        vector_wait(score_in, i * 2 + s + 2)
                        sixteen(score[:, s], rest, top[:, s], at[:, s])
                        if s == 0 and not first:
                            finish(i - 1)
                        after()
                        nc.vector.tensor_copy(atf[:, s], at[:, s]).then_inc(score_free, 1)
                    done(nc.vector.tensor_tensor(
                        cand[:, :, :].rearrange("p t (a b) -> p t a b", a=TOPK),
                        top[:, 0].unsqueeze(3).to_broadcast([P, TT, TOPK, TOPK]),
                        top[:, 1].unsqueeze(2).to_broadcast([P, TT, TOPK, TOPK]), ALU.add))
                    after()
                    sixteen(cand, left, best, where)
                    after()
                    done(nc.vector.tensor_scalar(part[:, 0], where[:, :, :], 4, None, ALU.logical_shift_right))
                    done(nc.vector.tensor_scalar(part[:, 1], where[:, :, :], TOPK - 1, None, ALU.bitwise_and))
                    after()
                    done(nc.vector.tensor_copy(partf[:, :, :, :], part[:, :, :, :]))
                    done(nc.vector.tensor_copy(tot[:, :], best[:, :, 0]))
                    after()
                    nc.vector.tensor_tensor(best[:, :, :], best[:, :, :],
                                            tot[:, :].unsqueeze(2).to_broadcast([P, TT, TOPK]),
                                            ALU.subtract).then_inc(exp_ready, 1)
                    for s in range(2):
                        nc.vector.tensor_tensor(
                            hit[:, s], partf[:, s].unsqueeze(3).to_broadcast([P, TT, TOPK, TOPK]),
                            iota16.unsqueeze(1).unsqueeze(1).to_broadcast([P, TT, TOPK, TOPK]),
                            ALU.is_equal).then_inc(hit_ready, 1)
                    assert n[0] == STEPS - FINISH, n[0]

                head(0, first=True)
                with dve.Fori(1, HEADS) as i:
                    head(i)
                head(HEADS, last=True)


FINISH = 5
STEPS = 3 * 4 * TT + 1 + 3 + 2 + 4


def gate_matrix(nc, k, f, d):
    with ExitStack() as ctx:
        hotJ = ctx.enter_context(nc.sbuf_tensor("hotJ", [P, 4, GT, NK], F32))
        hotI = ctx.enter_context(nc.sbuf_tensor("hotI", [P, 4, GT, NK], F32))
        stage = [f.stage, ctx.enter_context(nc.sbuf_tensor("stage1", [P, NK, P], F32))]
        second, first, gated, used, copied, apart, built = named_semaphores(
            nc, ctx, "gx", "second first gated used copied apart built")

        def chunks():
            return [(0, 0, SAMP // GT)] + [(t, (SAMP + (t - 1) * P) // GT, P // GT) for t in range(1, TT)]

        with nc.Block("gate_matrix") as block:
            @block.vector
            def _(dve):
                iota = k.const[:, C_IOTA:C_IOTA + NK].unsqueeze(1).to_broadcast([P, GT, NK])
                with dve.Fori(0, T // GT // 4) as i:
                    for s in range(4):
                        tokens = bass.ds(i * (4 * GT) + s * GT, GT)
                        dve.wait_ge(used, i * 4 + s + 1)
                        nc.vector.tensor_tensor(hotI[:, s], f.pick[:, 0, tokens].unsqueeze(2).to_broadcast([P, GT, NK]),
                                                iota, ALU.is_equal).then_inc(first, 1)
                        if s < 3:
                            nc.vector.tensor_tensor(hotJ[:, s],
                                                    f.pick[:, 1, tokens].unsqueeze(2).to_broadcast([P, GT, NK]),
                                                    iota, ALU.is_equal).then_inc(second, 1)

            @block.gpsimd
            def _(pool):
                with pool.Fori(0, T // GT // 4) as i:
                    for s in range(4):
                        tokens = bass.ds(i * (4 * GT) + s * GT, GT)
                        pool.wait_ge(first, i * 4 + s + 1)
                        nc.gpsimd.tensor_tensor(hotI[:, s], hotI[:, s],
                                                f.pick[:, 2, tokens].unsqueeze(2).to_broadcast([P, GT, NK]),
                                                ALU.mult).then_inc(gated, 1)

            @block.tensor
            def _(pe):
                pe.sem_inc(used, 4)
                with pe.Fori(0, T // GT // 4) as i:
                    for s in range(4):
                        if s < 3:
                            pe.wait_ge(second, i * 3 + s + 1)
                        else:
                            pe.wait_ge(built, i + 1)
                        pe.wait_ge(gated, i * 4 + s + 1)
                        pe.wait_ge(copied, i * 4 + s + 1)
                        for j in range(GT):
                            last = nc.tensor.matmul(k.ps[:, s, j * NK:(j + 1) * NK], hotJ[:, s, j, :], hotI[:, s, j, :],
                                                    start=True, stop=True)
                        last.then_inc(used, 1)

            @block.scalar
            def _(act):
                act.sem_inc(copied, 4)
                for t, g0, groups in chunks():
                    if t >= 2:
                        act.wait_ge(f.stored[t % 2], 16 * (t // 2))
                    with act.Fori(0, groups // 4) as i:
                        act.wait_ge(used, i * 4 + (g0 + 4))
                        for j in range(GT):
                            last = nc.scalar.activation(hotJ[:, 3, j, :], k.const[:, C_IOTA:C_IOTA + NK], ACT.Abs,
                                                        bias=f.pick[:, 1, bass.ds(i * (4 * GT) + ((g0 + 3) * GT + j), 1)],
                                                        scale=-1.0)
                        last.then_inc(apart, 1)
                        act.wait_ge(apart, i + (g0 // 4 + 1))
                        nc.scalar.activation(hotJ[:, 3], hotJ[:, 3], ACT.Relu, bias=k.const[:, C_ONES:C_ONES + 1],
                                             scale=-1.0).then_inc(built, 1)
                        for s in range(4):
                            act.wait_ge(used, i * 4 + (g0 + s + 5))
                            nc.scalar.activation(stage[t % 2][:, :, bass.ds(i * (4 * GT) + s * GT, GT)],
                                                 k.ps[:, s, :].rearrange("p (t i) -> p i t", t=GT),
                                                 ACT.Copy).then_inc(copied, 1)

            @block.sync
            def _(sp):
                for t, g0, groups in chunks():
                    sp.wait_ge(copied, 4 + g0 + groups)
                    tokens, n = slice(g0 * GT, (g0 + groups) * GT), groups * GT
                    rows = slice(0, NK if t < TT - 1 else EARLY)
                    sp.dma_start(d["gates"][rows, :, tokens].rearrange("i j t -> j i t"),
                                 stage[t % 2][:, rows, 0:n]).then_inc(f.stored[t % 2], 16)
                sp.wait_ge(f.stored[1], 16 * (TT // 2))


def expert_pass(nc, k, d, f):
    n, pre = NK // GB, PRE
    HU, YU = 2 * GB, 2 * KD
    with ExitStack() as ctx:
        u = ctx.enter_context(nc.sbuf_tensor("ex_u", [P, GB, D], F32))
        v = ctx.enter_context(nc.sbuf_tensor("ex_v", [P, GB, D], F32))
        gate = ctx.enter_context(nc.sbuf_tensor("ex_gate", [P, GB, T], F32))
        hid = ctx.enter_context(nc.sbuf_tensor("ex_hidden", [P, GB, T], F32))
        uH, uL, vH, vL = (ctx.enter_context(nc.sbuf_tensor(f"ex_{x}", [P, GB, D], F32R)) for x in ("uH", "uL", "vH", "vL"))
        wH, wL = (ctx.enter_context(nc.sbuf_tensor(f"ex_{x}", [P, 2, GB, T], F32R)) for x in ("wH", "wL"))
        (u0, u1, v0, v1, g0, g1, h_in, u_high, u_low, v_high, v_low, hidden, activated, gated, rounded, weighted,
         hidden_free, mixed, added) = named_semaphores(
            nc, ctx, "ex", "u0 u1 v0 v1 g0 g1 h_in u_high u_low v_high v_low hidden activated gated rounded weighted "
            "hidden_free mixed added")
        u_in, v_in, g_in = (u0, u1), (v0, v1), (g0, g1)

        def slots(early):
            return (1,) if early else (0, 1)

        def computed(b, s, early):
            return b + 1 if early else b * GB + (s + 1 - pre)

        with nc.Block("expert_pass") as block:
            @block.sync
            def _(sp):
                def load(x, name, sem, b, s):
                    sp.dma_start(x[:, s, :], d[name][bass.ds(b * GB + s, 1)].rearrange("o p m -> p (o m)")
                                 ).then_inc(sem[s], 16)

                def load_hidden(b):
                    sp.dma_start(hid[:, 0, :], d["hidden"][bass.ds(b, 1)].rearrange("o p m -> p (o m)")
                                 ).then_inc(h_in, 16)

                load(u, "u", u_in, 0, 1)
                for s in range(GB):
                    load(v, "v", v_in, 0, s)
                load_hidden(0)
                sp.wait_ge(f.stored[0], 16 * ((TT + 1) // 2))
                for s in range(GB):
                    load(gate, "gates", g_in, 0, s)

                def further(b, early=False, next_early=False, first=False):
                    for s in slots(next_early):
                        if s in slots(early):
                            sp.wait_ge(u_low, computed(b, s, early))
                        load(u, "u", u_in, b + 1, s)
                    if next_early:
                        sp.wait_ge(hidden_free, b * GB + (GB + 1))
                        load_hidden(b + 1)
                    if first:
                        sp.dma_start(d["gates"][EARLY:NK, :, T - P:T].rearrange("i j t -> j i t"),
                                     f.stage[:, EARLY:NK, :]).then_inc(f.late, 16)
                    for s in range(GB):
                        sp.wait_ge(gated, b * GB + s + 1)
                        load(gate, "gates", g_in, b + 1, s)
                    for s in range(GB):
                        sp.wait_ge(v_low, b * GB + s + 1)
                        load(v, "v", v_in, b + 1, s)

                further(0, True, True, first=True)
                with sp.Fori(1, pre - 1) as b:
                    further(b, True, True)
                sp.wait_ge(f.late, 16)
                further(pre - 1, True, False)
                with sp.Fori(pre, n - 1) as b:
                    further(b)

            @block.scalar
            def _(act):
                def split_u(b, s, early=False):
                    act.wait_ge(u_in[s], b * 16 + (16 if early or s == 1 else 16 - 16 * pre))
                    nc.scalar.activation(uH[:, s, :], u[:, s, :], ACT.Copy).then_inc(u_high, 1)

                def split_v(b, s):
                    act.wait_ge(v_in[s], b * 16 + 16)
                    nc.scalar.activation(vH[:, s, :], v[:, s, :], ACT.Copy).then_inc(v_high, 1)

                def step(b, early=False, next_early=False, first=False, final=False):
                    for s in slots(early):
                        act.wait_ge(hidden_free, b * GB + s + 1)
                        for h in range(2):
                            act.wait_ge(hidden, computed(b, s, early) * 2 + (h - 1))
                            nc.scalar.activation(hid[:, s, halves(h)], k.ps[:, 2 * s + h, 0:H2],
                                                 ACT.Gelu).then_inc(activated, 1)
                        for r in () if final else (s,) if early == next_early else slots(next_early):
                            split_u(b + 1, r, next_early)
                    if not first:
                        act.wait_ge(mixed, b * YU)
                        for s in range(GB):
                            split_v(b, s)

                split_u(0, 1, True)
                for s in range(GB):
                    split_v(0, s)
                act.sem_inc(hidden_free, GB)
                step(0, True, True, first=True)
                with act.Fori(1, pre - 1) as b:
                    step(b, True, True)
                step(pre - 1, True, False)
                with act.Fori(pre, n - 1) as b:
                    step(b)
                step(n - 1, final=True)

            @block.gpsimd
            def _(pool):
                def low(x, xH, xL, high, sem, count, s):
                    pool.wait_ge(high, count)
                    nc.gpsimd.tensor_tensor(xL[:, s, :], x[:, s, :], xH[:, s, :].bitcast(F32),
                                            ALU.subtract).then_inc(sem, 1)

                def low_u(b, early=False):
                    for s in slots(early):
                        low(u, uH, uL, u_high, u_low, computed(b, s, early), s)

                def low_v(b):
                    for s in range(GB):
                        low(v, vH, vL, v_high, v_low, b * GB + s + 1, s)

                low_u(0, True)
                low_v(0)
                low_u(1, True)
                with pool.Fori(1, pre - 1) as b:
                    low_u(b + 1, True)
                    low_v(b)
                low_u(pre)
                low_v(pre - 1)
                with pool.Fori(pre, n - 1) as b:
                    low_u(b + 1)
                    low_v(b)
                low_v(n - 1)

            @block.tensor
            def _(pe):
                def hide(b, early=False, before=False, first=False):
                    for s in slots(early):
                        pe.wait_ge(u_low, computed(b, s, early))
                        for h in range(2):
                            if not first and s in slots(before):
                                pe.wait_ge(activated, computed(b - 1, s, before) * 2 + (h - 1))
                            pairs = []
                            for c in range(KD):
                                rows = slice(c * P, (c + 1) * P)
                                pairs += [(uH[:, s, rows], k.h[0][:, c, halves(h)]), (uH[:, s, rows], k.h[1][:, c, halves(h)]),
                                          (uL[:, s, rows], k.h[0][:, c, halves(h)])]
                            accumulate(nc, k.ps[:, 2 * s + h, 0:H2], pairs).then_inc(hidden, 1)

                def mix(b, parity):
                    pe.wait_ge(weighted, b * GB + GB)
                    pe.wait_ge(v_low, b * GB + GB)
                    for c in range(KD):
                        rows = slice(c * P, (c + 1) * P)
                        for h in range(2):
                            y = 2 * c + h
                            pe.wait_ge(added, b * YU + y + 1)
                            pairs = []
                            for s in range(GB):
                                high, low = wH[:, parity, s, halves(h)], wL[:, parity, s, halves(h)]
                                pairs += [(vH[:, s, rows], high), (vH[:, s, rows], low), (vL[:, s, rows], high)]
                            accumulate(nc, k.ps[:, 4 + y % 4, 0:H2], pairs).then_inc(mixed, 1)

                pe.sem_inc(added, 4)
                hide(0, True, first=True)
                with pe.Fori(0, pre - 2, 2) as b:
                    for j in range(2):
                        hide(b + (j + 1), True, True)
                        mix(b + j, j)
                hide(pre - 1, True, True)
                mix(pre - 2, 0)
                hide(pre, False, True)
                mix(pre - 1, 1)
                with pe.Fori(pre, n - 2, 2) as b:
                    for j in range(2):
                        hide(b + (j + 1))
                        mix(b + j, j)
                hide(n - 1)
                mix(n - 2, 0)
                mix(n - 1, 1)

            @block.vector
            def _(dve):
                def weigh(b, parity, s, early=False):
                    if s in slots(early):
                        dve.wait_ge(activated, computed(b, s, early) * 2)
                    else:
                        dve.wait_ge(h_in, b * 16 + 16)
                    dve.wait_ge(g_in[s], b * 16 + 16)
                    nc.vector.tensor_tensor(hid[:, s, :], hid[:, s, :], gate[:, s, :], ALU.mult).then_inc(gated, 1)
                    dve.wait_ge(gated, b * GB + s + 1)
                    nc.vector.tensor_copy(wH[:, parity, s, :], hid[:, s, :]).then_inc(rounded, 1)
                    dve.wait_ge(rounded, b * GB + s + 1)
                    nc.vector.tensor_tensor(wL[:, parity, s, :], hid[:, s, :], wH[:, parity, s, :].bitcast(F32),
                                            ALU.subtract).then_inc(weighted, 1)
                    dve.wait_ge(weighted, b * GB + s + 1)
                    dve.sem_inc(hidden_free, 1)

                def add(b, units):
                    for y in units:
                        dve.wait_ge(mixed, b * YU + y + 1)
                        x = k.xT[:, y // 2, halves(y % 2)]
                        nc.vector.tensor_tensor(x, x, k.ps[:, 4 + y % 4, 0:H2], ALU.add).then_inc(added, 1)

                def turn(b, parity, early=False):
                    weigh(b + 1, 1 - parity, 0, early)
                    add(b, range(2))
                    weigh(b + 1, 1 - parity, 1, early)
                    add(b, range(2, YU))

                for s in range(GB):
                    weigh(0, 0, s, early=True)
                with dve.Fori(0, pre - 2, 2) as b:
                    for j in range(2):
                        turn(b + j, j, early=True)
                turn(pre - 2, 0, early=True)
                turn(pre - 1, 1)
                with dve.Fori(pre, n - 2, 2) as b:
                    for j in range(2):
                        turn(b + j, j)
                turn(n - 2, 0)
                add(n - 1, range(YU))


def layer_embedding(nc, k, d, w):
    KP = 256 // P
    with ExitStack() as ctx:
        pT = ctx.enter_context(nc.sbuf_tensor("le_p", [P, KP, T], F32))
        split = [ctx.enter_context(nc.sbuf_tensor(f"le_p{n}", [P, KP, T], F32R)) for n in ("high", "low")]
        gate = ctx.enter_context(nc.sbuf_tensor("le_gate", [P, 2, T], F32))
        p_in, p_high, p_low, gated, valued, gate_done, term, added = named_semaphores(
            nc, ctx, "le", "p_in p_high p_low gated valued gate_done term added")

        with nc.Block("layer_embedding") as block:
            @block.sync
            def _(sp):
                sp.dma_start(pT[:, :, :], d["pT"]).then_inc(p_in, 16)
                w.sync(sp)

            @block.gpsimd
            def _(pool):
                w.rest(pool)

            @block.tensor
            def _(pe):
                with pe.Fori(0, KD // 2) as i:
                    for s in range(2):
                        w.await_block(pe, i, s)
                        pe.wait_ge(gate_done, i * 2 + 1)
                        for h in range(2):
                            last = accumulate(nc, k.ps[:, 4 * s + h, 0:H2],
                                              [x for c in range(KD)
                                               for x in split_products(w.parts(s, c), both(k.h, c, halves(h)))])
                        last.then_inc(gated, 1)
                        pe.wait_ge(p_low, 1)
                        pe.wait_ge(term, i * 2 + 1)
                        for h in range(2):
                            last = accumulate(nc, k.ps[:, 4 * s + 2 + h, 0:H2],
                                              [x for c in range(KP)
                                               for x in split_products(w.parts(s, KD + c), both(split, c, halves(h)))])
                        last.then_inc(valued, 1)

            @block.scalar
            def _(act):
                def pair(i, more):
                    for s in range(2):
                        act.wait_ge(added, i * 2 + 1)
                        act.wait_ge(gated, i * 2 + s + 1)
                        nc.scalar.activation(gate[:, s, :].rearrange("p (h t) -> p h t", h=2),
                                             k.ps[:, 4 * s:4 * s + 2, 0:H2], ACT.Sigmoid).then_inc(gate_done, 1)
                        if more:
                            act.wait_ge(valued, i * 2 + s + 1)
                            w.round(act, i + 1, s)

                act.sem_inc(gate_done, 1)
                act.wait_ge(p_in, 16)
                nc.scalar.activation(split[0][:, :, :], pT[:, :, :], ACT.Copy).then_inc(p_high, 1)
                with act.Fori(0, KD // 2 - 1) as i:
                    pair(i, True)
                pair(KD // 2 - 1, False)

            @block.vector
            def _(dve):
                dve.sem_inc(term, 1)
                dve.sem_inc(added, 1)
                dve.wait_ge(p_high, 1)
                nc.vector.tensor_tensor(split[1][:, :, :], pT[:, :, :], split[0][:, :, :].bitcast(F32),
                                        ALU.subtract).then_inc(p_low, 1)
                with dve.Fori(0, KD // 2) as i:
                    for s in range(2):
                        dve.wait_ge(gate_done, i * 2 + s + 2)
                        dve.wait_ge(valued, i * 2 + s + 1)
                        g = gate[:, s, :].rearrange("p (h t) -> p h t", h=2)
                        nc.vector.tensor_tensor(g, g, k.ps[:, 4 * s + 2:4 * s + 4, 0:H2], ALU.mult).then_inc(term, 1)
                        dve.wait_ge(term, i * 2 + s + 2)
                        x = k.xT[:, bass.ds(i * 2 + s, 1), :]
                        nc.vector.tensor_tensor(x, x, gate[:, s:s + 1, :], ALU.add).then_inc(added, 1)


def stream_step(nc, d):
    with ExitStack() as ctx:
        k = Core()

        def sb(name, shape, dtype=F32, c=ctx):
            return c.enter_context(nc.sbuf_tensor(name, shape, dtype))

        k.ps = ctx.enter_context(nc.psum_tensor("banks", [P, 8, 512], F32))
        k.xT = sb("xT", [P, KD, T])
        k.const = sb("const", [P, C_END])
        k.gain = sb("gain", [P, G_END])
        norm_sems = named_semaphores(nc, ctx, "norm", "squared summed rooted inverted normed high stored")
        counts = [0, 0, 0, 0]

        def norm(name, parts, split=None, ahead=None, store=None, hold=True):
            with nc.sbuf_tensor(f"{name}_square", [P, 2, T], F32) as k.square, \
                    nc.sbuf_tensor(f"{name}_rstd", [P, 2, T], F32) as k.rstd:
                rms_norm(nc, k, name, norm_sems, tuple(counts), parts, split, ahead, store, hold)
            chunks = sum(part[2] for part in parts)
            for j, n in enumerate((len(parts), chunks, chunks if split else 0, len(store or []))):
                counts[j] += n

        def norm_h(name, gain, ahead):
            with nc.sbuf_tensor(f"{name}_whole", [P, KD, T], F32) as whole:
                norm(name, [(lambda c: k.xT[:, c, :], lambda c: whole[:, c, :], KD, gain)], k.h, ahead)

        load_inputs(nc, k, d)
        with ExitStack() as inner:
            k.h = [sb(f"h{n}", [P, KD, T], F32R, c=inner) for n in ("high", "low")]
            with ExitStack() as mixer:
                a = Core()
                a.oA = sb("oA", [P, PAIRS, T], c=mixer)
                a.oB = sb("oB", [P, PAIRS, T], c=mixer)
                a.softmax = named_semaphores(nc, mixer, "sm", SOFTMAX_SEMS)
                with ExitStack() as mla:
                    a.proj = sb("proj", [P, NQ + NC + 1, T], c=mla)
                    a.rope = sb("rope", [P, T], c=mla)
                    a.kdup = sb("kdup", [P, T], c=mla)
                    a.kdupS = sb("kdupS", [P, MLAK], c=mla)
                    a.keyS = sb("keyS", [P, NC, MLAK], c=mla)
                    a.valueS = sb("valueS", [P, PAST // P + 1, KVL], c=mla)
                    a.loaded, a.lift_in, a.key_stored = named_semaphores(nc, mla, "mla", "loaded lift_in key_stored")
                    a.latent_stored = norm_sems[-1]
                    with ExitStack() as stage:
                        w = Stream(nc, stage, "lp", d["w_small"], KD, NQ + NC + 1)
                        norm_h("norm_mix", G_MIX, w)
                        latent_projection(nc, k, d, a, w)
                    norm("norm_latents", [(lambda c: a.proj[:, c, :], lambda c: a.proj[:, c, :], NQ, G_Q),
                                          (lambda c: a.proj[:, NQ + c, :], lambda c: a.proj[:, NQ + c, :], NC, G_KV)],
                         store=[(d["o_latent"], a.proj[:, NQ:NQ + NC, :])], hold=False)
                    with nc.sbuf_tensor("turn", [P, T], F32) as a.turn:
                        rotary_key(nc, k, d, a)
                    a.wuv = sb("w_uv", [P, NC, HEADS * NOPE], c=mla)
                    a.wukT = sb("w_ukT", [P, PAIRS, KVL], c=mla)
                    a.qS = sb("qS", [P, HEADS, SAMP], c=mla)
                    latent_attention(nc, k, d, a)
                    latent_sample(nc, k, d, a)
                with ExitStack() as stage:
                    w = Stream(nc, stage, "gm", d["w_merge"], KD, 3 * KD, 6)
                    band_attention(nc, k, d, a, w)
                    a.mergedH, a.mergedL = (sb(f"merged{n}", [P, KD, T], F32R, c=stage) for n in ("high", "low"))
                    out = Stream(nc, stage, "op", d["w_out"], KD, KD)
                    with nc.sbuf_tensor("work", [P, 1, T], F32) as k.work:
                        gated_merge(nc, k, d, a, w, out)
                    output_projection(nc, k, d, a, out)
            with ExitStack() as ffn:
                f = Core()
                f.pick = sb("pick", [P, 3, T], c=ffn)
                with ExitStack() as stage:
                    w = Stream(nc, stage, "re", d["w_query"], KD, 2 * HEADS)
                    norm_h("norm_ffn", G_FFN, w)
                    retrieve(nc, k, d, f, w)
                f.stage = sb("stage0", [P, NK, P], c=ffn)
                *f.stored, f.late = named_semaphores(nc, ffn, "gates", "stored0 stored1 late")
                gate_matrix(nc, k, f, d)
                expert_pass(nc, k, d, f)
            with ExitStack() as stage:
                w = Stream(nc, stage, "le", d["w_ple"], KD + 256 // P, KD)
                norm_h("norm_ple", G_PLE, w)
                layer_embedding(nc, k, d, w)
        with nc.sbuf_tensor("y", [P, KD, T], F32) as y:
            norm("norm_final", [(lambda c: k.xT[:, c, :], lambda c: y[:, c, :], KD, G_FIN)],
                 store=[(d["o_y"], y[:, :, :])])


def kernel(**inputs):
    import concourse.bacc as bacc
    from concourse.bass_utils import run_bass_kernel_spmd

    x = {n: np.asarray(v) for n, v in inputs.items()}

    def blocks(w):
        kk, m = w.shape
        return np.ascontiguousarray(w.reshape(kk // P, P, m // P, P).transpose(2, 1, 0, 3))

    def feature_major(v):
        return np.ascontiguousarray(v.T.reshape(v.shape[1] // P, P, v.shape[0]).transpose(1, 0, 2))

    def columns(v):
        return v.reshape(-1, P).T

    def swapped(w):
        return np.concatenate([w[..., ROPE // 2:], w[..., :ROPE // 2]], -1)

    w_in = x["w_in"][0]
    o = np.cumsum([0, QL, KVL, ROPE, 512, 512, 512, D, D])
    kr = w_in[:, o[2]:o[3]]
    arrays = {}
    arrays["xT"] = feature_major(np.concatenate([x["x_prompt"][0], x["x_sample"][0]]))
    arrays["pT"] = feature_major(np.concatenate([x["p_prompt"][0, 0], x["p_sample"][0, 0]]))
    arrays["w_small"] = blocks(np.concatenate([w_in[:, :o[2]], kr, swapped(kr), np.zeros((D, 64), np.float32)], 1))
    for n, j in (("w_bq", 3), ("w_bk", 4), ("w_bv", 5)):
        arrays[n] = blocks(w_in[:, o[j]:o[j + 1]])
    values = np.concatenate([blocks(x["w_a_proj"][0]), blocks(x["w_b_proj"][0])], 2)
    arrays["w_merge"] = np.stack([blocks(w_in[:, o[6]:o[7]]), blocks(w_in[:, o[7]:o[8]]), values],
                                 1).reshape(3 * KD, P, KD, P)
    arrays["w_out"] = blocks(x["w_out"][0])
    arrays["w_query"] = blocks(x["w_query"][0])
    arrays["keys"] = x["sub_keys"][0].transpose(0, 3, 1, 2)
    arrays["w_ple"] = np.concatenate([blocks(x["w_ple_gate"][0]), blocks(x["w_ple_proj"][0])], 2)
    uq = x["w_uq"][0].reshape(QL, PAIRS, 2, NOPE + ROPE)
    nope, rot = uq[..., :NOPE], uq[..., NOPE:]
    rot = np.concatenate([rot, swapped(rot)], -1)
    uq = np.stack([np.concatenate([nope[:, :, 0], rot[:, :, 0]], -1),
                   np.concatenate([rot[:, :, 1], nope[:, :, 1]], -1)], 2)
    arrays["w_uq"] = uq.reshape(NQ, P, PAIRS, 2, P).transpose(2, 1, 3, 0, 4).reshape(PAIRS, P, -1)
    uk = x["w_uk"][0]
    arrays["w_uk"] = uk.reshape(NC, P, PAIRS, P).transpose(2, 1, 0, 3).reshape(PAIRS, P, -1)
    arrays["w_ukT"] = uk.reshape(KVL, PAIRS, P).transpose(2, 1, 0)
    arrays["w_uv"] = x["w_uv"][0].reshape(NC, P, HEADS * NOPE).transpose(1, 0, 2)
    lat = x["cache_latent"][0, 0]
    arrays["cache_latT"] = feature_major(lat)
    arrays["cache_lat"] = lat.reshape(PAST // P, P, KVL).transpose(1, 0, 2)
    arrays["cache_krT"] = np.concatenate([x["cache_krope"][0, 0].T] * 4)
    bk = x["cache_band_k"][0, 0].reshape(WIN, PAIRS, P)
    bv = x["cache_band_v"][0, 0].reshape(WIN, PAIRS, P)
    arrays["cache_bkT"] = bk.transpose(1, 2, 0)
    arrays["cache_bv"] = bv.reshape(QT, P, PAIRS, P).transpose(2, 1, 0, 3)
    arrays["cache_bv_kept"] = bv[SAMP:].reshape(WIN - SAMP, PAIRS * P)
    rel = x["rel_bias"][0]
    clip = (rel.shape[1] - 1) // 2
    dist = np.arange(P)[:, None] - (np.arange(WIN + P) - WIN)[None]
    bias = rel[:, np.clip(dist, -clip, clip) + clip]
    bias[:, :64, WIN + 64:] = NEG
    arrays["bias"] = bias.reshape(PAIRS, 2, P, WIN + P).transpose(0, 2, 1, 3)
    dist = (WIN + np.arange(SAMP))[:, None] - np.arange(BANDK)[None]
    arrays["biasS"] = rel[:, np.clip(dist, -clip, clip) + clip].reshape(PAIRS, 2 * SAMP, BANDK)
    arrays["u"] = x["expert_u"][0].reshape(NK, NK, KD, P).transpose(0, 3, 2, 1).reshape(NK, P, D)
    arrays["v"] = x["expert_v"][0].reshape(NK, NK, D)
    arrays["gains"] = np.concatenate([columns(x[n].reshape(-1)) for n in
                                      ("g_mix", "g_ffn", "g_ple", "g_final", "g_q_lora", "g_kv_lora")], 1)
    half = ROPE // 2
    freqs = (np.float32(10000.0) ** (-np.arange(half, dtype=np.float32) / np.float32(half))).astype(np.float32)
    pos = np.concatenate([np.arange(SEQ), PAST + np.arange(SAMP)]).astype(np.float32)
    ang = (freqs[:, None] * pos[None]).astype(np.float32)
    cos, sin = np.cos(ang), np.sin(ang)
    arrays["rope"] = np.concatenate([cos, cos, -sin, sin] * 2).astype(np.float32)
    const = np.zeros((P, C_END), np.float32)
    const[:, C_IDENT:C_IDENT + P] = np.eye(P)
    const[:, C_ONES:C_ONES + P] = 1.0
    const[:, C_IOTA:C_IOTA + P] = np.arange(P)
    const[:, C_DUP:C_DUP + P] = np.arange(P)[:, None] % ROPE == np.arange(P)[None] % ROPE
    const[0, C_MASKL:C_MASKL + 64] = 1.0
    const[0, C_MASKR + 64:C_MASKR + P] = NEG
    const[:, C_EPS] = EPS
    arrays["consts"] = const

    outs = {"o_y": [P, KD, T], "o_latent": [P, NC, T], "o_krope": [ROPE, T], "o_bkT": [PAIRS, P, SEQ],
            "o_bkS": [PAIRS, P, WIN], "o_bv": [PAIRS, P, QT, P], "o_bvS": [PAIRS, SAMP, P],
            "o_bvold": [WIN - SAMP, PAIRS * P]}
    nc = bacc.Bacc("TRN2", target_bir_lowering=False, num_devices=1)
    arrays = {n: np.ascontiguousarray(v) for n, v in arrays.items()}
    d = {n: nc.dram_tensor(f"in_{n}", v.shape, mybir.dt.from_np(v.dtype), kind="ExternalInput").ap()
         for n, v in arrays.items()}
    for n, shape in outs.items():
        d[n] = nc.dram_tensor(n, shape, F32, kind="ExternalOutput").ap()
    d["hidden"] = nc.dram_tensor("hidden_scratch", [PRE, P, T], F32, kind="Internal").ap()
    d["gates"] = nc.dram_tensor("gates_scratch", [NK, NK, T], F32, kind="Internal").ap()
    stream_step(nc, d)
    r = run_bass_kernel_spmd(nc, [{f"in_{n}": v for n, v in arrays.items()}], core_ids=[0]).results[0]

    def token_major(v):
        return v.transpose(2, 1, 0).reshape(v.shape[2], -1)

    y, latent = token_major(r["o_y"]), token_major(r["o_latent"])
    krope = r["o_krope"].T
    band_k = r["o_bkT"].transpose(2, 0, 1).reshape(1, 1, SEQ, HEADS, 64)
    band_kS = r["o_bkS"].transpose(2, 0, 1).reshape(1, 1, WIN, HEADS, 64)
    band_v = r["o_bv"].transpose(2, 1, 0, 3).reshape(1, 1, SEQ, HEADS, 64)
    band_vS = np.concatenate([r["o_bvold"], r["o_bvS"].transpose(1, 0, 2).reshape(SAMP, PAIRS * P)])
    return (y[None, :SEQ], y[None, SEQ:], latent[None, None, :SEQ], krope[None, None, :SEQ], band_k, band_v,
            latent[None, None, SEQ:], krope[None, None, SEQ:], band_kS, band_vS.reshape(1, 1, WIN, HEADS, 64))
```
